# Optimizing a Trainium2 kernel written in Bass

```python
import jax, jax.numpy as jnp
from jax import lax
import numpy as np

D_MODEL = 2048
BATCH = 1
SEQ = 512
DEPTH = 1

MEM_LEN = 256
EPS = 1e-6

HG_HEADS = 6
HG_DK = 128
HG_DV = 128
HG_WIDTH = HG_HEADS * HG_DK
HG_CHUNK = 64

DIL_GROUPS = ((128, 1), (512, 4), (2048, 16))
DIL_HEADS_PER_GROUP = 4
DIL_HEADS = DIL_HEADS_PER_GROUP * len(DIL_GROUPS)
DIL_HEAD_DIM = 64
DIL_WIDTH = DIL_HEADS * DIL_HEAD_DIM
DIL_QBLOCK = 128
ALIBI_MAX = 8.0

MEM_HEADS = 4
MEM_HEAD_DIM = 128
MEM_WIDTH = MEM_HEADS * MEM_HEAD_DIM

N_BRANCH = 3
MIX_WIDTH = HG_WIDTH + DIL_WIDTH + MEM_WIDTH
N_IN = 5 * HG_WIDTH + 3 * DIL_WIDTH + MEM_WIDTH + N_BRANCH * D_MODEL

PEER_HEADS = 8
PEER_NKEYS = 128
PEER_N_EXPERTS = PEER_NKEYS * PEER_NKEYS
PEER_HALF = 128
PEER_QDIM = 2 * PEER_HALF
PEER_TOPK = 16
PEER_TBLOCK = 64

kernel_name = "hybrid_hgrn2_dilated_mem_peer_encoder"

def rmsnorm(x, g):
    xf = x.astype(jnp.float32)
    y = xf * lax.rsqrt(jnp.mean(xf * xf, axis=-1, keepdims=True) + EPS)
    return (y * g.astype(jnp.float32)).astype(x.dtype)

def hgrn2_scan(q, k, v, logf):
    B, H, S, dk = q.shape
    dv = v.shape[-1]
    n = S // HG_CHUNK

    def chunks(t):
        return jnp.moveaxis(t.reshape(B, H, n, HG_CHUNK, t.shape[-1]), 2, 0)

    mask = jnp.tril(jnp.ones((HG_CHUNK, HG_CHUNK), dtype=bool))[:, :, None]

    def step(state, inp):
        qc, kc, vc, lf = inp
        b = jnp.cumsum(lf, axis=2)
        o_inter = jnp.einsum('bhtc,bhcv->bhtv', qc * jnp.exp(b), state)
        diff = b[:, :, :, None, :] - b[:, :, None, :, :]
        decay = jnp.exp(jnp.where(mask, diff, -jnp.inf))
        a = jnp.einsum('bhtsc,bhsc->bhts', qc[:, :, :, None, :] * decay, kc)
        o_intra = jnp.einsum('bhts,bhsv->bhtv', a, vc)
        b_last = b[:, :, -1:, :]
        new_state = jnp.exp(b_last[:, :, 0, :])[..., None] * state + jnp.einsum(
            'bhsc,bhsv->bhcv', kc * jnp.exp(b_last - b), vc)
        return new_state, o_inter + o_intra

    init = jnp.zeros((B, H, dk, dv), jnp.float32)
    _, ys = lax.scan(step, init, (chunks(q), chunks(k), chunks(v), chunks(logf)))
    return jnp.moveaxis(ys, 0, 2).reshape(B, H, S, dv)

def dilated_group_attn(q, k, v, slopes, dilation, n_side):
    B, Hg, S, hd = q.shape
    offs = jnp.arange(-n_side, n_side + 1) * dilation
    bias = -slopes[:, None] * jnp.abs(offs).astype(jnp.float32)[None, :]
    scale = hd ** -0.5

    def block(i):
        start = i * DIL_QBLOCK
        qb = lax.dynamic_slice_in_dim(q, start, DIL_QBLOCK, axis=2)
        pos = start + jnp.arange(DIL_QBLOCK)
        idx = pos[:, None] + offs[None, :]
        valid = (idx >= 0) & (idx < S)
        idxc = jnp.clip(idx, 0, S - 1)
        kb = k[:, :, idxc]
        vb = v[:, :, idxc]
        s = jnp.einsum('bhqd,bhqkd->bhqk', qb, kb).astype(jnp.float32) * scale + bias[None, :, None, :]
        s = jnp.where(valid[None, None], s, -1e30)
        lse = jax.nn.logsumexp(s, axis=-1)
        p = jnp.exp(s - lse[..., None]).astype(v.dtype)
        o = jnp.einsum('bhqk,bhqkd->bhqd', p, vb)
        return o, lse

    o, lse = lax.map(block, jnp.arange(S // DIL_QBLOCK))
    o = jnp.moveaxis(o, 0, 2).reshape(B, Hg, S, hd)
    lse = jnp.moveaxis(lse, 0, 2).reshape(B, Hg, S)
    return o, lse

def token_mixer(h, mem_n, w_in, b_gate, lb_f, lb_b, g_hg, w_mem_kv, w_up, w_out):
    B, S, D = h.shape
    f32 = jnp.float32
    sizes = [HG_WIDTH] * 5 + [DIL_WIDTH] * 3 + [MEM_WIDTH] + [D_MODEL] * N_BRANCH
    cuts = np.cumsum(sizes)[:-1].tolist()
    proj = h @ w_in
    (hq, hi, hff, hfb, hgate, dq, dk, dv, mq, gate_cols) = (
        *jnp.split(proj, cuts[:9], axis=-1)[:9], proj[..., cuts[8]:])

    def heads(t, nh, d):
        return t.reshape(B, S, nh, d).transpose(0, 2, 1, 3)

    def forget(z, lb):
        f = lb + (1.0 - lb) * jax.nn.sigmoid(z.astype(f32))
        return heads(1.0 - f, HG_HEADS, HG_DK), heads(jnp.log(f), HG_HEADS, HG_DK)

    q_hg = heads(hq.astype(f32), HG_HEADS, HG_DK)
    v_hg = heads(hi.astype(f32), HG_HEADS, HG_DV)
    k_f, logf_f = forget(hff, lb_f)
    k_b, logf_b = forget(hfb, lb_b)
    o_fwd = hgrn2_scan(q_hg, k_f, v_hg, logf_f)
    flip = lambda t: jnp.flip(t, axis=2)
    o_bwd = flip(hgrn2_scan(flip(q_hg), flip(k_b), flip(v_hg), flip(logf_b)))
    o_hg = o_fwd + o_bwd
    o_hg = o_hg * lax.rsqrt(jnp.mean(o_hg * o_hg, axis=-1, keepdims=True) + EPS) * g_hg.astype(f32)
    o_hg = o_hg.transpose(0, 2, 1, 3).reshape(B, S, HG_WIDTH)
    o_hg = (o_hg * jax.nn.silu(hgate.astype(f32))).astype(h.dtype)

    dq = heads(dq, DIL_HEADS, DIL_HEAD_DIM)
    dk = heads(dk, DIL_HEADS, DIL_HEAD_DIM)
    dv = heads(dv, DIL_HEADS, DIL_HEAD_DIM)
    slopes = jnp.exp2(-ALIBI_MAX * jnp.arange(1, DIL_HEADS + 1, dtype=f32) / DIL_HEADS)
    outs, lses = [], []
    for gi, (window, dil) in enumerate(DIL_GROUPS):
        sl = slice(gi * DIL_HEADS_PER_GROUP, (gi + 1) * DIL_HEADS_PER_GROUP)
        n_side = (window // 2) // dil
        o_g, lse_g = dilated_group_attn(dq[:, sl], dk[:, sl], dv[:, sl], slopes[sl], dil, n_side)
        outs.append(o_g)
        lses.append(lse_g)
    alpha = jax.nn.softmax(jnp.stack(lses, axis=0), axis=0)
    o_dil = jnp.concatenate(
        [alpha[gi][..., None].astype(h.dtype) * outs[gi] for gi in range(len(DIL_GROUPS))], axis=1)
    o_dil = o_dil.transpose(0, 2, 1, 3).reshape(B, S, DIL_WIDTH)

    q_m = heads(mq, MEM_HEADS, MEM_HEAD_DIM)
    kv = mem_n @ w_mem_kv
    M = kv.shape[1]
    k_m = kv[..., :MEM_WIDTH].reshape(B, M, MEM_HEADS, MEM_HEAD_DIM).transpose(0, 2, 1, 3)
    v_m = kv[..., MEM_WIDTH:].reshape(B, M, MEM_HEADS, MEM_HEAD_DIM).transpose(0, 2, 1, 3)
    s_m = jnp.einsum('bhqd,bhkd->bhqk', q_m, k_m).astype(f32) * (MEM_HEAD_DIM ** -0.5)
    p_m = jax.nn.softmax(s_m, axis=-1).astype(v_m.dtype)
    o_mem = jnp.einsum('bhqk,bhkd->bhqd', p_m, v_m).transpose(0, 2, 1, 3).reshape(B, S, MEM_WIDTH)

    gates = jax.nn.sigmoid((gate_cols + b_gate).astype(f32)).reshape(B, S, N_BRANCH, D).astype(h.dtype)
    w_up_hg, w_up_dil, w_up_mem = jnp.split(w_up, [HG_WIDTH, HG_WIDTH + DIL_WIDTH], axis=0)
    merged = (gates[:, :, 0] * (o_hg @ w_up_hg)
              + gates[:, :, 1] * (o_dil @ w_up_dil)
              + gates[:, :, 2] * (o_mem @ w_up_mem))
    return merged @ w_out

def peer_ffn(h, w_q, sub_keys, expert_u, expert_v):
    B, S, D = h.shape
    T = B * S
    xt = h.reshape(T, D)
    q = (xt @ w_q).reshape(T, PEER_HEADS, 2, PEER_HALF)
    s = jnp.einsum('thpc,pnc->thpn', q, sub_keys).astype(jnp.float32)
    top_s, top_i = lax.top_k(s, PEER_TOPK)
    cand_s = top_s[:, :, 0, :, None] + top_s[:, :, 1, None, :]
    cand_i = top_i[:, :, 0, :, None] * PEER_NKEYS + top_i[:, :, 1, None, :]
    kk = PEER_TOPK * PEER_TOPK
    best_s, best_pos = lax.top_k(cand_s.reshape(T, PEER_HEADS, kk), PEER_TOPK)
    expert_idx = jnp.take_along_axis(cand_i.reshape(T, PEER_HEADS, kk), best_pos, axis=-1)
    gate = jax.nn.softmax(best_s, axis=-1).astype(h.dtype)
    nb = T // PEER_TBLOCK
    n_sel = PEER_HEADS * PEER_TOPK
    xb = xt.reshape(nb, PEER_TBLOCK, D)
    ib = expert_idx.reshape(nb, PEER_TBLOCK, n_sel)
    gb = gate.reshape(nb, PEER_TBLOCK, n_sel)

    def block(args):
        xs, idx, g = args
        u_sel = expert_u[idx]
        a = jnp.einsum('tkd,td->tk', u_sel, xs)
        hid = jax.nn.gelu(a, approximate=False) * g
        return jnp.einsum('tk,tkd->td', hid, expert_v[idx])

    out = lax.map(block, (xb, ib, gb))
    return out.reshape(B, S, D)

def setup_inputs(seed: int = 0) -> dict:
    key = jax.random.key(seed)
    ks = jax.random.split(key, 20)
    f32 = jnp.float32

    def nrm(k, shape, scale):
        return jax.random.normal(k, shape, f32) * scale

    D = D_MODEL
    return {
        "x": nrm(ks[0], (BATCH, SEQ, D), 1.0),
        "mem": nrm(ks[1], (BATCH, MEM_LEN, D), 1.0),
        "g_mix": 1.0 + nrm(ks[2], (DEPTH, D), 0.02),
        "w_in": nrm(ks[3], (DEPTH, D, N_IN), D ** -0.5),
        "b_gate": nrm(ks[4], (DEPTH, N_BRANCH * D), 0.02),
        "lb_fwd_logits": nrm(ks[5], (DEPTH + 1, HG_WIDTH), 0.1),
        "lb_bwd_logits": nrm(ks[6], (DEPTH + 1, HG_WIDTH), 0.1),
        "g_hgrn": 1.0 + nrm(ks[7], (DEPTH, HG_DV), 0.02),
        "w_mem_kv": nrm(ks[8], (DEPTH, D, 2 * MEM_WIDTH), D ** -0.5),
        "g_mem": 1.0 + nrm(ks[9], (DEPTH, D), 0.02),
        "w_up": nrm(ks[10], (DEPTH, MIX_WIDTH, D), MIX_WIDTH ** -0.5),
        "w_out": nrm(ks[11], (DEPTH, D, D), D ** -0.5),
        "g_ffn": 1.0 + nrm(ks[12], (DEPTH, D), 0.02),
        "w_peer_q": nrm(ks[13], (DEPTH, D, PEER_HEADS * PEER_QDIM), D ** -0.5),
        "peer_sub_keys": nrm(ks[14], (DEPTH, 2, PEER_NKEYS, PEER_HALF), PEER_HALF ** -0.5),
        "peer_u": nrm(ks[15], (DEPTH, PEER_N_EXPERTS, D), D ** -0.5),
        "peer_v": nrm(ks[16], (DEPTH, PEER_N_EXPERTS, D), 0.5),
        "g_final": 1.0 + nrm(ks[17], (D,), 0.02),
    }

def reference(x, mem, g_mix, w_in, b_gate, lb_fwd_logits, lb_bwd_logits, g_hgrn, w_mem_kv, g_mem,
              w_up, w_out, g_ffn, w_peer_q, peer_sub_keys, peer_u, peer_v, g_final):
    lb_f_all = jnp.cumsum(jax.nn.softmax(lb_fwd_logits.astype(jnp.float32), axis=0), axis=0)
    lb_b_all = jnp.cumsum(jax.nn.softmax(lb_bwd_logits.astype(jnp.float32), axis=0), axis=0)
    for l in range(DEPTH):
        h = rmsnorm(x, g_mix[l])
        mem_n = rmsnorm(mem, g_mem[l])
        x = x + token_mixer(h, mem_n, w_in[l], b_gate[l], lb_f_all[l], lb_b_all[l], g_hgrn[l],
                            w_mem_kv[l], w_up[l], w_out[l])
        x = x + peer_ffn(rmsnorm(x, g_ffn[l]), w_peer_q[l], peer_sub_keys[l], peer_u[l], peer_v[l])
    return rmsnorm(x, g_final)


_drawn_inputs = setup_inputs


def setup_inputs(seed=0):
    import zlib

    import numpy as np

    out = dict(_drawn_inputs(seed))
    spreads = {}
    factors = {'b_gate': 5.08, 'g_hgrn': 14.327, 'g_mem': 7.655, 'g_final': 7.988, 'g_ffn': 3.147}
    for name, (base, spread) in spreads.items():
        noise = np.random.default_rng([zlib.crc32(name.encode()), seed]).standard_normal(out[name].shape)
        drawn = base * np.exp(spread * noise) if base else spread * noise
        out[name] = __import__('jax').numpy.asarray(drawn.astype(out[name].dtype))
    for name, factor in factors.items():
        out[name] = (out[name] * factor).astype(out[name].dtype)
    return out
```

```python
from contextlib import ExitStack

import concourse.bass as bass
from concourse import mybir

ALU = mybir.AluOpType
ACT = mybir.ActivationFunctionType
F32 = mybir.dt.float32
F32R = mybir.dt.float32r
U32 = mybir.dt.uint32
I32 = mybir.dt.int32
AX_X = mybir.AxisListType.X

P = 128
D = 2048
KT = D // P
T = 512
TT = T // P
MEM = 256
MT = MEM // P
EPS = 1e-6
HG = 6
DIL_G = 3
DIL_S = 2
MH = 4
PH = 8
TOPK = 16
NK = 128
LEVELS = [64, 32, 16, 8, 4, 2, 1]
HT = 8
HW = HT * P
DMW = T + 3 * P
NEG = -3.0e38

N_KV = 2 * MH
N_MQ = MH
N_DIL = 3 * DIL_G
N_DIL_GATES = 3
N_D = N_DIL + N_DIL_GATES
N_HGC = 5
N_HG_GATES = 7
N_H = N_HGC + N_HG_GATES
N_GATE = 3 * KT
C_MQ = N_KV
C_D = C_MQ + N_MQ
C_H = C_D + DIL_S * N_D
C_UP = C_H + HG * N_H
C_OUT = C_UP + KT
C_PQ = C_OUT + KT
C_U = C_PQ + 2 * PH
C_V = C_U + NK
HALVES = 2 * (C_V + NK)
U_1, U_2, U_3, U_B, U_C = 24, 8, 8, 64, 24
TB = 32
NTB = T // TB
assert DIL_S * N_DIL_GATES + HG * N_HG_GATES == N_GATE

C_ID, C_ONE, C_DM = 0, P, 2 * P
C_SCAN = C_DM + 3 * DMW
C_IOTA = C_SCAN + TT * (P + 1)
C_IO16 = C_IOTA + P
C_SL = C_IO16 + TOPK
NCONST = C_SL + 12
P_MIX, P_MEM, P_FFN, P_FIN = 0, KT, 2 * KT, 3 * KT
P_BG = 4 * KT
P_LBF = P_BG + N_GATE
P_LBB = P_LBF + 2 * HG
P_HG = P_LBB + 2 * HG
NPRM = P_HG + 1


class Steps:

    def __init__(self, sem, names, base=0):
        self.sem, self.names, self.n = sem, list(names), len(names)
        self.where = {s: k + 1 for k, s in enumerate(self.names)}
        self.base, self.next = base, 0
        assert len(self.where) == self.n

    def done(self, instruction, name):
        assert self.names[self.next % self.n] == name, (self.names[self.next % self.n], name)
        self.next += 1
        instruction.then_inc(self.sem, 1)

    def at(self, name, it=0):
        return it * self.n + (self.base + self.where[name])

    def wait(self, eng, name, it=0):
        eng.wait_ge(self.sem, self.at(name, it))

    def wait_iterations(self, eng, it):
        eng.wait_ge(self.sem, it * self.n + self.base)


def norm_names():
    act = [f"sq{k}" for k in range(KT)] + ["sqrt"] + [f"hi{k}" for k in range(KT)]
    pe = [f"mm{k}" for k in range(KT)]
    dve = ["ms", "rcp"]
    for k in range(KT):
        dve += [f"xn{k}"] + ([f"lo{k - 1}"] if k else [])
    return act, pe, dve + [f"lo{KT - 1}"]


def mem_names():
    u = [(h, tt) for h in range(MH) for tt in range(TT)]
    pe = [f"vt{h}" for h in range(MH)] + [f"sc{h}{tt}" for h, tt in u[:2]]
    for k, (h, tt) in enumerate(u):
        pe += [f"pt{h}{tt}", f"pv{h}{tt}"] + ([f"sc{u[k + 2][0]}{u[k + 2][1]}"] if k + 2 < len(u) else [])
    dve = [f"vm{h}" for h in range(MH)]
    for h, tt in u:
        dve += [f"{s}{h}{tt}" for s in ("mx", "nm", "rc", "sp", "ev")] + ([f"ov{h}"] if tt == TT - 1 else [])
    return pe, dve, [f"ex{h}{tt}" for h, tt in u]


TRIPLES = [(tt, a) for tt in range(TT) for a in range(2)]


def dil_names():
    pe = [f"vt{g}" for g in range(3)]
    dve = ["slopes"] + [f"vp{g}{a}" for g in range(3) for a in range(2)]
    act = []
    for q in range(len(TRIPLES)):
        pe += [f"{s}{q}{g}" for s in ("sc", "pt", "pv") for g in range(3)]
        for g in range(3):
            dve += [f"sm{q}{g}", f"mx{q}{g}"]
        dve += [f"{s}{q}" for s in ("nm", "mm", "dd", "zs", "z", "rz", "w")]
        dve += [f"sp{q}{g}" for g in range(3)] + [f"ev{q}{g}" for g in range(3)]
        act += [f"ed{q}"] + [f"ex{q}{g}" for g in range(3)]
    return pe, dve + [f"od{g}" for g in range(3)], act


def hg_names():
    dve = ["par", "f0", "f1", "k0", "k1", "ks", "vn", "sc0", "sc1", "t00", "t01", "a0"]
    act = ["ln0", "ln1"]
    for l in range(7):
        if l < 6:
            dve += [f"t{l + 1}0", f"t{l + 1}1"]
        dve += [f"qo{l}", f"qe{l}", f"ke{l}", f"ko{l}"]
        if l:
            dve += [f"wait{l - 1}", f"cp{l - 1}"]
        act += [f"ee{l}", f"eo{l}"]
    dve += ["ts0", "ts1", "wait6", "cp6", "qs0", "ks0", "qs1", "ks1", "et0", "et1",
            "sf1", "sb2", "sf2", "sb1", "sf3", "sb0", "silu", "ms", "rcp", "o1", "o2"]
    act += ["dec", "x10", "x20", "x11", "x21", "sq", "sqrt"]
    pe = ["vt", "p0"] + [f"pl{l}" for l in range(7)] + ["kt0", "kt1", "u0", "u1", "o", "nm"]
    return pe, dve, act


def topk_names():
    dve = ["cp"]
    for w, s in ((0, "ma"), (1, "ia"), (None, "mr"), (2, "mb"), (3, "ib")):
        dve += [f"wait{w}"] * (w is not None) + [f"{s}{x}{p}" for x in range(TT) for p in range(2)]
    dve += ["if", "cand"]
    for w, s in ((4, "Ma"), (5, "Ia"), (None, "Mr"), (6, "Mb"), (7, "Ib")):
        dve += [f"wait{w}"] * (w is not None) + [f"{s}{x}" for x in range(TT)]
    return dve + ["sub", "hi", "lo", "hif", "lof", "eq0", "pr0", "out0", "eq1", "pr1", "out1"]


def encoder_block_kernel(nc, x_t, mem_t, const, level_mask, params, sub_keys_t,
                         w_kv, w_in, w_up, w_out, w_pq, w_u, w_v, out_t):
    ctx = ExitStack()
    with ctx:
        def sb(name, shape, dt=F32):
            return ctx.enter_context(nc.sbuf_tensor(name, shape, dt))

        def sem(name):
            return ctx.enter_context(nc.semaphore(name))

        def dram(name, shape):
            return nc.dram_tensor(name, shape, F32, kind="Internal").ap()

        gate_dram = dram("gate_scratch", [N_GATE, P, T])
        mix_dram = dram("mix_scratch", [KT, P, T])
        res_dram = dram("residual_scratch", [KT, P, T])
        act_dram = dram("gelu_scratch", [NK, P, T])
        gmat_dram = dram("gate_matrix_scratch", [NTB, P, NK, TB])

        raw = [sb(f"w_raw{s}", [P, HT, P]) for s in range(4)]
        whi = [sb(f"w_hi{s}", [P, HT, P], F32R) for s in range(4)]
        wlo = [sb(f"w_lo{s}", [P, HT, P], F32R) for s in range(4)]
        xhi = sb("x_hi", [P, KT, T], F32R)
        xlo = sb("x_lo", [P, KT, T], F32R)
        ghi = sb("gate_hi", [P, T], F32R)
        glo = sb("gate_lo", [P, T], F32R)
        oh_i = sb("onehot_i", [P, 8, P], F32R)
        oh_jh = sb("onehot_j_gate_hi", [P, 8, P], F32R)
        oh_jl = sb("onehot_j_gate_lo", [P, 8, P], F32R)
        cst = sb("constants", [P, NCONST])
        lmask = sb("level_masks", [P, 7, P], I32)
        prm = sb("parameters", [P, NPRM])
        lbt = sb("lower_bounds", [P, HG, 4])
        small = sb("small", [P, 160])
        WA = 15400
        arena = sb("arena", [P, WA])

        ident = cst[:, C_ID:C_ID + P]
        ones = cst[:, C_ONE:C_ONE + P]
        dist = cst[:, C_DM:C_DM + 3 * DMW].rearrange("p (g w) -> p g w", g=3)
        scan_ones = cst[:, C_SCAN:C_SCAN + TT * (P + 1)]
        iota = cst[:, C_IOTA:C_IOTA + P]
        iota16 = cst[:, C_IO16:C_IO16 + TOPK]

        bank = [ctx.enter_context(nc.psum_tensor(f"bank{b}", [P, T], F32)) for b in range(8)]
        acc = bank[0:2]

        w_loaded = [sem(f"w_loaded{s}") for s in range(4)]
        w_hi_made = sem("w_hi_made")
        w_lo_made = sem("w_lo_made")
        half_done = sem("half_done")
        acc_free = sem("acc_free")
        consts_in = sem("consts_in")
        mem_in = sem("mem_in")
        x_in = sem("x_in")
        lb_dve = sem("lower_bound_dve")
        lb_act = sem("lower_bound_act")
        pads_zero = sem("pads_zero")
        gate_out = [sem(f"gate_columns_out{b}") for b in range(2)]
        mem_out = [sem(f"mem_out{b}") for b in range(2)]
        dil_out = sem("dil_out")
        hg_out = sem("hg_out")
        mix_in = [sem(f"mix_in{b}") for b in range(4)]
        mix_hi = sem("mix_hi")
        mix_lo = sem("mix_lo")
        gate_in = [sem(f"gate_columns_in{b}") for b in range(2)]
        gates_made = sem("gates_made")
        merged_hi = sem("merged_hi")
        merged_lo = sem("merged_lo")
        xres_in = [sem(f"xres_in{b}") for b in range(2)]
        out_read = sem("out_read")
        residual_out = sem("residual_out")
        sub_keys_in = sem("sub_keys_in")
        acc2_free = sem("acc2_free")
        score_done = sem("score_done")
        score_saved = sem("score_saved")
        gate_exp = sem("gate_exp")
        gate_soft = sem("gate_soft")
        sel_turned = sem("sel_turned")
        sel_saved = sem("sel_saved")
        block_cols = sem("block_cols")
        onehots = sem("onehots")
        gmat_done = sem("gmat_done")
        gmat_saved = sem("gmat_saved")
        gmat_out = [sem(f"gmat_out{b}") for b in range(2)]
        gelu_out = [sem(f"gelu_out{b}") for b in range(2)]
        residual_in = sem("residual_in")
        gmat_in = [sem(f"gmat_in{b}") for b in range(2)]
        gelu_in = [sem(f"gelu_in{b}") for b in range(2)]
        hid_product = sem("hid_product")
        hid_hi = sem("hid_hi")
        hid_lo = sem("hid_lo")
        y_added = sem("y_added")
        result_out = [sem(f"result_out{b}") for b in range(2)]
        na, npe, nd = norm_names()
        scaled_only = [s for s in nd if not s.startswith("lo")]
        norm = [(Steps(sem(f"norm_act{r}"), na), Steps(sem(f"norm_pe{r}"), npe),
                 Steps(sem(f"norm_dve{r}"), nd if r < 3 else scaled_only)) for r in range(4)]
        mp, md, ma = (Steps(sem(f"mem_{e}"), n) for e, n in zip(("pe", "dve", "act"), mem_names()))
        dp, dd, da = (Steps(sem(f"dil_{e}"), n, b) for e, n, b in zip(("pe", "dve", "act"), dil_names(), (0, 1, 0)))
        hp, hd, ha = (Steps(sem(f"hg_{e}"), n, b) for e, n, b in zip(("pe", "dve", "act"), hg_names(), (0, 1, 0)))
        UP = ["bg", "m1", "m2", "m3", "a1", "a2"]
        up = Steps(sem("merge_dve"), UP, 2 * len(UP))
        tk = Steps(sem("topk_dve"), topk_names(), 1)

        def carve(at, *shape):
            n = 1
            for k in shape:
                n *= k
            assert at + n <= WA, (at, shape)
            v = arena[:, at:at + n]
            names = "abcd"[:len(shape)]
            if len(shape) > 1:
                v = v.rearrange(f"p ({' '.join(names)}) -> p {' '.join(names)}",
                                **{k: s for k, s in zip(names[:-1], shape[:-1])})
            return v

        class Area:
            def __init__(self, at=0):
                self.at = at

            def __call__(self, *shape):
                v = carve(self.at, *shape)
                n = 1
                for k in shape:
                    n *= k
                self.at += n
                return v

        a = Area()
        src_x = a(KT, T)
        src_mem = a(KT, MEM)
        nsq = a(2, T)
        ntmp = a(2, T)
        nrm = a(T)
        a = Area()
        qm = a(MH, T)
        vm = a(MT, MH, P)
        pm = a(2, MEM)
        ptm = a(2, MT, P)
        om = a(2, T)
        m_end = a.at
        kvm = carve(KT * T, N_KV, MEM)
        vp = carve(m_end, 3, 2, TT, P)
        a = Area()
        pd = a(3, T)
        ptd = a(3, TT, P)
        od = a(3, T)
        assert a.at <= m_end and m_end + 3 * 2 * TT * P <= KT * T
        gst = carve(WA - 2 * T, 2, T)
        qkv = carve(WA - 2 * T - 9 * T, 3, 3, T)
        a = Area()
        hq = a(T)
        hv = a(T)
        hf = a(2, T)
        hk = a(2, T)
        hgt = a(T)
        hsg = a(T)
        hlf = a(2, TT, P + 1)
        hb = a(2, TT, P + 1)
        hksum = a(T)
        ht = a(2, T)
        he = a(2, T)
        hkl = a(2, T)
        hql = a(2, T)
        hqs = a(2, T)
        hkn = a(2, 3, P)
        hvn = a(TT, P)
        hst = a(2, 3, P)
        hres = a(T)
        assert a.at <= WA - 2 * T
        hkst = hf
        ham = hv.rearrange("p (a b) -> p a b", a=TT)
        hosq, hr = hkl[:, 0], hkl[:, 1]
        a = Area()
        merged = a(KT, T)
        ob = a(4, T)
        gt = a(2, 3, T)
        umul = a(2, T)
        xres = ob
        a = Area()
        qpt = a(2, T)
        scores = a(TT, 2 * PH, NK)
        sw = a(TT, 2, NK)
        sw2 = a(TT, 2, NK)
        cand = a(TT, TOPK, TOPK)
        cand2 = a(TT, TOPK, TOPK)
        sel = a(3, TT, P)
        v16 = a(TT, 2, TOPK)
        eq = sw.rearrange("p a b c -> p a (b c)").rearrange("p a (b c) -> p a b c", b=TOPK)
        eq2 = sw2.rearrange("p a b c -> p a (b c)").rearrange("p a (b c) -> p a b c", b=TOPK)
        tab = cst[:, C_DM:C_DM + 3 * DMW]
        i16 = tab[:, 0:128].bitcast(U32).rearrange("p (a b c) -> p a b c", a=TT, b=2)
        i16f = tab[:, 128:256].rearrange("p (a b c) -> p a b c", a=TT, b=2)
        best = tab[:, 256:320].rearrange("p (a b) -> p a b", a=TT)
        pos = tab[:, 320:384].bitcast(U32).rearrange("p (a b) -> p a b", a=TT)
        phi = tab[:, 384:448].bitcast(U32).rearrange("p (a b) -> p a b", a=TT)
        plo = tab[:, 448:512].bitcast(U32).rearrange("p (a b) -> p a b", a=TT)
        phif = tab[:, 512:576].rearrange("p (a b) -> p a b", a=TT)
        plof = tab[:, 576:640].rearrange("p (a b) -> p a b", a=TT)
        bsum = tab[:, 768:800]
        brcp = tab[:, 800:832]
        cur = tab[:, 896:896 + 4 * TB].rearrange("p (a b) -> p a b", a=4)
        skt = tab[:, 1024:1024 + 2 * NK].rearrange("p (a b) -> p a b", a=2)
        eg = qpt
        gstage = carve(2 * T, 2, NK, TB)
        iit = carve(2 * T + 2 * NK * TB, T)
        jjt = carve(3 * T + 2 * NK * TB, T)
        gtt = carve(4 * T + 2 * NK * TB, T)
        assert 5 * T + 2 * NK * TB <= 2 * T + TT * 2 * PH * NK + 4096
        a = Area()
        y = a(KT, T)
        gsb = a(2, NTB, 4 * TB)
        agb = a(2, T)
        htmp = a(2, T)

        mxs = small[:, 0:8]
        dsl = small[:, 8:14]
        dmx, dnm, ddd, ded, dsum, dzs, dw = (small[:, 16 + 4 * k:19 + 4 * k] for k in range(7))
        dmm, dz, drz = (small[:, 44 + k:45 + k] for k in range(3))
        hpar = small[:, 56:60]
        hdec = small[:, 60:68].rearrange("p (d t) -> p d t", d=2)
        bgc = small[:, 68:74].rearrange("p (u b) -> p u b", u=2)
        lbs = small[:, 80:160]
        gate_cols = gate_dram.rearrange("(b j) p t -> j p b t", b=3)
        dil_tiles = mix_dram[HG:2 * HG].rearrange("(g s) p t -> s p g t", s=2)

        block = ctx.enter_context(nc.Block())

        @block.sync
        def _(sp):
            def stream(w, first):
                skip = 4 if first == 0 else 0
                for s in range(skip):
                    sp.dma_start(raw[s][:], w[s]).then_inc(w_loaded[s], 16)
                with sp.Fori(skip // 4, w.shape[0] // 4) as i:
                    for s in range(4):
                        sp.wait_ge(w_lo_made, 4 * i + (first + s - 3))
                        sp.dma_start(raw[s][:], w[4 * i + s]).then_inc(w_loaded[s], 16)

            m = 0
            for w in (w_kv, w_in, w_up, w_out, w_pq, w_u, w_v):
                stream(w, m)
                m += w.shape[0]
            assert m == HALVES

        @block.gpsimd
        def _(pool):
            with pool.Fori(0, HALVES // 4) as i:
                for s in range(4):
                    pool.wait_ge(w_hi_made, 4 * i + (s + 1))
                    nc.gpsimd.tensor_tensor(wlo[s][:], raw[s][:], whi[s][:], ALU.subtract).then_inc(w_lo_made, 1)

        @block.scalar
        def _(act):
            A = nc.scalar

            def round_half(q, s, first=False):
                act.wait_ge(w_loaded[s], 16 * q + 16)
                if not first:
                    act.wait_ge(half_done, 4 * q + (s - 3))
                A.activation(whi[s][:], raw[s][:], ACT.Copy).then_inc(w_hi_made, 1)

            def ahead(n, i, per, part):
                m = 2 * n + 4 + part
                round_half(i * (per // 2) + m // 4, m % 4)

            def chunk_ready(n, i, per):
                act.wait_ge(half_done, i * (2 * per) + (2 * n + 2))

            act.dma_start(src_mem, mem_t).then_inc(mem_in, 16)
            act.dma_start(cst[:], const).then_inc(consts_in, 16)
            act.dma_start(prm[:], params).then_inc(consts_in, 16)
            act.dma_start(lmask[:], level_mask).then_inc(consts_in, 16)
            act.dma_start(src_x, x_t).then_inc(x_in, 16)
            act.sem_inc(acc_free, 2)
            for s_ in (*gate_out, dil_out, hg_out, *gelu_out, *gmat_out):
                act.sem_inc(s_, 16)
            for s_ in (gates_made, gmat_saved, score_saved):
                act.sem_inc(s_, 1)
            for s in range(4):
                round_half(0, s, first=True)

            def norm_squares(r, src, width):
                na_, np_, _ = norm[r]
                for k in range(KT):
                    if k >= 2:
                        np_.wait(act, f"mm{k - 2}")
                    na_.done(A.activation(nsq[:, k % 2, 0:width], src[:, k], ACT.Square), f"sq{k}")

            def norm_root(r, width):
                norm[r][2].wait(act, "ms")
                norm[r][0].done(A.activation(nrm[:, 0:width], nrm[:, 0:width], ACT.Sqrt), "sqrt")

            def norm_hi(r, width):
                for k in range(KT):
                    norm[r][2].wait(act, f"xn{k}")
                    norm[r][0].done(A.activation(xhi[:, k, 0:width], ntmp[:, k % 2, 0:width], ACT.Copy), f"hi{k}")

            act.wait_ge(mem_in, 16)
            norm_squares(0, src_mem, MEM)
            norm_root(0, MEM)
            norm_hi(0, MEM)
            act.wait_ge(lb_dve, 6)
            A.activation(lbs[:, 24:48], lbs[:, 0:24], ACT.Exp).then_inc(lb_act, 1)
            act.wait_ge(x_in, 16)
            norm[0][1].wait(act, f"mm{KT - 1}")
            norm_squares(1, src_x, T)

            norm[0][2].wait(act, f"lo{KT - 1}")
            with act.Fori(0, N_KV // 2) as i:
                for u in range(2):
                    ahead(u, i, 2, 0)
                    chunk_ready(u, i, 2)
                    A.activation(kvm[:, 2 * i + u], acc[u][:, 0:MEM], ACT.Copy).then_inc(acc_free, 1)
                    ahead(u, i, 2, 1)
            norm_root(1, T)
            norm_hi(1, T)
            norm[1][2].wait(act, f"lo{KT - 1}")
            with act.Fori(0, N_MQ // 2) as i:
                for u in range(2):
                    ahead(C_MQ + u, i, 2, 0)
                    chunk_ready(C_MQ + u, i, 2)
                    A.activation(qm[:, 2 * i + u], acc[u][:], ACT.Copy).then_inc(acc_free, 1)
                    ahead(C_MQ + u, i, 2, 1)
            for h in range(MH):
                for tt in range(TT):
                    u = (h * TT + tt) % 2
                    md.wait(act, f"nm{h}{tt}")
                    ma.done(A.activation(pm[:, u], bank[2 + u][:, 0:MEM], ACT.Exp, bias=mxs[:, 2 + u:3 + u],
                                         scale=float(P) ** -0.5, accum_out=mxs[:, 4 + u:5 + u]), f"ex{h}{tt}")
                if h:
                    md.wait(act, f"ov{h - 1}")
                    act.dma_start(mix_dram[2 * HG + h - 1], om[:, (h - 1) % 2]).then_inc(mem_out[(h - 1) % 2], 16)
            md.wait(act, f"ov{MH - 1}")
            act.dma_start(mix_dram[2 * HG + MH - 1], om[:, (MH - 1) % 2]).then_inc(mem_out[(MH - 1) % 2], 16)

            def gate_chunk_out(n, i, per, b, waited, tile):
                act.wait_ge(gate_out[b], waited + 16)
                A.activation(gst[:, b], acc[n % 2][:], ACT.Copy).then_inc(acc_free, 1)

            def gate_store(n, i, per, b, tile):
                act.wait_ge(acc_free, i * per + (n + 3))
                act.dma_start(gate_dram[tile], gst[:, b]).then_inc(gate_out[b], 16)

            with act.Fori(0, DIL_S) as i:
                for c in range(N_DIL):
                    n = C_D + c
                    ahead(n, i, N_D, 0)
                    chunk_ready(n, i, N_D)
                    if c == 0:
                        dd.wait_iterations(act, i)
                    A.activation(qkv[:, c // 3, c % 3], acc[n % 2][:], ACT.Copy,
                                 scale=0.125 if c < 3 else 1.0).then_inc(acc_free, 1)
                    ahead(n, i, N_D, 1)
                for q in range(len(TRIPLES)):
                    dd.wait(act, f"dd{q}", i)
                    da.done(A.activation(ded, ddd, ACT.Exp), f"ed{q}")
                    for g in range(3):
                        da.done(A.activation(pd[:, g], pd[:, g], ACT.Exp, bias=dnm[:, g:g + 1],
                                             accum_out=dsum[:, g:g + 1]), f"ex{q}{g}")
                    if q < 2 * N_DIL_GATES:
                        n = C_D + N_DIL + q // 2
                        x = q // 2
                        ahead(n, i, N_D, q % 2)
                        if q % 2:
                            chunk_ready(n, i, N_D)
                            gate_chunk_out(n, i, N_D, x % 2, i * (32 if x % 2 == 0 else 16) + 16 * (x // 2), None)
                            gate_store(n, i, N_D, x % 2, i * N_DIL_GATES + x)
                dd.wait(act, "od2", i)
                act.dma_start(dil_tiles[i], od).then_inc(dil_out, 16)

            act.wait_ge(dil_out, 16 * DIL_S + 16)
            act.wait_ge(mem_out[0], 32)
            act.wait_ge(mem_out[1], 32)
            act.wait_ge(pads_zero, 4)
            with act.Fori(0, HG) as i:
                for c in range(N_HGC):
                    n = C_H + c
                    a_ = acc[n % 2]
                    ahead(n, i, N_H, 0)
                    chunk_ready(n, i, N_H)
                    if c == 0:
                        hd.wait_iterations(act, i)
                        A.activation(hq, a_[:], ACT.Copy).then_inc(acc_free, 1)
                    elif c == 1:
                        A.activation(hv, a_[:], ACT.Copy).then_inc(acc_free, 1)
                    elif c < 4:
                        A.activation(hf[:, c - 2], a_[:], ACT.Sigmoid).then_inc(acc_free, 1)
                    else:
                        A.activation(hgt, a_[:], ACT.Copy)
                        A.activation(hsg, a_[:], ACT.Sigmoid).then_inc(acc_free, 1)
                    ahead(n, i, N_H, 1)
                for d in range(2):
                    hd.wait(act, f"f{d}", i)
                    ha.done(A.activation(hlf[:, d, :, 1:P + 1], hf[:, d].rearrange("p (a b) -> p a b", a=TT),
                                         ACT.Ln), f"ln{d}")
                for x in range(2 * N_HG_GATES):
                    n = C_H + N_HGC + x // 2
                    ahead(n, i, N_H, x % 2)
                    if x % 2:
                        g = x // 2
                        chunk_ready(n, i, N_H)
                        gate_chunk_out(n, i, N_H, g % 2, i * (64 if g % 2 == 0 else 48)
                                       + (16 * (g // 2) + (64 if g % 2 == 0 else 32)), None)
                    l = x - 1
                    if 0 <= l < 7:
                        blk = 2 * LEVELS[l]
                        te = ht.rearrange("p a b -> p (a b)").rearrange("p (m c) -> p m c", c=blk)
                        ee = he.rearrange("p a b -> p (a b)").rearrange("p (m c) -> p m c", c=blk)
                        hd.wait(act, f"t{l}1", i)
                        if l:
                            hd.wait(act, f"ko{l - 1}", i)
                        ha.done(A.activation(ee[:, :, 0:blk // 2], te[:, :, 0:blk // 2], ACT.Exp, scale=-1.0), f"ee{l}")
                        ha.done(A.activation(ee[:, :, blk // 2:blk], te[:, :, blk // 2:blk], ACT.Exp), f"eo{l}")
                    if x == 8:
                        hd.wait(act, "ts1", i)
                        ha.done(A.activation(hdec, hb[:, :, :, P], ACT.Exp), "dec")
                        for d in range(2):
                            if d:
                                hd.wait(act, "ks0", i)
                            ha.done(A.activation(he[:, 0].rearrange("p (a b) -> p a b", a=TT),
                                                 hb[:, d, :, 1 - d:P + 1 - d], ACT.Exp), f"x1{d}")
                            ha.done(A.activation(he[:, 1], ht[:, d], ACT.Exp, scale=-1.0), f"x2{d}")
                    if x == 12:
                        hp.wait(act, "o", i)
                        hd.wait(act, "sb0", i)
                        ha.done(A.activation(hosq, bank[2][:], ACT.Square), "sq")
                    if x % 2:
                        gate_store(n, i, N_H, g % 2, i * N_HG_GATES + (DIL_S * N_DIL_GATES + g))
                hd.wait(act, "ms", i)
                ha.done(A.activation(hr, hr, ACT.Sqrt), "sqrt")
                hd.wait(act, "o2", i)
                act.dma_start(mix_dram[i], hres).then_inc(hg_out, 16)

            act.dma_start(skt, sub_keys_t).then_inc(sub_keys_in, 16)

            act.wait_ge(hg_out, 16 * HG + 16)
            act.wait_ge(gate_out[0], 16 * (2 * DIL_S + 4 * HG) + 16)
            act.wait_ge(gate_out[1], 16 * (DIL_S + 3 * HG) + 16)
            hd.wait_iterations(act, HG)
            act.dma_start(gt[:, 0], gate_cols[0]).then_inc(gate_in[0], 16)
            for k in range(4):
                act.dma_start(ob[:, k], mix_dram[k]).then_inc(mix_in[k], 16)
            act.wait_ge(half_done, 2 * C_UP)
            for k in range(KT):
                act.wait_ge(mix_in[k % 4], 16 * (k // 4 + 1))
                A.activation(xhi[:, k], ob[:, k % 4], ACT.Copy).then_inc(mix_hi, 1)
                if 1 <= k <= KT - 4:
                    act.wait_ge(mix_lo, k)
                    act.dma_start(ob[:, (k - 1) % 4], mix_dram[k + 3]).then_inc(mix_in[(k - 1) % 4], 16)

            def merge_tile(u, i, last):
                if not last:
                    up.wait_iterations(act, 2 * i + u)
                    act.dma_start(gt[:, 1 - u], gate_cols[2 * i + (u + 1)]).then_inc(gate_in[1 - u], 16)
                ahead(C_UP + u, i, 2, 0)
                act.wait_ge(gate_in[u], 16 * i + 16)
                up.wait(act, "bg", 2 * i + u)
                for b in range(3):
                    A.activation(gt[:, u, b], gt[:, u, b], ACT.Sigmoid, bias=bgc[:, u, b:b + 1]).then_inc(gates_made, 1)
                ahead(C_UP + u, i, 2, 1)

            E2 = KT // 2 - 1
            with act.Fori(0, E2) as i:
                for u in range(2):
                    merge_tile(u, i, False)
            merge_tile(0, E2, False)
            merge_tile(1, E2, True)

            up.wait_iterations(act, KT)
            act.wait_ge(mix_lo, KT)
            act.dma_start(xres[:, 0], x_t[:, 0]).then_inc(xres_in[0], 16)
            act.wait_ge(half_done, 2 * C_OUT)
            for k in range(KT):
                A.activation(xhi[:, k], merged[:, k], ACT.Copy).then_inc(merged_hi, 1)

            def out_tile(u, i, last):
                if not last:
                    act.wait_ge(out_read, 2 * i + u + 1)
                    act.dma_start(xres[:, 1 - u], x_t[:, 2 * i + (u + 1)]).then_inc(xres_in[1 - u], 16)
                ahead(C_OUT + u, i, 2, 0)
                ahead(C_OUT + u, i, 2, 1)

            with act.Fori(0, E2) as i:
                for u in range(2):
                    out_tile(u, i, False)
            out_tile(0, E2, False)
            out_tile(1, E2, True)

            act.wait_ge(out_read, KT + 1)
            act.dma_start(res_dram.rearrange("k p t -> p k t"), y).then_inc(residual_out, 16)
            norm_squares(2, y, T)
            norm_root(2, T)
            norm_hi(2, T)
            act.wait_ge(residual_out, 16)
            norm[2][2].wait(act, f"lo{KT - 1}")
            act.sem_inc(acc2_free, 2)

            with act.Fori(0, PH) as i:
                for u in range(2):
                    ahead(C_PQ + u, i, 2, 0)
                    chunk_ready(C_PQ + u, i, 2)
                    A.activation(qpt[:, u], acc[u][:], ACT.Copy).then_inc(acc2_free, 1)
                    ahead(C_PQ + u, i, 2, 1)
                for u in range(2):
                    act.wait_ge(score_done, 2 * i + (u + 1))
                    A.activation(scores[:, :, 2 * i + u], bank[2 + u][:].rearrange("p (a b) -> p a b", a=TT), ACT.Copy)\
                        .then_inc(score_saved, 1)

            def expert_chunk(c, i, per):
                n = C_U + c
                u = c % 2
                ahead(n, i, per, 0)
                chunk_ready(n, i, per)
                act.wait_ge(gelu_out[u], i * (8 * per) + 16 * (c // 2) + 16)
                A.activation(eg[:, u], acc[n % 2][:], ACT.Gelu).then_inc(acc2_free, 1)
                ahead(n, i, per, 1)
                act.wait_ge(acc2_free, i * per + (2 * PH + c + 3))
                act.dma_start(act_dram[i * per + c], eg[:, u]).then_inc(gelu_out[u], 16)

            def expert_chunks(first, count):
                with act.Fori(0, count // 2) as i:
                    for u in range(2):
                        expert_chunk(first + u, i, 2)

            expert_chunks(0, U_1)
            tk.wait_iterations(act, PH)
            A.activation(sel[:, 2], sel[:, 2], ACT.Exp).then_inc(gate_exp, 1)
            expert_chunks(U_1, U_2)
            expert_chunks(U_1 + U_2, U_3)
            act.wait_ge(sel_saved, 5)
            first = U_1 + U_2 + U_3
            with act.Fori(0, NTB // 2) as i:
                for c in range(8):
                    expert_chunk(first + c, i, 8)
                    b = c // 4
                    if c % 4 == 0:
                        act.wait_ge(gmat_out[b], 16 * i + 16)
                    for g in range(2):
                        q = 2 * c + g
                        act.wait_ge(gmat_done, 16 * i + (q + 1) + 1)
                        t0 = 4 * (q % 8)
                        A.activation(gstage[:, b, :, t0:t0 + 4].rearrange("p j t -> p t j"),
                                     bank[2 + q % 2][:].rearrange("p (t j) -> p t j", t=4), ACT.Copy)\
                            .then_inc(gmat_saved, 1)
                    if c % 4 == 3:
                        act.wait_ge(gmat_saved, 16 * i + (2 * c + 2) + 1)
                        act.dma_start(gmat_dram[2 * i + b], gstage[:, b]).then_inc(gmat_out[b], 16)
            expert_chunks(first + U_B, U_C)

            for b in range(2):
                act.wait_ge(gmat_out[b], 16 * (NTB // 2) + 16)
                act.wait_ge(gelu_out[b], 16 * (NK // 2) + 16)
            act.dma_start(y, res_dram.rearrange("k p t -> p k t")).then_inc(residual_in, 16)

            def load_gates(s, r):
                act.dma_start(gsb[:, r], gmat_dram[:, :, bass.ds(8 * s + 4 * r, 4), :]
                              .rearrange("b p j t -> p b (j t)")).then_inc(gmat_in[r], 16)

            def load_gelu(s, k):
                act.dma_start(agb[:, k % 2], act_dram[8 * s + k]).then_inc(gelu_in[k % 2], 16)

            def hidden(s, k, half):
                act.wait_ge(hid_product, 8 * s + (k + 1))
                A.activation(xhi[:, 8 * half + k], htmp[:, k % 2], ACT.Copy).then_inc(hid_hi, 1)

            for r in range(2):
                load_gates(0, r)
                load_gelu(0, r)
            act.wait_ge(half_done, 2 * C_V)
            for k in range(8):
                hidden(0, k, 0)
                load_gelu(0 if k < 6 else 1, (k + 2) % 8)
                if k % 4 == 3:
                    load_gates(1, k // 4)

            def sub_block(s, par, prepare, more):
                for x in range(KT):
                    if prepare and x % 2 == 0:
                        k = x // 2
                        hidden(s + 1, k, 1 - par)
                        if k < 6:
                            load_gelu(s + 1, k + 2)
                        elif more:
                            load_gelu(s + 2, k - 6)
                        if more and k % 4 == 3:
                            load_gates(s + 2, k // 4)
                    m = 2 * C_V + KT * par + x + 4
                    if isinstance(s, int) and 2 * C_V + KT * s + x + 4 >= HALVES:
                        continue
                    if isinstance(s, int):
                        m = 2 * C_V + KT * s + x + 4
                        round_half(m // 4, m % 4)
                    else:
                        round_half((s - par) * 4 + m // 4, m % 4)

            with act.Fori(0, 7) as i:
                for par in range(2):
                    sub_block(2 * i + par, par, True, True)
            sub_block(14, 0, True, False)
            sub_block(15, 1, False, False)

            act.wait_ge(y_added, NK * 2)
            norm_squares(3, y, T)
            norm_root(3, T)
            for k in range(KT):
                norm[3][2].wait(act, f"xn{k}")
                act.dma_start(out_t[k], ntmp[:, k % 2]).then_inc(result_out[k % 2], 16)
            for b in range(2):
                act.wait_ge(result_out[b], 16 * (KT // 2))

        @block.vector
        def _(dve):
            V = nc.vector

            for s_ in (dd.sem, hd.sem, tk.sem, out_read, onehots):
                dve.sem_inc(s_, 1)
            dve.wait_ge(consts_in, 48)
            lgt = prm[:, P_LBF:P_LBF + 24].rearrange("p (d l h) -> p d l h", d=2, l=2)
            sh = lbs[:, 0:24].rearrange("p (d l h) -> p d l h", d=2, l=2)
            ex = lbs[:, 24:48].rearrange("p (d l h) -> p d l h", d=2, l=2)
            mx = lbs[:, 48:60].rearrange("p (d h) -> p d h", d=2)
            sm = lbs[:, 60:72].rearrange("p (d h) -> p d h", d=2)
            count = [0]

            def pause(steps, after, name, it):
                steps.wait(dve, after, it)
                steps.done(V.memset(small[:, 76:77], 0.0), name)

            def link(ins):
                count[0] += 1
                ins.then_inc(lb_dve, 1)
                dve.wait_ge(lb_dve, count[0])

            link(V.tensor_tensor(mx[:, 0], lgt[:, 0, 0], lgt[:, 0, 1], ALU.max))
            link(V.tensor_tensor(mx[:, 1], lgt[:, 1, 0], lgt[:, 1, 1], ALU.max))
            for d in range(2):
                for l in range(2):
                    link(V.tensor_tensor(sh[:, d, l], lgt[:, d, l], mx[:, d], ALU.subtract))

            def norm_rest(r, src, width, gcol, outputs):
                na_, np_, nd_ = norm[r]
                b = bank[7 - r % 2]
                np_.wait(dve, f"mm{KT - 1}")
                nd_.done(V.tensor_scalar(nrm[:, 0:width], b[:, 0:width], 1.0 / D, EPS, ALU.mult, ALU.add), "ms")
                na_.wait(dve, "sqrt")
                nd_.done(V.reciprocal(nrm[:, 0:width], nrm[:, 0:width]), "rcp")
                nd_.wait(dve, "rcp")

                def lo(k):
                    na_.wait(dve, f"hi{k}")
                    nd_.done(V.tensor_tensor(xlo[:, k, 0:width], ntmp[:, k % 2, 0:width],
                                             xhi[:, k, 0:width], ALU.subtract), f"lo{k}")

                for k in range(KT):
                    if not outputs and k >= 2:
                        dve.wait_ge(result_out[k % 2], 16 * (k // 2))
                    if outputs and k >= 2:
                        nd_.wait(dve, f"lo{k - 2}")
                    nd_.done(V.scalar_tensor_tensor(ntmp[:, k % 2, 0:width], src[:, k], prm[:, gcol + k:gcol + k + 1],
                                                    nrm[:, 0:width], ALU.mult, ALU.mult), f"xn{k}")
                    if outputs and k:
                        lo(k - 1)
                if outputs:
                    lo(KT - 1)

            dve.wait_ge(mem_in, 16)
            norm_rest(0, src_mem, MEM, P_MEM, True)
            dve.wait_ge(lb_act, 1)
            for d in range(2):
                link(V.tensor_tensor(sm[:, d], ex[:, d, 0], ex[:, d, 1], ALU.add))
            link(V.reciprocal(sm, sm))
            for d in range(2):
                link(V.tensor_tensor(lbt[:, :, 2 * d], ex[:, d, 0], sm[:, d], ALU.mult))
            for d in range(2):
                link(V.tensor_scalar(lbt[:, :, 2 * d + 1], lbt[:, :, 2 * d], -1.0, 1.0, ALU.mult, ALU.add))
            dve.wait_ge(x_in, 16)
            dve.wait_ge(half_done, 2 * N_KV)
            norm_rest(1, src_x, T, P_MIX, True)

            for h in range(MH):
                mp.wait(dve, f"vt{h}")
                md.done(V.tensor_copy(vm[:, :, h, :], bank[4 + h % 2][:, 0:MEM].rearrange("p (a b) -> p a b", a=MT)),
                        f"vm{h}")
            for h in range(MH):
                for tt in range(TT):
                    u = (h * TT + tt) % 2
                    mp.wait(dve, f"sc{h}{tt}")
                    md.done(V.reduce_max(mxs[:, u:u + 1], bank[2 + u][:, 0:MEM], AX_X), f"mx{h}{tt}")
                    md.wait(dve, f"mx{h}{tt}")
                    md.done(V.tensor_scalar(mxs[:, 2 + u:3 + u], mxs[:, u:u + 1], -float(P) ** -0.5, None, ALU.mult),
                            f"nm{h}{tt}")
                    ma.wait(dve, f"ex{h}{tt}")
                    md.done(V.reciprocal(mxs[:, 6 + u:7 + u], mxs[:, 4 + u:5 + u]), f"rc{h}{tt}")
                    md.wait(dve, f"rc{h}{tt}")
                    md.done(V.tensor_scalar(pm[:, u], pm[:, u], mxs[:, 6 + u:7 + u], None, ALU.mult), f"sp{h}{tt}")
                    mp.wait(dve, f"pt{h}{tt}")
                    md.done(V.tensor_copy(ptm[:, u], bank[4 + u][:, 0:MEM].rearrange("p (a b) -> p a b", a=MT)),
                            f"ev{h}{tt}")
                if h >= 2:
                    dve.wait_ge(mem_out[h % 2], 16)
                mp.wait(dve, f"pv{h}{TT - 1}")
                md.done(V.tensor_copy(om[:, h % 2], bank[6 + h % 2][:]), f"ov{h}")

            V.memset(vp, 0.0).then_inc(pads_zero, 1)
            dve.wait_ge(pads_zero, 1)
            dve.wait_ge(mem_out[0], 32)
            dve.wait_ge(mem_out[1], 32)
            md.wait(dve, f"ov{MH - 1}")
            with dve.Fori(0, DIL_S) as i:
                dd.done(V.tensor_copy(dsl, cst[:, bass.ds(C_SL + 6 * i, 6)]), "slopes")
                for g in range(3):
                    dp.wait(dve, f"vt{g}", i)
                    for a_ in range(2):
                        vals = bank[2 + g][:].rearrange("p (s c) -> p s c", s=TT)
                        dd.done(V.tensor_copy(vp[:, g, a_, :, 64 * a_:64 * a_ + 64], vals[:, :, 64 * a_:64 * a_ + 64]),
                                f"vp{g}{a_}")
                dd.wait(dve, "slopes", i)
                for q, (tt, a_) in enumerate(TRIPLES):
                    for g in range(3):
                        dp.wait(dve, f"sc{q}{g}", i)
                        dd.done(V.scalar_tensor_tensor(pd[:, g], dist[:, g, 3 * P - P * tt:3 * P - P * tt + T],
                                                       dsl[:, 2 * g + a_:2 * g + a_ + 1], bank[2 + g][:],
                                                       ALU.mult, ALU.add), f"sm{q}{g}")
                        dd.wait(dve, f"sm{q}{g}", i)
                        dd.done(V.reduce_max(dmx[:, g:g + 1], pd[:, g], AX_X), f"mx{q}{g}")
                    dd.wait(dve, f"mx{q}2", i)
                    dd.done(V.tensor_scalar(dnm, dmx, -1.0, None, ALU.mult), f"nm{q}")
                    dd.done(V.reduce_max(dmm, dmx, AX_X), f"mm{q}")
                    dd.wait(dve, f"mm{q}", i)
                    dd.done(V.tensor_scalar(ddd, dmx, dmm, None, ALU.subtract), f"dd{q}")
                    da.wait(dve, f"ex{q}2", i)
                    dd.done(V.tensor_tensor(dzs, ded, dsum, ALU.mult), f"zs{q}")
                    dd.wait(dve, f"zs{q}", i)
                    dd.done(V.reduce_sum(dz, dzs, AX_X), f"z{q}")
                    dd.wait(dve, f"z{q}", i)
                    dd.done(V.reciprocal(drz, dz), f"rz{q}")
                    dd.wait(dve, f"rz{q}", i)
                    dd.done(V.tensor_scalar(dw, ded, drz, None, ALU.mult), f"w{q}")
                    dd.wait(dve, f"w{q}", i)
                    for g in range(3):
                        dd.done(V.tensor_scalar(pd[:, g], pd[:, g], dw[:, g:g + 1], None, ALU.mult), f"sp{q}{g}")
                    for g in range(3):
                        dp.wait(dve, f"pt{q}{g}", i)
                        dd.done(V.tensor_copy(ptd[:, g], bank[2 + g][:].rearrange("p (a b) -> p a b", a=TT)),
                                f"ev{q}{g}")
                dve.wait_ge(dil_out, 16 * i + 16)
                dp.wait(dve, f"pv{len(TRIPLES) - 1}2", i)
                for g in range(3):
                    dd.done(V.tensor_copy(od[:, g], bank[5 + g][:]), f"od{g}")

            dd.wait_iterations(dve, DIL_S)
            dve.wait_ge(dil_out, 16 * DIL_S + 16)
            dp.wait(dve, f"pv{len(TRIPLES) - 1}2", DIL_S - 1)
            for d in range(2):
                V.memset(hlf[:, d, :, 0:1], 0.0).then_inc(pads_zero, 1)
            V.memset(hst, 0.0).then_inc(pads_zero, 1)
            with dve.Fori(0, HG) as i:
                hd.done(V.tensor_copy(hpar, lbt[:, i]), "par")
                for d in range(2):
                    dve.wait_ge(acc_free, i * N_H + (C_H + 2 + d + 3))
                    hd.wait(dve, "par", i)
                    hd.done(V.tensor_scalar(hf[:, d], hf[:, d], hpar[:, 2 * d + 1:2 * d + 2], hpar[:, 2 * d:2 * d + 1],
                                            ALU.mult, ALU.add), f"f{d}")
                for d in range(2):
                    hd.wait(dve, f"f{d}", i)
                    hd.done(V.tensor_scalar(hk[:, d], hf[:, d], -1.0, 1.0, ALU.mult, ALU.add), f"k{d}")
                hd.wait(dve, "k1", i)
                hd.done(V.tensor_tensor(hksum, hk[:, 0], hk[:, 1], ALU.add), "ks")
                hp.wait(dve, "vt", i)
                hd.done(V.tensor_copy(hvn, bank[2][:].rearrange("p (a b) -> p a b", a=TT)), "vn")
                for d in range(2):
                    ha.wait(dve, f"ln{d}", i)
                    hd.done(V.tensor_tensor_scan(hb[:, d].rearrange("p a b -> p (a b)"), scan_ones,
                                                 hlf[:, d].rearrange("p a b -> p (a b)"), 0.0, ALU.mult, ALU.add),
                            f"sc{d}")
                hd.wait(dve, "sc1", i)

                def level_diff(l):
                    L = LEVELS[l]
                    for d in range(2):
                        b = hb[:, d, :, 1 - d:P + 1 - d].rearrange("p a (m c) -> p a m c", c=2 * L)
                        ref = hb[:, d, :, L:P:2 * L] if 2 * L < P else hb[:, d, :, L:L + 1]
                        if l:
                            ha.wait(dve, f"eo{l - 1}", i)
                        o = ht[:, d].rearrange("p (a m c) -> p a m c", a=TT, c=2 * L)
                        hd.done(V.tensor_tensor(o, b, ref.unsqueeze(3).broadcast_to([P, TT, P // (2 * L), 2 * L]),
                                                ALU.subtract), f"t{l}{d}")

                level_diff(0)
                hp.wait(dve, "p0", i)
                hd.done(V.tensor_copy(ham, bank[3][:].rearrange("p (a b) -> p a b", a=TT)), "a0")

                def keep_level(l):
                    hp.wait(dve, f"pl{l}", i)
                    pause(hd, f"cp{l - 1}" if l else "a0", f"wait{l}", i)
                    hd.done(V.copy_predicated(ham, lmask[:, l:l + 1, :].broadcast_to([P, TT, P]),
                                              bank[4 + l % 2][:].rearrange("p (a b) -> p a b", a=TT)), f"cp{l}")

                for l in range(7):
                    L = LEVELS[l]
                    if l < 6:
                        level_diff(l + 1)
                    ha.wait(dve, f"eo{l}", i)
                    if l >= 2:
                        hp.wait(dve, f"pl{l - 2}", i)

                    def half(ap, odd):
                        return ap.rearrange("p (m c) -> p m c", c=2 * L)[:, :, L * odd:L * odd + L]

                    b = l % 2
                    hd.done(V.tensor_tensor(half(hql[:, b], 1), half(hq, 1), half(he[:, 0], 1), ALU.mult), f"qo{l}")
                    hd.done(V.tensor_tensor(half(hql[:, b], 0), half(hq, 0), half(he[:, 1], 0), ALU.mult), f"qe{l}")
                    hd.done(V.tensor_tensor(half(hkl[:, b], 0), half(hk[:, 0], 0), half(he[:, 0], 0), ALU.mult), f"ke{l}")
                    hd.done(V.tensor_tensor(half(hkl[:, b], 1), half(hk[:, 1], 1), half(he[:, 1], 1), ALU.mult), f"ko{l}")
                    if l:
                        keep_level(l - 1)
                for d in range(2):
                    ha.wait(dve, "eo6", i)
                    hd.done(V.tensor_tensor(ht[:, d].rearrange("p (a b) -> p a b", a=TT),
                                            hb[:, d, :, 1 - d:P + 1 - d],
                                            hb[:, d, :, P:P + 1].broadcast_to([P, TT, P]), ALU.subtract), f"ts{d}")
                keep_level(6)
                for d in range(2):
                    ha.wait(dve, f"x2{d}", i)
                    hd.done(V.tensor_tensor(hqs[:, d], hq, he[:, d], ALU.mult), f"qs{d}")
                    hd.done(V.tensor_tensor(hkst[:, d], hk[:, d], he[:, 1 - d], ALU.mult), f"ks{d}")
                for d in range(2):
                    hp.wait(dve, f"kt{d}", i)
                    hd.done(V.tensor_copy(hkn[:, d], bank[4 + d][:, 0:3 * P].rearrange("p (a b) -> p a b", a=3)),
                            f"et{d}")
                hp.wait(dve, "u1", i)
                uf, ub = bank[6], bank[7]
                hd.done(V.tensor_copy(hst[:, 0, 0], uf[:, 0:P]), "sf1")
                hd.done(V.tensor_copy(hst[:, 1, 2], ub[:, 2 * P:3 * P]), "sb2")
                hd.wait(dve, "sb2", i)
                hd.done(V.scalar_tensor_tensor(hst[:, 0, 1], hst[:, 0, 0], hdec[:, 0, 1:2], uf[:, P:2 * P],
                                               ALU.mult, ALU.add), "sf2")
                hd.done(V.scalar_tensor_tensor(hst[:, 1, 1], hst[:, 1, 2], hdec[:, 1, 2:3], ub[:, P:2 * P],
                                               ALU.mult, ALU.add), "sb1")
                hd.wait(dve, "sb1", i)
                hd.done(V.scalar_tensor_tensor(hst[:, 0, 2], hst[:, 0, 1], hdec[:, 0, 2:3], uf[:, 2 * P:3 * P],
                                               ALU.mult, ALU.add), "sf3")
                hd.done(V.scalar_tensor_tensor(hst[:, 1, 0], hst[:, 1, 1], hdec[:, 1, 1:2], ub[:, 0:P],
                                               ALU.mult, ALU.add), "sb0")
                hd.done(V.tensor_tensor(hsg, hsg, hgt, ALU.mult), "silu")
                hp.wait(dve, "nm", i)
                hd.done(V.tensor_scalar(hr, bank[3][:], 1.0 / P, EPS, ALU.mult, ALU.add), "ms")
                ha.wait(dve, "sqrt", i)
                hd.done(V.reciprocal(hr, hr), "rcp")
                hd.wait(dve, "rcp", i)
                dve.wait_ge(hg_out, 16 * i + 16)
                hd.done(V.scalar_tensor_tensor(hres, bank[2][:], prm[:, P_HG:P_HG + 1], hr, ALU.mult, ALU.mult), "o1")
                hd.wait(dve, "o1", i)
                hd.done(V.tensor_tensor(hres, hres, hsg, ALU.mult), "o2")

            for k in range(KT):
                dve.wait_ge(mix_hi, k + 1)
                V.tensor_tensor(xlo[:, k], ob[:, k % 4], xhi[:, k], ALU.subtract).then_inc(mix_lo, 1)
            dve.wait_ge(hg_out, 16 * HG + 16)
            dve.sem_inc(up.sem, 2 * len(UP))
            bg_v = prm[:, P_BG:P_BG + N_GATE].rearrange("p (b j) -> p b j", b=3)
            with dve.Fori(0, KT // 2) as i:
                for u in range(2):
                    j = 2 * i + u
                    dve.wait_ge(gates_made, 6 * i + 3 * u + 1)
                    up.done(V.tensor_copy(bgc[:, u], bg_v[:, :, 2 * i + u]), "bg")
                    dve.wait_ge(gates_made, 6 * i + (3 * u + 3) + 1)
                    dve.wait_ge(half_done, 4 * i + (2 * C_UP + 2 * u + 2))
                    bk = bank[3 * u:3 * u + 3]
                    up.done(V.tensor_tensor(merged[:, 2 * i + u], gt[:, u, 0], bk[0][:], ALU.mult), "m1")
                    up.done(V.tensor_tensor(umul[:, 0], gt[:, u, 1], bk[1][:], ALU.mult), "m2")
                    up.done(V.tensor_tensor(umul[:, 1], gt[:, u, 2], bk[2][:], ALU.mult), "m3")
                    up.wait(dve, "m2", j)
                    up.done(V.tensor_tensor(merged[:, 2 * i + u], merged[:, 2 * i + u], umul[:, 0], ALU.add), "a1")
                    up.wait(dve, "a1", j)
                    up.done(V.tensor_tensor(merged[:, 2 * i + u], merged[:, 2 * i + u], umul[:, 1], ALU.add), "a2")

            for k in range(KT):
                dve.wait_ge(merged_hi, k + 1)
                V.tensor_tensor(xlo[:, k], merged[:, k], xhi[:, k], ALU.subtract).then_inc(merged_lo, 1)
            with dve.Fori(0, KT // 2) as i:
                for u in range(2):
                    dve.wait_ge(xres_in[u], 16 * i + 16)
                    dve.wait_ge(half_done, 4 * i + (2 * C_OUT + 2 * u + 2))
                    dve.wait_ge(merged_lo, KT)
                    V.tensor_tensor(y[:, 2 * i + u], xres[:, u], acc[u][:], ALU.add).then_inc(out_read, 1)
            dve.wait_ge(out_read, KT + 1)
            norm_rest(2, y, T, P_FFN, True)

            with dve.Fori(0, PH) as i:
                dve.wait_ge(score_saved, 2 * i + 2 + 1)
                tk.wait_iterations(dve, i)
                pairs = [(x, p) for x in range(TT) for p in range(2)]
                tk.done(V.tensor_copy(sw, scores[:, :, bass.ds(2 * i, 2), :]), "cp")
                pause(tk, "cp", "wait0", i)
                for x, p in pairs:
                    tk.done(V.max(v16[:, x, p, 0:8], sw[:, x, p]), f"ma{x}{p}")
                pause(tk, "ma31", "wait1", i)
                for x, p in pairs:
                    tk.done(V.max_index(i16[:, x, p, 0:8], v16[:, x, p, 0:8], sw[:, x, p]), f"ia{x}{p}")
                for x, p in pairs:
                    tk.done(V.match_replace(sw2[:, x, p], v16[:, x, p, 0:8], sw[:, x, p], NEG), f"mr{x}{p}")
                pause(tk, "mr31", "wait2", i)
                for x, p in pairs:
                    tk.done(V.max(v16[:, x, p, 8:16], sw2[:, x, p]), f"mb{x}{p}")
                pause(tk, "mb31", "wait3", i)
                for x, p in pairs:
                    tk.done(V.max_index(i16[:, x, p, 8:16], v16[:, x, p, 8:16], sw2[:, x, p]), f"ib{x}{p}")
                tk.wait(dve, "ib31", i)
                tk.done(V.tensor_copy(i16f, i16), "if")
                tk.done(V.tensor_tensor(cand, v16[:, :, 0].unsqueeze(3).broadcast_to([P, TT, TOPK, TOPK]),
                                        v16[:, :, 1].unsqueeze(2).broadcast_to([P, TT, TOPK, TOPK]), ALU.add), "cand")
                pause(tk, "cand", "wait4", i)
                cf = cand.rearrange("p a b c -> p a (b c)")
                cf2 = cand2.rearrange("p a b c -> p a (b c)")
                for x in range(TT):
                    tk.done(V.max(best[:, x, 0:8], cf[:, x]), f"Ma{x}")
                pause(tk, "Ma3", "wait5", i)
                for x in range(TT):
                    tk.done(V.max_index(pos[:, x, 0:8], best[:, x, 0:8], cf[:, x]), f"Ia{x}")
                for x in range(TT):
                    tk.done(V.match_replace(cf2[:, x], best[:, x, 0:8], cf[:, x], NEG), f"Mr{x}")
                pause(tk, "Mr3", "wait6", i)
                for x in range(TT):
                    tk.done(V.max(best[:, x, 8:16], cf2[:, x]), f"Mb{x}")
                pause(tk, "Mb3", "wait7", i)
                for x in range(TT):
                    tk.done(V.max_index(pos[:, x, 8:16], best[:, x, 8:16], cf2[:, x]), f"Ib{x}")
                tk.done(V.tensor_tensor(sel[:, 2, :, bass.ds(TOPK * i, TOPK)], best,
                                        best[:, :, 0:1].broadcast_to([P, TT, TOPK]), ALU.subtract), "sub")
                tk.wait(dve, "Ib3", i)
                tk.done(V.tensor_scalar(phi, pos, 4, None, ALU.logical_shift_right), "hi")
                tk.done(V.tensor_scalar(plo, pos, 15, None, ALU.bitwise_and), "lo")
                tk.wait(dve, "lo", i)
                tk.done(V.tensor_copy(phif, phi), "hif")
                tk.done(V.tensor_copy(plof, plo), "lof")
                for p, f in ((0, phif), (1, plof)):
                    tk.wait(dve, "lof", i)
                    tk.done(V.tensor_tensor(
                        eq.rearrange("p a b c -> p (a b) c"), f.rearrange("p a b -> p (a b)").unsqueeze(2).broadcast_to([P, TT * TOPK, TOPK]),
                        iota16.unsqueeze(1).broadcast_to([P, TT * TOPK, TOPK]), ALU.is_equal), f"eq{p}")
                    tk.wait(dve, f"eq{p}", i)
                    tk.done(V.tensor_tensor(eq2, eq, i16f[:, :, p].unsqueeze(2).broadcast_to([P, TT, TOPK, TOPK]),
                                            ALU.mult), f"pr{p}")
                    tk.wait(dve, f"pr{p}", i)
                    tk.done(V.reduce_sum(sel[:, p, :, bass.ds(TOPK * i, TOPK)], eq2, AX_X), f"out{p}")
            dve.wait_ge(gate_exp, 1)
            e = sel[:, 2].rearrange("p a (h k) -> p (a h) k", k=TOPK)
            V.reduce_sum(bsum, e, AX_X).then_inc(gate_soft, 1)
            dve.wait_ge(gate_soft, 1)
            V.reciprocal(brcp, bsum).then_inc(gate_soft, 1)
            dve.wait_ge(gate_soft, 2)
            V.tensor_tensor(e, e, brcp.unsqueeze(2).broadcast_to([P, TT * PH, TOPK]), ALU.mult).then_inc(gate_soft, 1)
            dve.wait_ge(sel_turned, 3)
            V.tensor_copy(iit, bank[4][:]).then_inc(sel_saved, 1)
            V.tensor_copy(jjt, bank[5][:]).then_inc(sel_saved, 1)
            V.tensor_copy(gtt, bank[6][:]).then_inc(sel_saved, 1)
            dve.wait_ge(sel_saved, 3)
            V.tensor_copy(ghi[:], gtt).then_inc(sel_saved, 1)
            dve.wait_ge(sel_saved, 4)
            V.tensor_tensor(glo[:], gtt, ghi[:], ALU.subtract).then_inc(sel_saved, 1)
            dve.wait_ge(sel_saved, 5)
            with dve.Fori(0, NTB // 2) as i:
                for b in range(2):
                    for k, s in enumerate((iit, jjt, ghi[:].bitcast(F32), glo[:].bitcast(F32))):
                        dve.wait_ge(onehots, 16 * i + 8 * b + 1)
                        V.tensor_copy(cur[:, k], s[:, bass.ds((2 * TB) * i + TB * b, TB)]).then_inc(block_cols, 1)
                    dve.wait_ge(block_cols, 8 * i + (4 * b + 4))
                    for g in range(8):
                        q = 8 * b + g
                        dve.wait_ge(gmat_done, 16 * i + q - 1 + 1) if q >= 1 else dve.wait_ge(gmat_done, 16 * i + 1)
                        for x in range(4):
                            t, slot = 4 * g + x, 4 * (q % 2) + x
                            V.tensor_scalar(oh_i[:, slot], iota, cur[:, 0, t:t + 1], None, ALU.is_equal)
                            V.tensor_scalar(oh_jh[:, slot], iota, cur[:, 1, t:t + 1], cur[:, 2, t:t + 1],
                                            ALU.is_equal, ALU.mult)
                            last = V.tensor_scalar(oh_jl[:, slot], iota, cur[:, 1, t:t + 1], cur[:, 3, t:t + 1],
                                                   ALU.is_equal, ALU.mult)
                        last.then_inc(onehots, 1)

            dve.wait_ge(residual_in, 16)

            def product(s, k):
                dve.wait_ge(gmat_in[k // 4], 16 * s + 16)
                dve.wait_ge(gelu_in[k % 2], 64 * s + 16 * (k // 2 + 1))
                if not (isinstance(s, int) and s == 0 and k < 2):
                    dve.wait_ge(hid_lo, 8 * s + (k - 1))
                g4 = gsb[:, k // 4].rearrange("p b (j t) -> p b j t", j=4)
                V.tensor_tensor(htmp[:, k % 2].rearrange("p (b t) -> p b t", b=NTB),
                                agb[:, k % 2].rearrange("p (b t) -> p b t", b=NTB), g4[:, :, k % 4], ALU.mult)\
                    .then_inc(hid_product, 1)

            def low_part(s, k, half):
                dve.wait_ge(hid_hi, 8 * s + (k + 1))
                V.tensor_tensor(xlo[:, 8 * half + k], htmp[:, k % 2], xhi[:, 8 * half + k], ALU.subtract)\
                    .then_inc(hid_lo, 1)

            dve.wait_ge(half_done, 2 * C_V)
            for k in range(8):
                product(0, k)
                low_part(0, k, 0)

            def sub_block_add(s, par, prepare):
                for x in range(KT):
                    if prepare and x % 2 == 0:
                        product(s + 1, x // 2)
                    dve.wait_ge(half_done, KT * s + (2 * C_V + x + 1))
                    if not (isinstance(s, int) and s == 0):
                        dve.wait_ge(y_added, KT * s + (x + 1 - KT))
                    V.tensor_tensor(y[:, x], y[:, x], acc[x % 2][:], ALU.add).then_inc(y_added, 1)
                    if prepare and x % 2:
                        low_part(s + 1, x // 2, 1 - par)

            sub_block_add(0, 0, True)
            sub_block_add(1, 1, True)
            with dve.Fori(1, 7) as i:
                for par in range(2):
                    sub_block_add(2 * i + par, par, True)
            sub_block_add(14, 0, True)
            sub_block_add(15, 1, False)
            dve.wait_ge(y_added, 2 * NK)
            norm_rest(3, y, T, P_FIN, False)

        @block.tensor
        def _(pe):
            M = nc.tensor

            def half(m, s, out, tiles, k0, first, last, width=T):
                pe.wait_ge(w_lo_made, m + 1)
                for k in tiles:
                    h, l = xhi[:, k0 + k, 0:width], xlo[:, k0 + k, 0:width]
                    f, e = first and k == tiles[0], last and k == tiles[-1]
                    M.matmul(out, whi[s][:, k], h, start=f, stop=False)
                    M.matmul(out, whi[s][:, k], l, start=False, stop=False)
                    ins = M.matmul(out, wlo[s][:, k], h, start=False, stop=e)
                return ins

            def chunk_half(n, i, per, x, width=T, k0=0):
                s = (2 * n + x) % 4
                half(i * (2 * per) + (2 * n + x), s, acc[n % 2][:, 0:width], list(range(8)), 8 * x, x == 0, x == 1,
                     width).then_inc(half_done, 1)

            def take_acc(n, i, per):
                pe.wait_ge(acc_free, i * per + (n + 1))

            def take_acc2(n, i, per):
                pe.wait_ge(acc2_free, i * per + (n - C_PQ + 1))

            def norm_sums(r, width):
                na_, np_, _ = norm[r]
                for k in range(KT):
                    na_.wait(pe, f"sq{k}")
                    np_.done(M.matmul(bank[7 - r % 2][:, 0:width], ones, nsq[:, k % 2, 0:width],
                                      start=(k == 0), stop=(k == KT - 1)), f"mm{k}")

            pe.sem_inc(gmat_done, 1)
            pe.wait_ge(consts_in, 48)
            norm_sums(0, MEM)
            norm_sums(1, T)
            with pe.Fori(0, N_KV // 2) as i:
                for u in range(2):
                    take_acc(u, i, 2)
                    for x in range(2):
                        norm[0][2].wait(pe, f"lo{8 * x + 7}")
                        chunk_half(u, i, 2, x, MEM)
            with pe.Fori(0, N_MQ // 2) as i:
                for u in range(2):
                    take_acc(C_MQ + u, i, 2)
                    for x in range(2):
                        norm[1][2].wait(pe, f"lo{8 * x + 7}")
                        chunk_half(C_MQ + u, i, 2, x)

            pe.wait_ge(acc_free, C_D + 2)
            for h in range(MH):
                if h >= 2:
                    md.wait(pe, f"vm{h - 2}")
                for m in range(MT):
                    ins = M.transpose(bank[4 + h % 2][:, P * m:P * m + P], kvm[:, MH + h, P * m:P * m + P], ident)
                mp.done(ins, f"vt{h}")

            units = [(h, tt) for h in range(MH) for tt in range(TT)]

            def mem_scores(k):
                h, tt = units[k]
                if k >= 2:
                    ma.wait(pe, f"ex{units[k - 2][0]}{units[k - 2][1]}")
                mp.done(M.matmul(bank[2 + k % 2][:, 0:MEM], qm[:, h, P * tt:P * tt + P], kvm[:, h],
                                 start=True, stop=True), f"sc{h}{tt}")

            mem_scores(0)
            mem_scores(1)
            for k, (h, tt) in enumerate(units):
                u = k % 2
                md.wait(pe, f"sp{h}{tt}")
                if k < 2:
                    md.wait(pe, f"vm{MH - 1}")
                for m in range(MT):
                    ins = M.transpose(bank[4 + u][:, P * m:P * m + P], pm[:, u, P * m:P * m + P], ident)
                mp.done(ins, f"pt{h}{tt}")
                md.wait(pe, f"ev{h}{tt}")
                if tt == 0 and h >= 2:
                    md.wait(pe, f"ov{h - 2}")
                for m in range(MT):
                    ins = M.matmul(bank[6 + h % 2][:, P * tt:P * tt + P], vm[:, m, h], ptm[:, u, m],
                                   start=(m == 0), stop=(m == MT - 1))
                mp.done(ins, f"pv{h}{tt}")
                if k + 2 < len(units):
                    mem_scores(k + 2)

            md.wait(pe, f"ov{MH - 1}")
            pe.wait_ge(pads_zero, 1)
            with pe.Fori(0, DIL_S) as i:
                for c in range(N_DIL):
                    take_acc(C_D + c, i, N_D)
                    for x in range(2):
                        chunk_half(C_D + c, i, N_D, x)
                pe.wait_ge(acc_free, i * N_D + (C_D + N_DIL + 2))
                dd.wait_iterations(pe, i)
                for g in range(3):
                    for st in range(TT):
                        ins = M.transpose(bank[2 + g][:, P * st:P * st + P], qkv[:, 2, g, P * st:P * st + P], ident)
                    dp.done(ins, f"vt{g}")
                for q, (tt, a_) in enumerate(TRIPLES):
                    for g in range(3):
                        dd.wait(pe, f"ev{q - 1}{g}" if q else f"vp{g}1", i)
                        r = slice(64 * a_, 64 * a_ + 64)
                        dp.done(M.matmul(bank[2 + g][:], qkv[r, 0, g, P * tt:P * tt + P], qkv[r, 1, g],
                                         start=True, stop=True), f"sc{q}{g}")
                    if q < 2 * N_DIL_GATES:
                        n = C_D + N_DIL + q // 2
                        if q % 2 == 0:
                            take_acc(n, i, N_D)
                        chunk_half(n, i, N_D, q % 2)
                    for g in range(3):
                        dd.wait(pe, f"sp{q}{g}", i)
                        for st in range(TT):
                            ins = M.transpose(bank[2 + g][:, P * st:P * st + P], pd[:, g, P * st:P * st + P], ident)
                        dp.done(ins, f"pt{q}{g}")
                    for g in range(3):
                        dd.wait(pe, f"ev{q}{g}", i)
                        for st in range(TT):
                            ins = M.matmul(bank[5 + g][:, P * tt:P * tt + P], vp[:, g, a_, st], ptd[:, g, st],
                                           start=(a_ == 0 and st == 0), stop=(a_ == 1 and st == TT - 1))
                        dp.done(ins, f"pv{q}{g}")

            dd.wait_iterations(pe, DIL_S)
            with pe.Fori(0, HG) as i:
                for c in range(N_HGC):
                    take_acc(C_H + c, i, N_H)
                    for x in range(2):
                        chunk_half(C_H + c, i, N_H, x)

                def per_tile(out, lhs, rhs, name):
                    for tt in range(TT):
                        ins = M.matmul(out[:, P * tt:P * tt + P], lhs[:, P * tt:P * tt + P],
                                       rhs[:, P * tt:P * tt + P], start=True, stop=True)
                    hp.done(ins, name)

                for x in range(2 * N_HG_GATES):
                    n = C_H + N_HGC + x // 2
                    if x % 2 == 0:
                        take_acc(n, i, N_H)
                    chunk_half(n, i, N_H, x % 2)
                    if x == 0:
                        hd.wait_iterations(pe, i)
                        for tt in range(TT):
                            ins = M.transpose(bank[2][:, P * tt:P * tt + P], hv[:, P * tt:P * tt + P], ident)
                        hp.done(ins, "vt")
                    if x == 1:
                        hd.wait(pe, "ks", i)
                        per_tile(bank[3], hksum, hq, "p0")
                    l = x - 3
                    if 0 <= l < 7:
                        hd.wait(pe, f"ko{l}", i)
                        if l >= 2:
                            hd.wait(pe, f"cp{l - 2}", i)
                        per_tile(bank[4 + l % 2], hkl[:, l % 2], hql[:, l % 2], f"pl{l}")
                    if x == 10:
                        for d in range(2):
                            hd.wait(pe, f"ks{d}", i)
                            for k in range(3):
                                t0 = P * (k + d)
                                ins = M.transpose(bank[4 + d][:, P * k:P * k + P], hkst[:, d, t0:t0 + P], ident)
                            hp.done(ins, f"kt{d}")
                    if x == 11:
                        for d in range(2):
                            hd.wait(pe, f"et{d}", i)
                            for k in range(3):
                                ins = M.matmul(bank[6 + d][:, P * k:P * k + P], hkn[:, d, k], hvn[:, k + d],
                                               start=True, stop=True)
                            hp.done(ins, f"u{d}")
                    if x == 12:
                        hd.wait(pe, "sb0", i)
                        for tt in range(TT):
                            o = bank[2][:, P * tt:P * tt + P]
                            cols = slice(P * tt, P * tt + P)
                            if tt:
                                M.matmul(o, hst[:, 0, tt - 1], hqs[:, 0, cols], start=True, stop=False)
                            if tt < TT - 1:
                                M.matmul(o, hst[:, 1, tt], hqs[:, 1, cols], start=(tt == 0), stop=False)
                            ins = M.matmul(o, hvn[:, tt], ham[:, tt], start=False, stop=True)
                        hp.done(ins, "o")
                    if x == 13:
                        ha.wait(pe, "sq", i)
                        hp.done(M.matmul(bank[3][:], ones, hosq, start=True, stop=True), "nm")

            pe.wait_ge(acc_free, C_UP + 2)
            hd.wait_iterations(pe, HG)
            with pe.Fori(0, KT // 2) as i:
                for u in range(2):
                    up.wait(pe, "m3", 2 * i + (u - 2))
                    bk = [b[:] for b in bank[3 * u:3 * u + 3]]
                    m = 4 * i + (2 * C_UP + 2 * u)
                    pe.wait_ge(mix_lo, 8)
                    half(m, 2 * u, bk[0], range(6), 0, True, True)
                    half(m, 2 * u, bk[1], range(6, 8), 0, True, False).then_inc(half_done, 1)
                    pe.wait_ge(mix_lo, KT)
                    half(m + 1, 2 * u + 1, bk[1], range(4), 8, False, True)
                    half(m + 1, 2 * u + 1, bk[2], range(4, 8), 8, True, True).then_inc(half_done, 1)

            up.wait(pe, "m3", KT - 1)
            with pe.Fori(0, KT // 2) as i:
                for u in range(2):
                    if u == 0:
                        pe.wait_ge(out_read, 2 * i + 1)
                    for x in range(2):
                        pe.wait_ge(merged_lo, 8 * x + 8)
                        chunk_half(C_OUT + u, i, 2, x)
            norm_sums(2, T)

            pe.wait_ge(sub_keys_in, 16)
            with pe.Fori(0, PH) as i:
                def scores_of(u):
                    pe.wait_ge(acc2_free, 2 * i + (u + 3))
                    pe.wait_ge(score_saved, 2 * i + 1)
                    for tt in range(TT):
                        ins = M.matmul(bank[2 + u][:, P * tt:P * tt + P], qpt[:, u, P * tt:P * tt + P], skt[:, u],
                                       start=True, stop=True)
                    ins.then_inc(score_done, 1)

                for u in range(2):
                    take_acc2(C_PQ + u, i, 2)
                    for x in range(2):
                        norm[2][2].wait(pe, f"lo{8 * x + 7}")
                        chunk_half(C_PQ + u, i, 2, x)
                        if u == 1 and x == 0:
                            scores_of(0)
                scores_of(1)

            def expert_chunks(first, count):
                with pe.Fori(0, count // 2) as i:
                    for u in range(2):
                        n = C_U + first + u
                        take_acc2(n, i, 2)
                        for x in range(2):
                            chunk_half(n, i, 2, x)

            expert_chunks(0, U_1)
            expert_chunks(U_1, U_2)
            pe.wait_ge(gate_soft, 3)
            for k in range(3):
                for tt in range(TT):
                    ins = M.transpose(bank[4 + k][:, P * tt:P * tt + P], sel[:, k, tt], ident)
                ins.then_inc(sel_turned, 1)
            expert_chunks(U_1 + U_2, U_3)
            first = U_1 + U_2 + U_3
            with pe.Fori(0, NTB // 2) as i:
                for c in range(8):
                    n = C_U + first + c
                    take_acc2(n, i, 8)
                    for x in range(2):
                        chunk_half(n, i, 8, x)
                        q = 2 * c + x
                        pe.wait_ge(onehots, 16 * i + (q + 1) + 1)
                        pe.wait_ge(gmat_saved, (16 * i + (q - 1) if q else 16 * i) + 1)
                        for k in range(4):
                            o = bank[2 + q % 2][:, P * k:P * k + P]
                            slot = 4 * (q % 2) + k
                            M.matmul(o, oh_i[:, slot], oh_jh[:, slot], start=True, stop=False)
                            ins = M.matmul(o, oh_i[:, slot], oh_jl[:, slot], start=False, stop=True)
                        ins.then_inc(gmat_done, 1)
            expert_chunks(first + U_B, U_C)

            pe.wait_ge(acc2_free, 2 * PH + NK + 2)

            def sub_block_products(s, par):
                for x in range(KT):
                    if not (isinstance(s, int) and s == 0 and x < 2):
                        pe.wait_ge(y_added, KT * s + (x - 1))
                    pe.wait_ge(hid_lo, 8 * s + 8)
                    m = KT * s + (2 * C_V + x)
                    half(m, (2 * C_V + x) % 4, acc[x % 2][:], list(range(8)), 8 * par, True, True)\
                        .then_inc(half_done, 1)

            sub_block_products(0, 0)
            sub_block_products(1, 1)
            with pe.Fori(1, 8) as i:
                for par in range(2):
                    sub_block_products(2 * i + par, par)
            pe.wait_ge(y_added, 2 * NK)
            norm_sums(3, T)


def _constants():
    import numpy as np

    c = np.zeros((P, NCONST), np.float32)
    c[:, C_ID:C_ID + P] = np.eye(P)
    c[:, C_ONE:C_ONE + P] = 1
    gap = np.arange(DMW)[None, :] - 3 * P - np.arange(P)[:, None]
    for g, dil in enumerate((1, 4, 16)):
        ok = (gap % dil == 0) & (np.abs(gap) <= 64 * dil)
        c[:, C_DM + g * DMW:C_DM + (g + 1) * DMW] = np.where(ok, np.abs(gap), 1e32)
    s = np.ones((TT, P + 1))
    s[:, 0] = 0
    c[:, C_SCAN:C_SCAN + TT * (P + 1)] = s.reshape(-1)
    c[:, C_IOTA:C_IOTA + P] = np.arange(P)
    c[:, C_IO16:C_IO16 + TOPK] = np.arange(TOPK)
    heads = np.arange(12).reshape(3, 2, 2).transpose(1, 0, 2).reshape(-1)
    c[:, C_SL:C_SL + 12] = -np.exp2(-8.0 * (heads + 1) / 12)
    k = np.arange(P)
    m = np.zeros((P, 7, P), np.int32)
    for l, L in enumerate(LEVELS):
        blk, odd = k // (2 * L), (k // L) % 2
        m[:, l] = (blk[:, None] == blk[None, :]) & (odd[:, None] != odd[None, :])
    return c, m


def kernel(**inputs):
    import numpy as np
    import concourse.bacc as bacc
    from concourse import mybir as _mybir
    from concourse.bass_utils import run_bass_kernel_spmd

    a = {k: np.asarray(v) for k, v in inputs.items()}

    def cols(v):
        return v.reshape(-1, P).T

    def rows(v):
        return np.ascontiguousarray(v.T.reshape(KT, P, -1).transpose(1, 0, 2))

    def halves(w):
        n = w.shape[1] // P
        return np.ascontiguousarray(w.reshape(2, HT, P, n, P).transpose(3, 0, 2, 1, 4)).reshape(2 * n, P, HT, P)

    w_in = a["w_in"][0]
    hg = w_in[:, :5 * HG * P].reshape(D, 5, HG, P)
    dil = w_in[:, 5 * HG * P:5 * HG * P + 18 * P].reshape(D, 3, 3, 2, P)
    mq = w_in[:, 5 * HG * P + 18 * P:5 * HG * P + 18 * P + MH * P]
    gates = w_in[:, 5 * HG * P + 18 * P + MH * P:].reshape(D, N_GATE, P)
    order = [mq]
    g = 0
    for s in range(DIL_S):
        order += [dil[:, :, :, s].reshape(D, -1), gates[:, g:g + N_DIL_GATES].reshape(D, -1)]
        g += N_DIL_GATES
    for h in range(HG):
        order += [hg[:, :, h].reshape(D, -1), gates[:, g:g + N_HG_GATES].reshape(D, -1)]
        g += N_HG_GATES
    w_in = halves(np.concatenate(order, 1))

    u = a["peer_u"][0].reshape(P, NK, 2, HT, P).transpose(1, 2, 4, 3, 0)
    v = a["peer_v"][0].reshape(P, NK // 8, 8, KT, P).transpose(1, 3, 0, 2, 4)
    const, mask = _constants()
    prm = np.concatenate([cols(a["g_mix"][0]), cols(a["g_mem"][0]), cols(a["g_ffn"][0]), cols(a["g_final"]),
                          cols(a["b_gate"][0])]
                         + [cols(a[n][l]) for n in ("lb_fwd_logits", "lb_bwd_logits") for l in range(2)]
                         + [cols(a["g_hgrn"][0])], 1)
    arrays = {
        "x_t": rows(a["x"][0]), "mem_t": rows(a["mem"][0]), "const": const, "level_mask": mask,
        "params": np.ascontiguousarray(prm),
        "sub_keys_t": np.ascontiguousarray(a["peer_sub_keys"][0].transpose(2, 0, 1)),
        "w_kv": halves(a["w_mem_kv"][0]), "w_in": w_in, "w_up": halves(a["w_up"][0]),
        "w_out": halves(a["w_out"][0]), "w_pq": halves(a["w_peer_q"][0]),
        "w_u": np.ascontiguousarray(u).reshape(2 * NK, P, HT, P),
        "w_v": np.ascontiguousarray(v).reshape(2 * NK, P, HT, P),
    }
    nc = bacc.Bacc("TRN2", target_bir_lowering=False, num_devices=1)
    args = [nc.dram_tensor(n, x.shape, _mybir.dt.from_np(x.dtype), kind="ExternalInput").ap()
            for n, x in arrays.items()]
    out = nc.dram_tensor("out_t", [KT, P, T], _mybir.dt.float32, kind="ExternalOutput").ap()
    encoder_block_kernel(nc, *args, out)
    r = run_bass_kernel_spmd(nc, [arrays], core_ids=[0])
    got = np.asarray(r.results[0]["out_t"]).reshape(D, T)
    return np.ascontiguousarray(got.T).reshape(1, T, D)
```

```python
from contextlib import ExitStack

import concourse.bass as bass
from concourse import mybir

ALU = mybir.AluOpType
ACT = mybir.ActivationFunctionType
F32 = mybir.dt.float32
F32R = mybir.dt.float32r
U32 = mybir.dt.uint32
I32 = mybir.dt.int32
AX_X = mybir.AxisListType.X

P = 128
D = 2048
KT = D // P
T = 512
TT = T // P
MEM = 256
MT = MEM // P
EPS = 1e-6
HG = 6
DIL_G = 3
DIL_S = 2
MH = 4
PH = 8
TOPK = 16
NK = 128
LEVELS = [64, 32, 16, 8, 4, 2, 1]
HT = 8
HW = HT * P
DMW = T + 3 * P
NEG = -3.0e38

N_KV = 2 * MH
N_MQ = MH
N_DIL = 3 * DIL_G
N_MEM_GATES = 4
N_DIL_GATES = 1
N_D = N_DIL + N_DIL_GATES
N_HGC = 5
N_HG_GATES = 7
N_H = N_HGC + N_HG_GATES
N_GATE = 3 * KT
C_MQ = N_KV
C_MG = C_MQ + N_MQ
C_D = C_MG + N_MEM_GATES
C_H = C_D + DIL_S * N_D
C_UP = C_H + HG * N_H
C_OUT = C_UP + KT
C_PQ = C_OUT + KT
C_U = C_PQ + 2 * PH
C_V = C_U + NK
HALVES = 2 * (C_V + NK)
U_1, U_2, U_3, U_B, U_C = 24, 8, 8, 64, 24
TB = 32
NTB = T // TB
assert N_MEM_GATES + DIL_S * N_DIL_GATES + HG * N_HG_GATES == N_GATE
DILATIONS = (1, 4, 16)
REACH = 64

C_ID, C_ONE, C_DM = 0, P, 2 * P
C_SCAN = C_DM + 3 * DMW
C_IOTA = C_SCAN + TT * (P + 1)
C_IO16 = C_IOTA + P
C_SL = C_IO16 + TOPK
NCONST = C_SL + 12
P_MIX, P_MEM, P_FFN, P_FIN = 0, KT, 2 * KT, 3 * KT
P_BG = 4 * KT
P_LBF = P_BG + N_GATE
P_LBB = P_LBF + 2 * HG
P_HG = P_LBB + 2 * HG
NPRM = P_HG + 1


class Steps:

    def __init__(self, sem, names, base=0):
        self.sem, self.names, self.n = sem, list(names), len(names)
        self.where = {s: k + 1 for k, s in enumerate(self.names)}
        self.base, self.next = base, 0
        assert len(self.where) == self.n

    def done(self, instruction, name):
        assert self.names[self.next % self.n] == name, (self.names[self.next % self.n], name)
        self.next += 1
        instruction.then_inc(self.sem, 1)

    def at(self, name, it=0):
        return it * self.n + (self.base + self.where[name])

    def wait(self, eng, name, it=0):
        eng.wait_ge(self.sem, self.at(name, it))

    def wait_iterations(self, eng, it):
        eng.wait_ge(self.sem, it * self.n + self.base)


def norm_names(r):
    act = ["sqrt"] + [f"hi{k}" for k in range(KT)]
    xn, lo = [f"xn{k}" for k in range(KT)], [f"lo{k}" for k in range(KT)]
    dve = ["ms", "rcp"]
    if r in (0, 2):
        for k in range(KT):
            dve += [xn[k]] + ([lo[k - 1]] if k else [])
        return act, dve + [lo[-1]]
    return act, dve + xn + (lo if r == 1 else [])


def mem_names():
    u = [(h, tt) for h in range(MH) for tt in range(TT)]
    pe = [f"vt{h}" for h in range(MH)] + [f"sc{h}{tt}" for h, tt in u[:2]]
    for k, (h, tt) in enumerate(u):
        pe += [f"pt{h}{tt}", f"pv{h}{tt}"] + ([f"sc{u[k + 2][0]}{u[k + 2][1]}"] if k + 2 < len(u) else [])
    dve = [f"vm{h}" for h in range(MH)]
    for h, tt in u:
        dve += [f"{s}{h}{tt}" for s in ("mx", "nm", "rc", "sp", "ev")] + ([f"ov{h}"] if tt == TT - 1 else [])
    return pe, dve, [f"ex{h}{tt}" for h, tt in u]


PREPARED_AT = [0, 2, 4, 6, 8, 10, 12, 13]


def key_tiles(g, tt):
    r = -(-REACH * DILATIONS[g] // P)
    return max(0, tt - r), min(TT, tt + r + 1)


TRIPLES = [(tt, a) for tt in range(TT) for a in range(2)]


def dil_names():
    pe = [f"vt{g}" for g in range(3)]
    dve = ["slopes"] + [f"vp{g}{a}" for g in range(3) for a in range(2)]
    act = []
    n = len(TRIPLES)
    pe += [f"sc{q}{g}" for q in range(2) for g in range(3)]
    for q in range(n):
        pe += [f"{s}{r}{g}" for s, r in (("pt", q), ("sc", q + 2), ("pv", q)) if r < n for g in range(3)]
        for r in ([0, 1] if q == 0 else [q + 1] if q + 1 < n else []):
            for g in range(3):
                dve += [f"sm{r}{g}", f"mx{r}{g}"]
            dve += [f"{s}{r}" for s in ("nm", "mm", "dd")]
        dve += [f"{s}{q}" for s in ("zs", "z", "rz", "w")]
        dve += [f"sp{q}{g}" for g in range(3)] + [f"ev{q}{g}" for g in range(3)]
        act += [f"ed{q}"] + [f"ex{q}{g}" for g in range(3)]
    return pe, dve + [f"od{g}" for g in range(3)], act


def hg_names():
    dve = ["par", "f0", "f1", "k0", "k1", "ks", "vn", "sc0", "sc1", "t00", "t01", "a0"]
    act = ["ln0", "ln1"]
    for l in range(7):
        if l < 6:
            dve += [f"t{l + 1}0", f"t{l + 1}1"]
        dve += [f"qo{l}", f"qe{l}", f"ke{l}", f"ko{l}"]
        if l:
            dve += [f"wait{l - 1}", f"cp{l - 1}"]
        act += [f"ee{l}", f"eo{l}"]
    dve += ["ts0", "ts1", "wait6", "cp6", "qs0", "ks0", "qs1", "ks1", "et0", "et1",
            "sf1", "sb2", "sf2", "sb1", "sf3", "sb0", "silu", "ms", "rcp", "o1", "o2"]
    act += ["dec", "x10", "x20", "x11", "x21", "sq", "sqrt"]
    pe = ["vt", "p0"] + [f"pl{l}" for l in range(7)] + ["kt0", "kt1", "u0", "u1", "o", "nm"]
    return pe, dve, act


def topk_names():
    dve = ["cp"]
    for w, s in ((0, "ma"), (1, "ia"), (None, "mr"), (2, "mb"), (3, "ib")):
        dve += [f"wait{w}"] * (w is not None) + [f"{s}{x}{p}" for x in range(TT) for p in range(2)]
    dve += ["if", "cand"]
    for w, s in ((4, "Ma"), (5, "Ia"), (None, "Mr"), (6, "Mb"), (7, "Ib")):
        dve += [f"wait{w}"] * (w is not None) + [f"{s}{x}" for x in range(TT)]
    return dve + ["sub", "hi", "lo", "hif", "lof", "eq0", "pr0", "out0", "eq1", "pr1", "out1"]


def encoder_block_kernel(nc, x_t, mem_t, const, level_mask, params, sub_keys_t,
                         w_kv, w_in, w_up, w_out, w_pq, w_u, w_v, out_t):
    ctx = ExitStack()
    with ctx:
        def sb(name, shape, dt=F32):
            return ctx.enter_context(nc.sbuf_tensor(name, shape, dt))

        def sem(name):
            return ctx.enter_context(nc.semaphore(name))

        def dram(name, shape):
            return nc.dram_tensor(name, shape, F32, kind="Internal").ap()

        gate_dram = dram("gate_scratch", [N_GATE, P, T])
        mix_dram = dram("mix_scratch", [KT, P, T])
        res_dram = dram("residual_scratch", [KT, P, T])
        act_dram = dram("gelu_scratch", [NK, P, T])
        gmat_dram = dram("gate_matrix_scratch", [NTB, P, NK, TB])

        raw = [sb(f"w_raw{s}", [P, HT, P]) for s in range(4)]
        whi = [sb(f"w_hi{s}", [P, HT, P], F32R) for s in range(4)]
        wlo = [sb(f"w_lo{s}", [P, HT, P], F32R) for s in range(4)]
        xhi = sb("x_hi", [P, KT, T], F32R)
        xlo = sb("x_lo", [P, KT, T], F32R)
        early = sb("early_mix_or_one_hots", [P, 8, T])
        ghi, glo = early[:, 0].bitcast(F32R), early[:, 1].bitcast(F32R)
        oh_i = early[:, 2:4].rearrange("p a b -> p (a b)").rearrange("p (a b) -> p a b", b=P).bitcast(F32R)
        oh_j = early[:, 4:8].rearrange("p a b -> p (a b)").rearrange("p (a h b) -> p a h b", h=2, b=P).bitcast(F32R)
        cst = sb("constants", [P, NCONST])
        lmask = sb("level_masks", [P, 7, P], I32)
        prm = sb("parameters", [P, NPRM])
        lbt = sb("lower_bounds", [P, HG, 4])
        small = sb("small", [P, 160])
        WA = 15400
        arena = sb("arena", [P, WA])

        ident = cst[:, C_ID:C_ID + P]
        ones = cst[:, C_ONE:C_ONE + P]
        dist = cst[:, C_DM:C_DM + 3 * DMW].rearrange("p (g w) -> p g w", g=3)
        scan_ones = cst[:, C_SCAN:C_SCAN + TT * (P + 1)]
        iota = cst[:, C_IOTA:C_IOTA + P]
        iota16 = cst[:, C_IO16:C_IO16 + TOPK]

        bank = [ctx.enter_context(nc.psum_tensor(f"bank{b}", [P, T], F32)) for b in range(8)]
        acc = bank[0:2]

        w_loaded = [sem(f"w_loaded{s}") for s in range(4)]
        w_hi_made = sem("w_hi_made")
        w_lo_made = sem("w_lo_made")
        half_done = sem("half_done")
        acc_free = sem("acc_free")
        consts_in = sem("consts_in")
        masks_in = sem("masks_in")
        mem_in = [sem(f"mem_in{b}") for b in range(2)]
        x_in = [sem(f"x_in{b}") for b in range(2)]
        lb_dve = sem("lower_bound_dve")
        lb_act = sem("lower_bound_act")
        pads_zero = sem("pads_zero")
        gate_out = [sem(f"gate_columns_out{b}") for b in range(2)]
        mem_out = [sem(f"mem_out{b}") for b in range(2)]
        dil_out = sem("dil_out")
        hg_out = sem("hg_out")
        mix_in = [sem(f"mix_in{b}") for b in range(3)]
        mix_hi = sem("mix_hi")
        mix_lo = sem("mix_lo")
        gate_in = [sem(f"gate_columns_in{b}") for b in range(2)]
        gates_made = sem("gates_made")
        merged_hi = sem("merged_hi")
        merged_lo = sem("merged_lo")
        xres_in = [sem(f"xres_in{b}") for b in range(2)]
        out_read = sem("out_read")
        residual_out = sem("residual_out")
        sub_keys_in = sem("sub_keys_in")
        acc2_free = sem("acc2_free")
        score_done = sem("score_done")
        score_saved = sem("score_saved")
        gate_exp = sem("gate_exp")
        gate_soft = sem("gate_soft")
        sel_turned = sem("sel_turned")
        sel_saved = sem("sel_saved")
        block_cols = sem("block_cols")
        onehots = sem("onehots")
        gmat_done = sem("gmat_done")
        gmat_hi = sem("gmat_hi")
        gmat_saved = sem("gmat_saved")
        gmat_out = [sem(f"gmat_out{b}") for b in range(2)]
        gelu_out = [sem(f"gelu_out{b}") for b in range(2)]
        residual_in = sem("residual_in")
        gmat_in = [sem(f"gmat_in{b}") for b in range(2)]
        gelu_in = [sem(f"gelu_in{b}") for b in range(4)]
        hid_product = sem("hid_product")
        hid_hi = sem("hid_hi")
        hid_lo = sem("hid_lo")
        y_added = sem("y_added")
        result_out = sem("result_out")
        squared = [sem(f"squared{r}") for r in range(4)]
        summed = [sem(f"squares_summed{r}") for r in range(4)]
        column_sums = sem("column_sums")
        norm = [tuple(Steps(sem(f"norm_{e}{r}"), n) for e, n in zip(("act", "dve"), norm_names(r)))
                for r in range(4)]
        mp, md, ma = (Steps(sem(f"mem_{e}"), n) for e, n in zip(("pe", "dve", "act"), mem_names()))
        dp, dd, da = (Steps(sem(f"dil_{e}"), n, b) for e, n, b in zip(("pe", "dve", "act"), dil_names(), (0, 1, 0)))
        hp, hd, ha = (Steps(sem(f"hg_{e}"), n, b) for e, n, b in zip(("pe", "dve", "act"), hg_names(), (0, 1, 0)))
        UP = ["bg", "m1", "m2", "m3", "a1", "a2"]
        up = Steps(sem("merge_dve"), UP, 2 * len(UP))
        tk = Steps(sem("topk_dve"), topk_names(), 1)

        def carve(at, *shape):
            n = 1
            for k in shape:
                n *= k
            assert at + n <= WA, (at, shape)
            v = arena[:, at:at + n]
            names = "abcd"[:len(shape)]
            if len(shape) > 1:
                v = v.rearrange(f"p ({' '.join(names)}) -> p {' '.join(names)}",
                                **{k: s for k, s in zip(names[:-1], shape[:-1])})
            return v

        class Area:
            def __init__(self, at=0):
                self.at = at

            def __call__(self, *shape):
                v = carve(self.at, *shape)
                n = 1
                for k in shape:
                    n *= k
                self.at += n
                return v

        a = Area()
        src_x = a(KT, T)
        src_mem = a(KT, MEM)
        nsq = a(2, T)
        ntmp = a(2, T)
        nrm = a(T)
        mhi = xlo[:, :, 0:MEM]
        mlo = xlo[:, :, MEM:2 * MEM]
        a = Area()
        qm = a(MH, T)
        vm = a(MT, MH, P)
        pm = a(2, MEM)
        ptm = a(2, MT, P)
        om = a(2, T)
        m_end = a.at
        kvm = carve(KT * T, N_KV, MEM)
        a = Area()
        pd = a(2, 3, T)
        ptd = a(3, TT, P)
        od = a(3, T)
        vp = a(3, 2, TT, P)
        assert a.at <= WA - 11 * T
        gst = carve(WA - 2 * T, 2, T)
        qkv = carve(WA - 2 * T - 9 * T, 3, 3, T)
        a = Area()
        hq = a(T)
        hv = a(T)
        hf = a(2, T)
        hk = a(2, T)
        hgt = a(T)
        hsg = a(T)
        hlf = a(2, TT, P + 1)
        hb = a(2, TT, P + 1)
        hksum = a(T)
        ht = a(2, T)
        he = a(2, T)
        hkl = a(2, T)
        hql = a(2, T)
        hqs = a(2, T)
        hkn = a(2, 3, P)
        hvn = a(TT, P)
        hst = a(2, 3, P)
        hres = a(T)
        assert a.at <= WA - 2 * T
        hkst = hf
        ham = hv.rearrange("p (a b) -> p a b", a=TT)
        hosq, hr = hkl[:, 0], hkl[:, 1]
        a = Area()
        merged = a(KT, T)
        xres = a(2, T)
        a(2, T)
        gt = a(2, 3, T)
        umul = a(2, T)
        late = merged[:, HT:KT]
        a = Area()
        qpt = a(2, T)
        scores = a(TT, 2 * PH, NK)
        sw = a(TT, 2, NK)
        sw2 = a(TT, 2, NK)
        cand = a(TT, TOPK, TOPK)
        cand2 = a(TT, TOPK, TOPK)
        sel = a(3, TT, P)
        v16 = a(TT, 2, TOPK)
        eq = sw.rearrange("p a b c -> p a (b c)").rearrange("p a (b c) -> p a b c", b=TOPK)
        eq2 = sw2.rearrange("p a b c -> p a (b c)").rearrange("p a (b c) -> p a b c", b=TOPK)
        tab = cst[:, C_DM:C_DM + 3 * DMW]
        i16 = tab[:, 0:128].bitcast(U32).rearrange("p (a b c) -> p a b c", a=TT, b=2)
        i16f = tab[:, 128:256].rearrange("p (a b c) -> p a b c", a=TT, b=2)
        best = tab[:, 256:320].rearrange("p (a b) -> p a b", a=TT)
        pos = tab[:, 320:384].bitcast(U32).rearrange("p (a b) -> p a b", a=TT)
        phi = tab[:, 384:448].bitcast(U32).rearrange("p (a b) -> p a b", a=TT)
        plo = tab[:, 448:512].bitcast(U32).rearrange("p (a b) -> p a b", a=TT)
        phif = tab[:, 512:576].rearrange("p (a b) -> p a b", a=TT)
        plof = tab[:, 576:640].rearrange("p (a b) -> p a b", a=TT)
        bsum = tab[:, 768:800]
        brcp = tab[:, 800:832]
        cur = tab[:, 896:896 + 4 * TB].rearrange("p (a b) -> p a b", a=4)
        skt = tab[:, 1024:1024 + 2 * NK].rearrange("p (a b) -> p a b", a=2)
        eg = qpt
        gstage = carve(2 * T, 2, NK, TB)
        iit = carve(2 * T + 2 * NK * TB, T)
        jjt = carve(3 * T + 2 * NK * TB, T)
        gtt = carve(4 * T + 2 * NK * TB, T)
        assert 5 * T + 2 * NK * TB <= 2 * T + TT * 2 * PH * NK + 4096
        a = Area()
        y = a(KT, T)
        gsb = a(2, NTB, 4 * TB)
        agb = a(4, T)
        htmp = a(2, T)

        mxs = small[:, 0:8]
        dsl = small[:, 8:14]
        dmx, dnm, ddd, ded, dsum = ([small[:, 80 + 32 * u + 4 * k:83 + 32 * u + 4 * k] for u in range(2)]
                                    for k in range(5))
        dzs, dw = (small[:, 16 + 4 * k:19 + 4 * k] for k in range(2))
        dmm, dz, drz = (small[:, 44 + k:45 + k] for k in range(3))
        hpar = small[:, 56:60]
        hdec = small[:, 60:68].rearrange("p (d t) -> p d t", d=2)
        bgc = small[:, 68:74].rearrange("p (u b) -> p u b", u=2)
        lbs = small[:, 80:160]
        gate_cols = gate_dram.rearrange("(b j) p t -> j p b t", b=3)
        dil_tiles = mix_dram[0:HG].rearrange("(g s) p t -> s p g t", s=2)

        block = ctx.enter_context(nc.Block())

        @block.sync
        def _(sp):
            def stream(w, first):
                skip = 4 if first == 0 else 0
                for s in range(skip):
                    sp.dma_start(raw[s][:], w[s]).then_inc(w_loaded[s], 16)
                with sp.Fori(skip // 4, w.shape[0] // 4) as i:
                    for s in range(4):
                        sp.wait_ge(w_lo_made, 4 * i + (first + s - 3))
                        sp.dma_start(raw[s][:], w[4 * i + s]).then_inc(w_loaded[s], 16)

            m = 0
            for w in (w_kv, w_in, w_up, w_out, w_pq, w_u, w_v):
                stream(w, m)
                m += w.shape[0]
            assert m == HALVES

        @block.gpsimd
        def _(pool):
            with pool.Fori(0, HALVES // 4) as i:
                for s in range(4):
                    pool.wait_ge(w_hi_made, 4 * i + (s + 1))
                    nc.gpsimd.tensor_tensor(wlo[s][:], raw[s][:], whi[s][:], ALU.subtract).then_inc(w_lo_made, 1)

        @block.scalar
        def _(act):
            A = nc.scalar

            def round_half(q, s, first=False):
                act.wait_ge(w_loaded[s], 16 * q + 16)
                if not first:
                    act.wait_ge(half_done, 4 * q + (s - 3))
                A.activation(whi[s][:], raw[s][:], ACT.Copy).then_inc(w_hi_made, 1)

            def ahead(n, i, per, part):
                m = 2 * n + 4 + part
                round_half(i * (per // 2) + m // 4, m % 4)

            def chunk_ready(n, i, per):
                act.wait_ge(half_done, i * (2 * per) + (2 * n + 2))

            for b in range(2):
                act.dma_start(src_mem[:, HT * b:HT * b + HT], mem_t[:, HT * b:HT * b + HT]).then_inc(mem_in[b], 16)
            act.dma_start(cst[:, 0:C_DM], const[:, 0:C_DM]).then_inc(consts_in, 16)
            act.dma_start(prm[:], params).then_inc(consts_in, 16)
            for b in range(2):
                act.dma_start(src_x[:, HT * b:HT * b + HT], x_t[:, HT * b:HT * b + HT]).then_inc(x_in[b], 16)
            act.dma_start(cst[:, C_DM:NCONST], const[:, C_DM:NCONST]).then_inc(masks_in, 16)
            act.dma_start(lmask[:], level_mask).then_inc(masks_in, 16)
            act.sem_inc(acc_free, 2)
            act.sem_inc(acc2_free, 2)
            for s_ in (*gate_out, dil_out, hg_out, *gelu_out, *gmat_out):
                act.sem_inc(s_, 16)
            for s_ in (gates_made, gmat_saved, score_saved):
                act.sem_inc(s_, 1)
            def square_tile(r, src, k, width=T):
                if k >= 2:
                    act.wait_ge(summed[r], k - 1)
                A.activation(nsq[:, k % 2, 0:width], src[:, k], ACT.Square).then_inc(squared[r], 1)

            def norm_root(r, width):
                norm[r][1].wait(act, "ms")
                norm[r][0].done(A.activation(nrm[:, 0:width], nrm[:, 0:width], ACT.Sqrt), "sqrt")

            def norm_hi(r, src, k, out):
                norm[r][1].wait(act, f"xn{k}")
                norm[r][0].done(A.activation(out, src, ACT.Copy), f"hi{k}")

            for k in range(KT):
                if k % HT == 0:
                    round_half(0, k // HT, first=True)
                    act.wait_ge(mem_in[k // HT], 16)
                square_tile(0, src_mem, k, MEM)
            for s in range(2, 4):
                round_half(0, s, first=True)
            norm_root(0, MEM)
            for k in range(KT):
                norm_hi(0, ntmp[:, k % 2, 0:MEM], k, mhi[:, k])
            act.wait_ge(lb_dve, 6)
            A.activation(lbs[:, 24:48], lbs[:, 0:24], ACT.Exp).then_inc(lb_act, 1)

            act.wait_ge(summed[0], KT)
            norm[0][1].wait(act, f"lo{KT - 1}")
            for c in range(N_KV):
                ahead(c, 0, 2, 0)
                if c == 5:
                    norm_root(1, T)
                chunk_ready(c, 0, 2)
                A.activation(kvm[:, c], acc[c % 2][:, 0:MEM], ACT.Copy).then_inc(acc_free, 1)
                ahead(c, 0, 2, 1)
                if c < 4:
                    for k in range(4 * c, 4 * c + 4):
                        if k % HT == 0:
                            act.wait_ge(x_in[k // HT], 16)
                        square_tile(1, src_x, k)
                if c >= 5:
                    for k in range((0, 6, 11)[c - 5], (6, 11, KT)[c - 5]):
                        norm_hi(1, src_x[:, k], k, xhi[:, k])
            norm[1][1].wait(act, f"lo{KT - 1}")
            with act.Fori(0, N_MQ // 2) as i:
                for u in range(2):
                    ahead(C_MQ + u, i, 2, 0)
                    chunk_ready(C_MQ + u, i, 2)
                    A.activation(qm[:, 2 * i + u], acc[u][:], ACT.Copy).then_inc(acc_free, 1)
                    ahead(C_MQ + u, i, 2, 1)
            def gate_chunk_out(n, i, per, b, waited):
                act.wait_ge(gate_out[b], waited + 16)
                A.activation(gst[:, b], acc[n % 2][:], ACT.Copy).then_inc(acc_free, 1)

            def gate_store(n, i, per, b, tile):
                act.wait_ge(acc_free, i * per + (n + 3))
                act.dma_start(gate_dram[tile], gst[:, b]).then_inc(gate_out[b], 16)

            for h in range(MH):
                for tt in range(TT):
                    u = (h * TT + tt) % 2
                    md.wait(act, f"nm{h}{tt}")
                    ma.done(A.activation(pm[:, u], bank[2 + u][:, 0:MEM], ACT.Exp, bias=mxs[:, 2 + u:3 + u],
                                         scale=float(P) ** -0.5, accum_out=mxs[:, 4 + u:5 + u]), f"ex{h}{tt}")
                    k = h * TT + tt
                    if k % 2 == 0 and k // 2 < 2 * N_MEM_GATES:
                        x = k // 2
                        n = C_MG + x // 2
                        ahead(n, 0, 2, x % 2)
                        if x % 2:
                            g = x // 2
                            chunk_ready(n, 0, 2)
                            gate_chunk_out(n, 0, 2, g % 2, 16 * (g // 2))
                            gate_store(n, 0, 2, g % 2, g)
                if h:
                    md.wait(act, f"ov{h - 1}")
                    act.dma_start(mix_dram[HG + h - 1], om[:, (h - 1) % 2]).then_inc(mem_out[(h - 1) % 2], 16)
            md.wait(act, f"ov{MH - 1}")
            act.dma_start(mix_dram[HG + MH - 1], om[:, (MH - 1) % 2]).then_inc(mem_out[(MH - 1) % 2], 16)

            with act.Fori(0, DIL_S) as i:
                for c in range(N_DIL):
                    n = C_D + c
                    ahead(n, i, N_D, 0)
                    chunk_ready(n, i, N_D)
                    if c == 0:
                        dd.wait_iterations(act, i)
                    A.activation(qkv[:, c // 3, c % 3], acc[n % 2][:], ACT.Copy,
                                 scale=0.125 if c < 3 else 1.0).then_inc(acc_free, 1)
                    ahead(n, i, N_D, 1)
                for q in range(len(TRIPLES)):
                    dd.wait(act, f"dd{q}", i)
                    u = q % 2
                    da.done(A.activation(ded[u], ddd[u], ACT.Exp), f"ed{q}")
                    for g in range(3):
                        lo, hi = (P * v for v in key_tiles(g, TRIPLES[q][0]))
                        da.done(A.activation(pd[:, u, g, lo:hi], pd[:, u, g, lo:hi], ACT.Exp, bias=dnm[u][:, g:g + 1],
                                             accum_out=dsum[u][:, g:g + 1]), f"ex{q}{g}")
                    if q < 2 * N_DIL_GATES:
                        x = q // 2
                        n = C_D + N_DIL + x
                        ahead(n, i, N_D, q % 2)
                        if q % 2:
                            chunk_ready(n, i, N_D)
                            gate_chunk_out(n, i, N_D, x % 2, i * (16 * ((N_DIL_GATES + 1 - x % 2) // 2))
                                           + 16 * (N_MEM_GATES // 2 + x // 2))
                            gate_store(n, i, N_D, x % 2, i * N_DIL_GATES + (N_MEM_GATES + x))
                dd.wait(act, "od2", i)
                act.dma_start(dil_tiles[i], od).then_inc(dil_out, 16)

            before_hg = [N_MEM_GATES // 2 + DIL_S * ((N_DIL_GATES + 1 - b) // 2) for b in range(2)]
            act.wait_ge(dil_out, 16 * DIL_S + 16)
            act.wait_ge(mem_out[0], 32)
            act.wait_ge(mem_out[1], 32)
            act.wait_ge(pads_zero, 4)
            act.dma_start(early[:], mix_dram[0:HT].rearrange("k p t -> p k t")).then_inc(mix_in[0], 16)
            with act.Fori(0, HG) as i:
                for c in range(N_HGC):
                    n = C_H + c
                    a_ = acc[n % 2]
                    ahead(n, i, N_H, 0)
                    chunk_ready(n, i, N_H)
                    if c == 0:
                        hd.wait_iterations(act, i)
                        A.activation(hq, a_[:], ACT.Copy).then_inc(acc_free, 1)
                    elif c == 1:
                        A.activation(hv, a_[:], ACT.Copy).then_inc(acc_free, 1)
                    elif c < 4:
                        A.activation(hf[:, c - 2], a_[:], ACT.Sigmoid).then_inc(acc_free, 1)
                    else:
                        A.activation(hgt, a_[:], ACT.Copy)
                        A.activation(hsg, a_[:], ACT.Sigmoid).then_inc(acc_free, 1)
                    ahead(n, i, N_H, 1)
                for d in range(2):
                    hd.wait(act, f"f{d}", i)
                    ha.done(A.activation(hlf[:, d, :, 1:P + 1], hf[:, d].rearrange("p (a b) -> p a b", a=TT),
                                         ACT.Ln), f"ln{d}")
                for x in range(2 * N_HG_GATES):
                    n = C_H + N_HGC + x // 2
                    ahead(n, i, N_H, x % 2)
                    if x % 2:
                        g = x // 2
                        chunk_ready(n, i, N_H)
                        gate_chunk_out(n, i, N_H, g % 2, i * (16 * ((N_HG_GATES + 1 - g % 2) // 2))
                                       + (16 * (g // 2) + 16 * before_hg[g % 2]))
                    l = x - 1
                    if 0 <= l < 7:
                        blk = 2 * LEVELS[l]
                        te = ht.rearrange("p a b -> p (a b)").rearrange("p (m c) -> p m c", c=blk)
                        ee = he.rearrange("p a b -> p (a b)").rearrange("p (m c) -> p m c", c=blk)
                        hd.wait(act, f"t{l}1", i)
                        if l:
                            hd.wait(act, f"ko{l - 1}", i)
                        ha.done(A.activation(ee[:, :, 0:blk // 2], te[:, :, 0:blk // 2], ACT.Exp, scale=-1.0), f"ee{l}")
                        ha.done(A.activation(ee[:, :, blk // 2:blk], te[:, :, blk // 2:blk], ACT.Exp), f"eo{l}")
                    if x == 8:
                        hd.wait(act, "ts1", i)
                        ha.done(A.activation(hdec, hb[:, :, :, P], ACT.Exp), "dec")
                        for d in range(2):
                            if d:
                                hd.wait(act, "ks0", i)
                            ha.done(A.activation(he[:, 0].rearrange("p (a b) -> p a b", a=TT),
                                                 hb[:, d, :, 1 - d:P + 1 - d], ACT.Exp), f"x1{d}")
                            ha.done(A.activation(he[:, 1], ht[:, d], ACT.Exp, scale=-1.0), f"x2{d}")
                    if x == 12:
                        hp.wait(act, "o", i)
                        hd.wait(act, "sb0", i)
                        ha.done(A.activation(hosq, bank[2][:], ACT.Square), "sq")
                    if x % 2:
                        gate_store(n, i, N_H, g % 2, i * N_HG_GATES + (N_MEM_GATES + DIL_S * N_DIL_GATES + g))
                hd.wait(act, "ms", i)
                ha.done(A.activation(hr, hr, ACT.Sqrt), "sqrt")
                hd.wait(act, "o2", i)
                act.dma_start(mix_dram[HG + MH + i], hres).then_inc(hg_out, 16)

            hd.wait_iterations(act, HG)
            act.wait_ge(half_done, 2 * C_UP)
            for k in range(KT):
                if k == 1:
                    act.dma_start(late[:, 0:HT - 1], mix_dram[HT:KT - 1].rearrange("k p t -> p k t"))\
                        .then_inc(mix_in[1], 16)
                if k == HT - 1:
                    act.wait_ge(hg_out, 16 * HG + 16)
                    act.dma_start(late[:, HT - 1], mix_dram[KT - 1]).then_inc(mix_in[2], 16)
                if k in (0, HT, KT - 1):
                    act.wait_ge(mix_in[(0, HT, KT - 1).index(k)], 16)
                A.activation(xhi[:, k], early[:, k] if k < HT else late[:, k - HT], ACT.Copy).then_inc(mix_hi, 1)
            for b in range(2):
                act.wait_ge(gate_out[b], 16 * (before_hg[b] + HG * ((N_HG_GATES + 1 - b) // 2)) + 16)
            act.dma_start(gt[:, 0], gate_cols[0]).then_inc(gate_in[0], 16)
            act.dma_start(xres[:, 0], x_t[:, 0]).then_inc(xres_in[0], 16)
            act.dma_start(skt, sub_keys_t).then_inc(sub_keys_in, 16)

            def merge_tile(u, i, last):
                if not last:
                    up.wait_iterations(act, 2 * i + u)
                    act.dma_start(gt[:, 1 - u], gate_cols[2 * i + (u + 1)]).then_inc(gate_in[1 - u], 16)
                ahead(C_UP + u, i, 2, 0)
                act.wait_ge(gate_in[u], 16 * i + 16)
                up.wait(act, "bg", 2 * i + u)
                for b in range(3):
                    A.activation(gt[:, u, b], gt[:, u, b], ACT.Sigmoid, bias=bgc[:, u, b:b + 1]).then_inc(gates_made, 1)
                ahead(C_UP + u, i, 2, 1)

            E2 = KT // 2 - 1
            with act.Fori(0, E2) as i:
                for u in range(2):
                    merge_tile(u, i, False)
            merge_tile(0, E2, False)
            merge_tile(1, E2, True)

            act.wait_ge(mix_lo, KT)
            act.wait_ge(half_done, 2 * C_OUT)
            for k in range(KT):
                up.wait(act, "a2", KT - 2 if k < KT - 1 else KT - 1)
                A.activation(xhi[:, k], merged[:, k], ACT.Copy).then_inc(merged_hi, 1)

            def out_tile(u, i, last):
                if not last:
                    act.wait_ge(out_read, 2 * i + u + 2)
                    act.dma_start(xres[:, 1 - u], x_t[:, 2 * i + (u + 1)]).then_inc(xres_in[1 - u], 16)
                ahead(C_OUT + u, i, 2, 0)
                ahead(C_OUT + u, i, 2, 1)
                act.wait_ge(summed[2], 2 * i + u + 1)
                act.wait_ge(out_read, 2 * i + u + 3)
                act.dma_start(res_dram[2 * i + u], y[:, 2 * i + u]).then_inc(residual_out, 16)
                A.activation(nsq[:, u], y[:, 2 * i + u], ACT.Square).then_inc(squared[2], 1)

            with act.Fori(0, E2) as i:
                for u in range(2):
                    out_tile(u, i, False)
            out_tile(0, E2, False)
            out_tile(1, E2, True)

            norm_root(2, T)
            act.wait_ge(half_done, 2 * C_PQ)
            for k in range(KT):
                norm_hi(2, ntmp[:, k % 2], k, xhi[:, k])
            act.wait_ge(residual_out, 16 * KT)
            norm[2][1].wait(act, f"lo{KT - 1}")

            with act.Fori(0, PH) as i:
                for u in range(2):
                    ahead(C_PQ + u, i, 2, 0)
                    chunk_ready(C_PQ + u, i, 2)
                    A.activation(qpt[:, u], acc[u][:], ACT.Copy).then_inc(acc2_free, 1)
                    ahead(C_PQ + u, i, 2, 1)
                for u in range(2):
                    act.wait_ge(score_done, 2 * i + (u + 1))
                    A.activation(scores[:, :, 2 * i + u], bank[2 + u][:].rearrange("p (a b) -> p a b", a=TT), ACT.Copy)\
                        .then_inc(score_saved, 1)

            def expert_chunk(c, i, per, beside=None, after=None):
                n = C_U + c
                u = c % 2
                ahead(n, i, per, 0)
                if beside is not None:
                    beside()
                chunk_ready(n, i, per)
                if after is not None:
                    after()
                act.wait_ge(gelu_out[u], i * (8 * per) + 16 * (c // 2) + 16)
                A.activation(eg[:, u], acc[n % 2][:], ACT.Gelu).then_inc(acc2_free, 1)
                ahead(n, i, per, 1)
                act.wait_ge(acc2_free, i * per + (2 * PH + c + 3))
                act.dma_start(act_dram[i * per + c], eg[:, u]).then_inc(gelu_out[u], 16)

            def expert_chunks(first, count):
                with act.Fori(0, count // 2) as i:
                    for u in range(2):
                        expert_chunk(first + u, i, 2)

            expert_chunks(0, U_1)
            tk.wait_iterations(act, PH)
            A.activation(sel[:, 2], sel[:, 2], ACT.Exp).then_inc(gate_exp, 1)
            expert_chunks(U_1, U_2)
            expert_chunks(U_1 + U_2, U_3)
            act.wait_ge(sel_saved, 5)
            first = U_1 + U_2 + U_3
            with act.Fori(0, NTB // 2) as i:
                for c in range(8):
                    b = c // 4

                    def save_high(q):
                        if q % 8 == 0:
                            act.wait_ge(gmat_out[b], 16 * i + 16)
                        act.wait_ge(gmat_done, 16 * i + (q + 1) + 1)
                        for x in range(2):
                            pair = bank[2 + 2 * (q % 2) + x][:].rearrange("p (t h j) -> p t h j", t=2, h=2)
                            t0 = 4 * (q % 8) + 2 * x
                            last = A.activation(gstage[:, b, :, t0:t0 + 2].rearrange("p j t -> p t j"),
                                                pair[:, :, 0], ACT.Copy)
                        last.then_inc(gmat_hi, 1)

                    expert_chunk(first + c, i, 8, lambda: save_high(2 * c), lambda: save_high(2 * c + 1))
                    if c % 4 == 3:
                        act.wait_ge(gmat_saved, 16 * i + (2 * c + 2) + 1)
                        act.dma_start(gmat_dram[2 * i + b], gstage[:, b]).then_inc(gmat_out[b], 16)

            for b in range(2):
                act.wait_ge(gmat_out[b], 16 * (NTB // 2) + 16)

            def load_gates(s, r):
                act.dma_start(gsb[:, r], gmat_dram[:, :, bass.ds(8 * s + 4 * r, 4), :]
                              .rearrange("b p j t -> p b (j t)")).then_inc(gmat_in[r], 16)

            def load_gelu(s, k):
                act.dma_start(agb[:, k % 4], act_dram[8 * s + k]).then_inc(gelu_in[k % 4], 16)

            def hidden(s, k, half):
                act.wait_ge(hid_product, 8 * s + (k + 1))
                A.activation(xhi[:, 8 * half + k], htmp[:, k % 2], ACT.Copy).then_inc(hid_hi, 1)

            for r in range(2):
                load_gates(0, r)
            for k in range(4):
                load_gelu(0, k)
            act.dma_start(y[:, 2:KT], res_dram[2:KT].rearrange("k p t -> p k t")).then_inc(residual_in, 16)
            expert_chunks(first + U_B, U_C - 2)

            def hidden_first(k):
                hidden(0, k, 0)
                load_gelu((k + 4) // 8, (k + 4) % 8)
                if k % 4 == 3:
                    load_gates(1, k // 4)

            expert_chunk(NK - 2, 0, 2)
            expert_chunk(NK - 1, 0, 2, lambda: [hidden_first(k) for k in range(4)])
            for b in range(2):
                act.wait_ge(gelu_out[b], 16 * (NK // 2) + 16)
            act.dma_start(y[:, 0:2], res_dram[0:2].rearrange("k p t -> p k t")).then_inc(residual_in, 16)
            for k in range(4, 8):
                hidden_first(k)

            def sub_block(s, par, prepare, more):
                for x in range(KT):
                    if prepare and x in PREPARED_AT:
                        k = PREPARED_AT.index(x)
                        hidden(s + 1, k, 1 - par)
                        if k < 4:
                            load_gelu(s + 1, k + 4)
                        elif more:
                            load_gelu(s + 2, k - 4)
                        if more and k % 4 == 3:
                            load_gates(s + 2, k // 4)
                    m = 2 * C_V + KT * par + x + 4
                    if isinstance(s, int) and s == 15:
                        if x < KT - 4:
                            round_half((2 * C_V + KT * s + x + 4) // 4, (x + 4) % 4)
                        act.wait_ge(y_added, KT * s + x + 1)
                        square_tile(3, y, x)
                    elif isinstance(s, int):
                        m = 2 * C_V + KT * s + x + 4
                        round_half(m // 4, m % 4)
                    else:
                        round_half((s - par) * 4 + m // 4, m % 4)

            with act.Fori(0, 7) as i:
                for par in range(2):
                    sub_block(2 * i + par, par, True, True)
            sub_block(14, 0, True, False)
            sub_block(15, 1, False, False)

            norm_root(3, T)
            for k in range(0, KT, 2):
                norm[3][1].wait(act, f"xn{k + 1}")
                act.dma_start(out_t[k:k + 2].rearrange("k p t -> p k t"), y[:, k:k + 2]).then_inc(result_out, 16)
            act.wait_ge(result_out, 16 * (KT // 2))

        @block.vector
        def _(dve):
            V = nc.vector

            for s_ in (dd.sem, hd.sem, tk.sem, onehots):
                dve.sem_inc(s_, 1)
            dve.sem_inc(out_read, 2)

            def sum_tile(r, k, width):
                dve.wait_ge(squared[r], k + 1)
                if k == 0:
                    V.tensor_copy(nrm[:, 0:width], nsq[:, 0, 0:width]).then_inc(summed[r], 1)
                else:
                    dve.wait_ge(summed[r], k)
                    V.tensor_tensor(nrm[:, 0:width], nrm[:, 0:width], nsq[:, k % 2, 0:width], ALU.add)\
                        .then_inc(summed[r], 1)

            for k in range(KT):
                sum_tile(0, k, MEM)
            dve.wait_ge(consts_in, 32)
            lgt = prm[:, P_LBF:P_LBF + 24].rearrange("p (d l h) -> p d l h", d=2, l=2)
            sh = lbs[:, 0:24].rearrange("p (d l h) -> p d l h", d=2, l=2)
            ex = lbs[:, 24:48].rearrange("p (d l h) -> p d l h", d=2, l=2)
            mx = lbs[:, 48:60].rearrange("p (d h) -> p d h", d=2)
            sm = lbs[:, 60:72].rearrange("p (d h) -> p d h", d=2)
            count = [0]

            def pause(steps, after, name, it):
                steps.wait(dve, after, it)
                steps.done(V.memset(small[:, 76:77], 0.0), name)

            def link(ins):
                count[0] += 1
                ins.then_inc(lb_dve, 1)
                dve.wait_ge(lb_dve, count[0])

            link(V.tensor_tensor(mx[:, 0], lgt[:, 0, 0], lgt[:, 0, 1], ALU.max))
            link(V.tensor_tensor(mx[:, 1], lgt[:, 1, 0], lgt[:, 1, 1], ALU.max))
            for d in range(2):
                for l in range(2):
                    link(V.tensor_tensor(sh[:, d, l], lgt[:, d, l], mx[:, d], ALU.subtract))

            def norm_rest(r, src, width, gcol, tmp, his=None, lows=None):
                na_, nd_ = norm[r]
                b = bank[7 - r % 2]
                dve.wait_ge(column_sums, r + 1)
                nd_.done(V.tensor_scalar(nrm[:, 0:width], b[:, 0:width], 1.0 / D, EPS, ALU.mult, ALU.add), "ms")
                na_.wait(dve, "sqrt")
                nd_.done(V.reciprocal(nrm[:, 0:width], nrm[:, 0:width]), "rcp")
                nd_.wait(dve, "rcp")

                ring = tmp is not None

                def scaled(k):
                    return tmp[:, k % 2, 0:width] if ring else src[:, k]

                def lo(k):
                    na_.wait(dve, f"hi{k}")
                    nd_.done(V.tensor_tensor(lows[:, k], scaled(k), his[:, k], ALU.subtract), f"lo{k}")

                for k in range(KT):
                    if ring and k >= 2:
                        nd_.wait(dve, f"lo{k - 2}")
                    nd_.done(V.scalar_tensor_tensor(scaled(k), src[:, k], prm[:, gcol + k:gcol + k + 1],
                                                    nrm[:, 0:width], ALU.mult, ALU.mult), f"xn{k}")
                    if ring and k:
                        lo(k - 1)
                if ring:
                    lo(KT - 1)
                elif his is not None:
                    dve.wait_ge(half_done, 2 * N_KV)
                    for k in range(KT):
                        lo(k)

            dve.wait_ge(mem_in[0], 16)
            dve.wait_ge(mem_in[1], 16)
            norm_rest(0, src_mem, MEM, P_MEM, ntmp, mhi, mlo)
            dve.wait_ge(lb_act, 1)
            for d in range(2):
                link(V.tensor_tensor(sm[:, d], ex[:, d, 0], ex[:, d, 1], ALU.add))
            link(V.reciprocal(sm, sm))
            for d in range(2):
                link(V.tensor_tensor(lbt[:, :, 2 * d], ex[:, d, 0], sm[:, d], ALU.mult))
            for d in range(2):
                link(V.tensor_scalar(lbt[:, :, 2 * d + 1], lbt[:, :, 2 * d], -1.0, 1.0, ALU.mult, ALU.add))
            for k in range(KT):
                sum_tile(1, k, T)
            dve.wait_ge(x_in[0], 16)
            dve.wait_ge(x_in[1], 16)
            norm_rest(1, src_x, T, P_MIX, None, xhi, xlo)

            for h in range(MH):
                mp.wait(dve, f"vt{h}")
                md.done(V.tensor_copy(vm[:, :, h, :], bank[4 + h % 2][:, 0:MEM].rearrange("p (a b) -> p a b", a=MT)),
                        f"vm{h}")
            for h in range(MH):
                for tt in range(TT):
                    u = (h * TT + tt) % 2
                    mp.wait(dve, f"sc{h}{tt}")
                    md.done(V.reduce_max(mxs[:, u:u + 1], bank[2 + u][:, 0:MEM], AX_X), f"mx{h}{tt}")
                    md.wait(dve, f"mx{h}{tt}")
                    md.done(V.tensor_scalar(mxs[:, 2 + u:3 + u], mxs[:, u:u + 1], -float(P) ** -0.5, None, ALU.mult),
                            f"nm{h}{tt}")
                    ma.wait(dve, f"ex{h}{tt}")
                    md.done(V.reciprocal(mxs[:, 6 + u:7 + u], mxs[:, 4 + u:5 + u]), f"rc{h}{tt}")
                    md.wait(dve, f"rc{h}{tt}")
                    md.done(V.tensor_scalar(pm[:, u], pm[:, u], mxs[:, 6 + u:7 + u], None, ALU.mult), f"sp{h}{tt}")
                    mp.wait(dve, f"pt{h}{tt}")
                    md.done(V.tensor_copy(ptm[:, u], bank[4 + u][:, 0:MEM].rearrange("p (a b) -> p a b", a=MT)),
                            f"ev{h}{tt}")
                if h >= 2:
                    dve.wait_ge(mem_out[h % 2], 16)
                mp.wait(dve, f"pv{h}{TT - 1}")
                md.done(V.tensor_copy(om[:, h % 2], bank[6 + h % 2][:]), f"ov{h}")

            dve.wait_ge(masks_in, 32)
            V.memset(vp, 0.0).then_inc(pads_zero, 1)
            dve.wait_ge(pads_zero, 1)
            dve.wait_ge(mem_out[0], 32)
            dve.wait_ge(mem_out[1], 32)
            md.wait(dve, f"ov{MH - 1}")
            with dve.Fori(0, DIL_S) as i:
                dd.done(V.tensor_copy(dsl, cst[:, bass.ds(C_SL + 6 * i, 6)]), "slopes")
                for g in range(3):
                    dp.wait(dve, f"vt{g}", i)
                    for a_ in range(2):
                        vals = bank[2 + g][:].rearrange("p (s c) -> p s c", s=TT)
                        dd.done(V.tensor_copy(vp[:, g, a_, :, 64 * a_:64 * a_ + 64], vals[:, :, 64 * a_:64 * a_ + 64]),
                                f"vp{g}{a_}")
                dd.wait(dve, "slopes", i)

                def maxima(q):
                    tt, a_ = TRIPLES[q]
                    u = q % 2
                    for g in range(3):
                        lo, hi = (P * v for v in key_tiles(g, tt))
                        dp.wait(dve, f"sc{q}{g}", i)
                        dd.done(V.scalar_tensor_tensor(pd[:, u, g, lo:hi],
                                                       dist[:, g, 3 * P - P * tt + lo:3 * P - P * tt + hi],
                                                       dsl[:, 2 * g + a_:2 * g + a_ + 1], bank[2 + g][:, lo:hi],
                                                       ALU.mult, ALU.add), f"sm{q}{g}")
                        dd.wait(dve, f"sm{q}{g}", i)
                        dd.done(V.reduce_max(dmx[u][:, g:g + 1], pd[:, u, g, lo:hi], AX_X), f"mx{q}{g}")
                    dd.wait(dve, f"mx{q}2", i)
                    dd.done(V.tensor_scalar(dnm[u], dmx[u], -1.0, None, ALU.mult), f"nm{q}")
                    dd.done(V.reduce_max(dmm, dmx[u], AX_X), f"mm{q}")
                    dd.wait(dve, f"mm{q}", i)
                    dd.done(V.tensor_scalar(ddd[u], dmx[u], dmm, None, ALU.subtract), f"dd{q}")

                maxima(0)
                for q, (tt, a_) in enumerate(TRIPLES):
                    u = q % 2
                    if q + 1 < len(TRIPLES):
                        maxima(q + 1)
                    da.wait(dve, f"ex{q}2", i)
                    dd.done(V.tensor_tensor(dzs, ded[u], dsum[u], ALU.mult), f"zs{q}")
                    dd.wait(dve, f"zs{q}", i)
                    dd.done(V.reduce_sum(dz, dzs, AX_X), f"z{q}")
                    dd.wait(dve, f"z{q}", i)
                    dd.done(V.reciprocal(drz, dz), f"rz{q}")
                    dd.wait(dve, f"rz{q}", i)
                    dd.done(V.tensor_scalar(dw, ded[u], drz, None, ALU.mult), f"w{q}")
                    dd.wait(dve, f"w{q}", i)
                    for g in range(3):
                        lo, hi = (P * v for v in key_tiles(g, tt))
                        dd.done(V.tensor_scalar(pd[:, u, g, lo:hi], pd[:, u, g, lo:hi], dw[:, g:g + 1], None,
                                                ALU.mult), f"sp{q}{g}")
                    for g in range(3):
                        lo, hi = key_tiles(g, tt)
                        dp.wait(dve, f"pt{q}{g}", i)
                        dd.done(V.tensor_copy(ptd[:, g, lo:hi],
                                              bank[2 + g][:, P * lo:P * hi].rearrange("p (a b) -> p a b", b=P)),
                                f"ev{q}{g}")
                dve.wait_ge(dil_out, 16 * i + 16)
                dp.wait(dve, f"pv{len(TRIPLES) - 1}2", i)
                for g in range(3):
                    dd.done(V.tensor_copy(od[:, g], bank[5 + g][:]), f"od{g}")

            dd.wait_iterations(dve, DIL_S)
            dve.wait_ge(dil_out, 16 * DIL_S + 16)
            dp.wait(dve, f"pv{len(TRIPLES) - 1}2", DIL_S - 1)
            for d in range(2):
                V.memset(hlf[:, d, :, 0:1], 0.0).then_inc(pads_zero, 1)
            V.memset(hst, 0.0).then_inc(pads_zero, 1)
            with dve.Fori(0, HG) as i:
                hd.done(V.tensor_copy(hpar, lbt[:, i]), "par")
                for d in range(2):
                    dve.wait_ge(acc_free, i * N_H + (C_H + 2 + d + 3))
                    hd.wait(dve, "par", i)
                    hd.done(V.tensor_scalar(hf[:, d], hf[:, d], hpar[:, 2 * d + 1:2 * d + 2], hpar[:, 2 * d:2 * d + 1],
                                            ALU.mult, ALU.add), f"f{d}")
                for d in range(2):
                    hd.wait(dve, f"f{d}", i)
                    hd.done(V.tensor_scalar(hk[:, d], hf[:, d], -1.0, 1.0, ALU.mult, ALU.add), f"k{d}")
                hd.wait(dve, "k1", i)
                hd.done(V.tensor_tensor(hksum, hk[:, 0], hk[:, 1], ALU.add), "ks")
                hp.wait(dve, "vt", i)
                hd.done(V.tensor_copy(hvn, bank[2][:].rearrange("p (a b) -> p a b", a=TT)), "vn")
                for d in range(2):
                    ha.wait(dve, f"ln{d}", i)
                    hd.done(V.tensor_tensor_scan(hb[:, d].rearrange("p a b -> p (a b)"), scan_ones,
                                                 hlf[:, d].rearrange("p a b -> p (a b)"), 0.0, ALU.mult, ALU.add),
                            f"sc{d}")
                hd.wait(dve, "sc1", i)

                def level_diff(l):
                    L = LEVELS[l]
                    for d in range(2):
                        b = hb[:, d, :, 1 - d:P + 1 - d].rearrange("p a (m c) -> p a m c", c=2 * L)
                        ref = hb[:, d, :, L:P:2 * L] if 2 * L < P else hb[:, d, :, L:L + 1]
                        if l:
                            ha.wait(dve, f"eo{l - 1}", i)
                        o = ht[:, d].rearrange("p (a m c) -> p a m c", a=TT, c=2 * L)
                        hd.done(V.tensor_tensor(o, b, ref.unsqueeze(3).broadcast_to([P, TT, P // (2 * L), 2 * L]),
                                                ALU.subtract), f"t{l}{d}")

                level_diff(0)
                hp.wait(dve, "p0", i)
                hd.done(V.tensor_copy(ham, bank[3][:].rearrange("p (a b) -> p a b", a=TT)), "a0")

                def keep_level(l):
                    hp.wait(dve, f"pl{l}", i)
                    pause(hd, f"cp{l - 1}" if l else "a0", f"wait{l}", i)
                    hd.done(V.copy_predicated(ham, lmask[:, l:l + 1, :].broadcast_to([P, TT, P]),
                                              bank[4 + l % 2][:].rearrange("p (a b) -> p a b", a=TT)), f"cp{l}")

                for l in range(7):
                    L = LEVELS[l]
                    if l < 6:
                        level_diff(l + 1)
                    ha.wait(dve, f"eo{l}", i)
                    if l >= 2:
                        hp.wait(dve, f"pl{l - 2}", i)

                    def half(ap, odd):
                        return ap.rearrange("p (m c) -> p m c", c=2 * L)[:, :, L * odd:L * odd + L]

                    b = l % 2
                    hd.done(V.tensor_tensor(half(hql[:, b], 1), half(hq, 1), half(he[:, 0], 1), ALU.mult), f"qo{l}")
                    hd.done(V.tensor_tensor(half(hql[:, b], 0), half(hq, 0), half(he[:, 1], 0), ALU.mult), f"qe{l}")
                    hd.done(V.tensor_tensor(half(hkl[:, b], 0), half(hk[:, 0], 0), half(he[:, 0], 0), ALU.mult), f"ke{l}")
                    hd.done(V.tensor_tensor(half(hkl[:, b], 1), half(hk[:, 1], 1), half(he[:, 1], 1), ALU.mult), f"ko{l}")
                    if l:
                        keep_level(l - 1)
                for d in range(2):
                    ha.wait(dve, "eo6", i)
                    hd.done(V.tensor_tensor(ht[:, d].rearrange("p (a b) -> p a b", a=TT),
                                            hb[:, d, :, 1 - d:P + 1 - d],
                                            hb[:, d, :, P:P + 1].broadcast_to([P, TT, P]), ALU.subtract), f"ts{d}")
                keep_level(6)
                for d in range(2):
                    ha.wait(dve, f"x2{d}", i)
                    hd.done(V.tensor_tensor(hqs[:, d], hq, he[:, d], ALU.mult), f"qs{d}")
                    hd.done(V.tensor_tensor(hkst[:, d], hk[:, d], he[:, 1 - d], ALU.mult), f"ks{d}")
                for d in range(2):
                    hp.wait(dve, f"kt{d}", i)
                    hd.done(V.tensor_copy(hkn[:, d], bank[4 + d][:, 0:3 * P].rearrange("p (a b) -> p a b", a=3)),
                            f"et{d}")
                hp.wait(dve, "u1", i)
                uf, ub = bank[6], bank[7]
                hd.done(V.tensor_copy(hst[:, 0, 0], uf[:, 0:P]), "sf1")
                hd.done(V.tensor_copy(hst[:, 1, 2], ub[:, 2 * P:3 * P]), "sb2")
                hd.wait(dve, "sb2", i)
                hd.done(V.scalar_tensor_tensor(hst[:, 0, 1], hst[:, 0, 0], hdec[:, 0, 1:2], uf[:, P:2 * P],
                                               ALU.mult, ALU.add), "sf2")
                hd.done(V.scalar_tensor_tensor(hst[:, 1, 1], hst[:, 1, 2], hdec[:, 1, 2:3], ub[:, P:2 * P],
                                               ALU.mult, ALU.add), "sb1")
                hd.wait(dve, "sb1", i)
                hd.done(V.scalar_tensor_tensor(hst[:, 0, 2], hst[:, 0, 1], hdec[:, 0, 2:3], uf[:, 2 * P:3 * P],
                                               ALU.mult, ALU.add), "sf3")
                hd.done(V.scalar_tensor_tensor(hst[:, 1, 0], hst[:, 1, 1], hdec[:, 1, 1:2], ub[:, 0:P],
                                               ALU.mult, ALU.add), "sb0")
                hd.done(V.tensor_tensor(hsg, hsg, hgt, ALU.mult), "silu")
                hp.wait(dve, "nm", i)
                hd.done(V.tensor_scalar(hr, bank[3][:], 1.0 / P, EPS, ALU.mult, ALU.add), "ms")
                ha.wait(dve, "sqrt", i)
                hd.done(V.reciprocal(hr, hr), "rcp")
                hd.wait(dve, "rcp", i)
                dve.wait_ge(hg_out, 16 * i + 16)
                hd.done(V.scalar_tensor_tensor(hres, bank[2][:], prm[:, P_HG:P_HG + 1], hr, ALU.mult, ALU.mult), "o1")
                hd.wait(dve, "o1", i)
                hd.done(V.tensor_tensor(hres, hres, hsg, ALU.mult), "o2")

            dve.sem_inc(up.sem, 2 * len(UP))
            for k in range(KT):
                dve.wait_ge(mix_hi, k + 1)
                V.tensor_tensor(xlo[:, k], early[:, k] if k < HT else late[:, k - HT], xhi[:, k], ALU.subtract)\
                    .then_inc(mix_lo, 1)
            dve.wait_ge(mix_lo, KT)
            dve.wait_ge(hg_out, 16 * HG + 16)
            bg_v = prm[:, P_BG:P_BG + N_GATE].rearrange("p (b j) -> p b j", b=3)
            with dve.Fori(0, KT // 2) as i:
                for u in range(2):
                    j = 2 * i + u
                    dve.wait_ge(gates_made, 6 * i + 3 * u + 1)
                    up.done(V.tensor_copy(bgc[:, u], bg_v[:, :, 2 * i + u]), "bg")
                    dve.wait_ge(gates_made, 6 * i + (3 * u + 3) + 1)
                    bk = bank[3 * u:3 * u + 3]
                    dve.wait_ge(half_done, 4 * i + (2 * C_UP + 2 * u + 1))
                    up.done(V.tensor_tensor(merged[:, 2 * i + u], gt[:, u, 1], bk[1][:], ALU.mult), "m1")
                    dve.wait_ge(half_done, 4 * i + (2 * C_UP + 2 * u + 2))
                    up.done(V.tensor_tensor(umul[:, 0], gt[:, u, 0], bk[0][:], ALU.mult), "m2")
                    up.done(V.tensor_tensor(umul[:, 1], gt[:, u, 2], bk[2][:], ALU.mult), "m3")
                    up.wait(dve, "m2", j)
                    up.done(V.tensor_tensor(merged[:, 2 * i + u], merged[:, 2 * i + u], umul[:, 0], ALU.add), "a1")
                    up.wait(dve, "a1", j)
                    up.done(V.tensor_tensor(merged[:, 2 * i + u], merged[:, 2 * i + u], umul[:, 1], ALU.add), "a2")

            up.wait(dve, "a2", KT - 1)
            V.memset(nrm, 0.0).then_inc(summed[2], 1)
            for k in range(KT):
                dve.wait_ge(merged_hi, k + 1)
                V.tensor_tensor(xlo[:, k], merged[:, k], xhi[:, k], ALU.subtract).then_inc(merged_lo, 1)
            with dve.Fori(0, KT // 2) as i:
                for u in range(2):
                    dve.wait_ge(xres_in[u], 16 * i + 16)
                    dve.wait_ge(half_done, 4 * i + (2 * C_OUT + 2 * u + 2))
                    dve.wait_ge(merged_lo, KT)
                    V.tensor_tensor(y[:, 2 * i + u], xres[:, u], acc[u][:], ALU.add).then_inc(out_read, 1)
                    dve.wait_ge(squared[2], 2 * i + (u + 1))
                    dve.wait_ge(summed[2], 2 * i + (u + 1))
                    V.tensor_tensor(nrm, nrm, nsq[:, u], ALU.add).then_inc(summed[2], 1)
            dve.wait_ge(out_read, KT + 2)
            norm_rest(2, y, T, P_FFN, ntmp, xhi, xlo)

            with dve.Fori(0, PH) as i:
                dve.wait_ge(score_saved, 2 * i + 2 + 1)
                tk.wait_iterations(dve, i)
                pairs = [(x, p) for x in range(TT) for p in range(2)]
                tk.done(V.tensor_copy(sw, scores[:, :, bass.ds(2 * i, 2), :]), "cp")
                pause(tk, "cp", "wait0", i)
                for x, p in pairs:
                    tk.done(V.max(v16[:, x, p, 0:8], sw[:, x, p]), f"ma{x}{p}")
                pause(tk, "ma31", "wait1", i)
                for x, p in pairs:
                    tk.done(V.max_index(i16[:, x, p, 0:8], v16[:, x, p, 0:8], sw[:, x, p]), f"ia{x}{p}")
                for x, p in pairs:
                    tk.done(V.match_replace(sw2[:, x, p], v16[:, x, p, 0:8], sw[:, x, p], NEG), f"mr{x}{p}")
                pause(tk, "mr31", "wait2", i)
                for x, p in pairs:
                    tk.done(V.max(v16[:, x, p, 8:16], sw2[:, x, p]), f"mb{x}{p}")
                pause(tk, "mb31", "wait3", i)
                for x, p in pairs:
                    tk.done(V.max_index(i16[:, x, p, 8:16], v16[:, x, p, 8:16], sw2[:, x, p]), f"ib{x}{p}")
                tk.wait(dve, "ib31", i)
                tk.done(V.tensor_copy(i16f, i16), "if")
                tk.done(V.tensor_tensor(cand, v16[:, :, 0].unsqueeze(3).broadcast_to([P, TT, TOPK, TOPK]),
                                        v16[:, :, 1].unsqueeze(2).broadcast_to([P, TT, TOPK, TOPK]), ALU.add), "cand")
                pause(tk, "cand", "wait4", i)
                cf = cand.rearrange("p a b c -> p a (b c)")
                cf2 = cand2.rearrange("p a b c -> p a (b c)")
                for x in range(TT):
                    tk.done(V.max(best[:, x, 0:8], cf[:, x]), f"Ma{x}")
                pause(tk, "Ma3", "wait5", i)
                for x in range(TT):
                    tk.done(V.max_index(pos[:, x, 0:8], best[:, x, 0:8], cf[:, x]), f"Ia{x}")
                for x in range(TT):
                    tk.done(V.match_replace(cf2[:, x], best[:, x, 0:8], cf[:, x], NEG), f"Mr{x}")
                pause(tk, "Mr3", "wait6", i)
                for x in range(TT):
                    tk.done(V.max(best[:, x, 8:16], cf2[:, x]), f"Mb{x}")
                pause(tk, "Mb3", "wait7", i)
                for x in range(TT):
                    tk.done(V.max_index(pos[:, x, 8:16], best[:, x, 8:16], cf2[:, x]), f"Ib{x}")
                tk.done(V.tensor_tensor(sel[:, 2, :, bass.ds(TOPK * i, TOPK)], best,
                                        best[:, :, 0:1].broadcast_to([P, TT, TOPK]), ALU.subtract), "sub")
                tk.wait(dve, "Ib3", i)
                tk.done(V.tensor_scalar(phi, pos, 4, None, ALU.logical_shift_right), "hi")
                tk.done(V.tensor_scalar(plo, pos, 15, None, ALU.bitwise_and), "lo")
                tk.wait(dve, "lo", i)
                tk.done(V.tensor_copy(phif, phi), "hif")
                tk.done(V.tensor_copy(plof, plo), "lof")
                for p, f in ((0, phif), (1, plof)):
                    tk.wait(dve, "lof", i)
                    tk.done(V.tensor_tensor(
                        eq.rearrange("p a b c -> p (a b) c"), f.rearrange("p a b -> p (a b)").unsqueeze(2).broadcast_to([P, TT * TOPK, TOPK]),
                        iota16.unsqueeze(1).broadcast_to([P, TT * TOPK, TOPK]), ALU.is_equal), f"eq{p}")
                    tk.wait(dve, f"eq{p}", i)
                    tk.done(V.tensor_tensor(eq2, eq, i16f[:, :, p].unsqueeze(2).broadcast_to([P, TT, TOPK, TOPK]),
                                            ALU.mult), f"pr{p}")
                    tk.wait(dve, f"pr{p}", i)
                    tk.done(V.reduce_sum(sel[:, p, :, bass.ds(TOPK * i, TOPK)], eq2, AX_X), f"out{p}")
            dve.wait_ge(gate_exp, 1)
            e = sel[:, 2].rearrange("p a (h k) -> p (a h) k", k=TOPK)
            V.reduce_sum(bsum, e, AX_X).then_inc(gate_soft, 1)
            dve.wait_ge(gate_soft, 1)
            V.reciprocal(brcp, bsum).then_inc(gate_soft, 1)
            dve.wait_ge(gate_soft, 2)
            V.tensor_tensor(e, e, brcp.unsqueeze(2).broadcast_to([P, TT * PH, TOPK]), ALU.mult).then_inc(gate_soft, 1)
            dve.wait_ge(sel_turned, 3)
            V.tensor_copy(iit, bank[4][:]).then_inc(sel_saved, 1)
            V.tensor_copy(jjt, bank[5][:]).then_inc(sel_saved, 1)
            V.tensor_copy(gtt, bank[6][:]).then_inc(sel_saved, 1)
            dve.wait_ge(sel_saved, 3)
            V.tensor_copy(ghi, gtt).then_inc(sel_saved, 1)
            dve.wait_ge(sel_saved, 4)
            V.tensor_tensor(glo, gtt, ghi, ALU.subtract).then_inc(sel_saved, 1)
            dve.wait_ge(sel_saved, 5)

            def save_products(i, q):
                b = q // 8
                dve.wait_ge(gmat_hi, 16 * i + (q + 1))
                for x in range(2):
                    pair = bank[2 + 2 * (q % 2) + x][:].rearrange("p (t h j) -> p t h j", t=2, h=2)
                    t0 = 4 * (q % 8) + 2 * x
                    o = gstage[:, b, :, t0:t0 + 2].rearrange("p j t -> p t j")
                    last = V.tensor_tensor(o, o, pair[:, :, 1], ALU.add)
                last.then_inc(gmat_saved, 1)

            with dve.Fori(0, NTB // 2) as i:
                for b in range(2):
                    for k, s in enumerate((iit, jjt, early[:, 0], early[:, 1])):
                        dve.wait_ge(onehots, 16 * i + 8 * b + 1)
                        V.tensor_copy(cur[:, k], s[:, bass.ds((2 * TB) * i + TB * b, TB)]).then_inc(block_cols, 1)
                    dve.wait_ge(block_cols, 8 * i + (4 * b + 4))
                    for g in range(8):
                        q = 8 * b + g
                        dve.wait_ge(gmat_done, 16 * i + max(q - 1, 0) + 1)
                        for x in range(4):
                            t, slot = 4 * g + x, 4 * (q % 2) + x
                            V.tensor_scalar(oh_i[:, slot], iota, cur[:, 0, t:t + 1], None, ALU.is_equal)
                            for h in range(2):
                                last = V.tensor_scalar(oh_j[:, slot, h], iota, cur[:, 1, t:t + 1],
                                                       cur[:, 2 + h, t:t + 1], ALU.is_equal, ALU.mult)
                        last.then_inc(onehots, 1)
                        if q >= 2:
                            save_products(i, q - 2)
                save_products(i, 14)
                save_products(i, 15)

            def product(s, k):
                dve.wait_ge(gmat_in[k // 4], 16 * s + 16)
                dve.wait_ge(gelu_in[k % 4], 32 * s + 16 * (k // 4 + 1))
                if not (isinstance(s, int) and s == 0 and k < 2):
                    dve.wait_ge(hid_lo, 8 * s + (k - 1))
                g4 = gsb[:, k // 4].rearrange("p b (j t) -> p b j t", j=4)
                V.tensor_tensor(htmp[:, k % 2].rearrange("p (b t) -> p b t", b=NTB),
                                agb[:, k % 4].rearrange("p (b t) -> p b t", b=NTB), g4[:, :, k % 4], ALU.mult)\
                    .then_inc(hid_product, 1)

            def low_part(s, k, half):
                dve.wait_ge(hid_hi, 8 * s + (k + 1))
                V.tensor_tensor(xlo[:, 8 * half + k], htmp[:, k % 2], xhi[:, 8 * half + k], ALU.subtract)\
                    .then_inc(hid_lo, 1)

            dve.wait_ge(half_done, 2 * C_V - 1)
            product(0, 0)
            for k in range(8):
                if k < 7:
                    product(0, k + 1)
                low_part(0, k, 0)
            dve.wait_ge(residual_in, 32)

            def sub_block_add(s, par, prepare):
                last = isinstance(s, int) and s == 15
                for x in range(KT):
                    if prepare and x in PREPARED_AT:
                        product(s + 1, PREPARED_AT.index(x))
                    dve.wait_ge(half_done, KT * s + (2 * C_V + x + 1))
                    if not (isinstance(s, int) and s == 0):
                        dve.wait_ge(y_added, KT * s + (x + 1 - KT))
                    V.tensor_tensor(y[:, x], y[:, x], acc[x % 2][:], ALU.add).then_inc(y_added, 1)
                    if prepare and x - 1 in PREPARED_AT:
                        low_part(s + 1, PREPARED_AT.index(x - 1), 1 - par)
                    if last:
                        sum_tile(3, x, T)

            sub_block_add(0, 0, True)
            sub_block_add(1, 1, True)
            with dve.Fori(1, 7) as i:
                for par in range(2):
                    sub_block_add(2 * i + par, par, True)
            sub_block_add(14, 0, True)
            sub_block_add(15, 1, False)
            norm_rest(3, y, T, P_FIN, None)

        @block.tensor
        def _(pe):
            M = nc.tensor

            def half(m, s, out, tiles, k0, first, last, his=xhi, los=xlo, ready=None):
                pe.wait_ge(w_lo_made, m + 1)
                for k in tiles:
                    if ready is not None:
                        ready(k0 + k)
                    h, l = his[:, k0 + k], los[:, k0 + k]
                    f, e = first and k == tiles[0], last and k == tiles[-1]
                    M.matmul(out, whi[s][:, k], h, start=f, stop=False)
                    M.matmul(out, whi[s][:, k], l, start=False, stop=False)
                    ins = M.matmul(out, wlo[s][:, k], h, start=False, stop=e)
                return ins

            def chunk_half(n, i, per, x, width=T, **operands):
                s = (2 * n + x) % 4
                half(i * (2 * per) + (2 * n + x), s, acc[n % 2][:, 0:width], list(range(8)), 8 * x, x == 0, x == 1,
                     **operands).then_inc(half_done, 1)

            def take_acc(n, i, per):
                pe.wait_ge(acc_free, i * per + (n + 1))

            def take_acc2(n, i, per):
                pe.wait_ge(acc2_free, i * per + (n - C_PQ + 1))

            def column_sum(r, width, steps):
                pe.wait_ge(summed[r], steps)
                M.matmul(bank[7 - r % 2][:, 0:width], ones, nrm[:, 0:width], start=True, stop=True)\
                    .then_inc(column_sums, 1)

            def chunk(n, i, per, ready=None):
                for x in range(2):
                    chunk_half(n, i, per, x, ready=ready)

            def tiles_split(r):
                return lambda k: norm[r][1].wait(pe, f"lo{k}")

            pe.sem_inc(gmat_done, 1)
            pe.wait_ge(consts_in, 32)
            column_sum(0, MEM, KT)
            for c in range(N_KV):
                take_acc(c, 0, 2)
                for x in range(2):
                    chunk_half(c, 0, 2, x, MEM, his=mhi, los=mlo, ready=tiles_split(0) if c == 0 else None)
                if c == 4:
                    column_sum(1, T, KT)
            for c in range(N_MQ):
                take_acc(C_MQ + c, 0, 2)
                chunk(C_MQ + c, 0, 2, tiles_split(1) if c == 0 else None)

            pe.wait_ge(acc_free, C_MG + 2)
            for h in range(MH):
                if h >= 2:
                    md.wait(pe, f"vm{h - 2}")
                for m in range(MT):
                    ins = M.transpose(bank[4 + h % 2][:, P * m:P * m + P], kvm[:, MH + h, P * m:P * m + P], ident)
                mp.done(ins, f"vt{h}")

            units = [(h, tt) for h in range(MH) for tt in range(TT)]

            def mem_scores(k):
                h, tt = units[k]
                if k >= 2:
                    ma.wait(pe, f"ex{units[k - 2][0]}{units[k - 2][1]}")
                mp.done(M.matmul(bank[2 + k % 2][:, 0:MEM], qm[:, h, P * tt:P * tt + P], kvm[:, h],
                                 start=True, stop=True), f"sc{h}{tt}")

            mem_scores(0)
            mem_scores(1)
            for k, (h, tt) in enumerate(units):
                u = k % 2
                if k % 2 == 0 and k // 2 < 2 * N_MEM_GATES:
                    n, x = C_MG + k // 4, (k // 2) % 2
                    if x == 0:
                        take_acc(n, 0, 2)
                    chunk_half(n, 0, 2, x)
                md.wait(pe, f"sp{h}{tt}")
                if k < 2:
                    md.wait(pe, f"vm{MH - 1}")
                for m in range(MT):
                    ins = M.transpose(bank[4 + u][:, P * m:P * m + P], pm[:, u, P * m:P * m + P], ident)
                mp.done(ins, f"pt{h}{tt}")
                md.wait(pe, f"ev{h}{tt}")
                if tt == 0 and h >= 2:
                    md.wait(pe, f"ov{h - 2}")
                for m in range(MT):
                    ins = M.matmul(bank[6 + h % 2][:, P * tt:P * tt + P], vm[:, m, h], ptm[:, u, m],
                                   start=(m == 0), stop=(m == MT - 1))
                mp.done(ins, f"pv{h}{tt}")
                if k + 2 < len(units):
                    mem_scores(k + 2)

            md.wait(pe, f"ov{MH - 1}")
            pe.wait_ge(pads_zero, 1)
            with pe.Fori(0, DIL_S) as i:
                for c in range(N_DIL):
                    take_acc(C_D + c, i, N_D)
                    for x in range(2):
                        chunk_half(C_D + c, i, N_D, x)
                pe.wait_ge(acc_free, i * N_D + (C_D + N_DIL + 2))
                dd.wait_iterations(pe, i)
                for g in range(3):
                    for st in range(TT):
                        ins = M.transpose(bank[2 + g][:, P * st:P * st + P], qkv[:, 2, g, P * st:P * st + P], ident)
                    dp.done(ins, f"vt{g}")

                def scores_of(q, after):
                    tt, a_ = TRIPLES[q]
                    r = slice(64 * a_, 64 * a_ + 64)
                    for g in range(3):
                        lo, hi = (P * v for v in key_tiles(g, tt))
                        dd.wait(pe, after.format(g=g), i)
                        dp.done(M.matmul(bank[2 + g][:, lo:hi], qkv[r, 0, g, P * tt:P * tt + P], qkv[r, 1, g, lo:hi],
                                         start=True, stop=True), f"sc{q}{g}")

                scores_of(0, "vp{g}1")
                scores_of(1, "sm0{g}")
                for q, (tt, a_) in enumerate(TRIPLES):
                    if q < 2 * N_DIL_GATES:
                        n = C_D + N_DIL + q // 2
                        if q % 2 == 0:
                            take_acc(n, i, N_D)
                        chunk_half(n, i, N_D, q % 2)
                    for g in range(3):
                        if q + 1 < len(TRIPLES):
                            dd.wait(pe, f"sm{q + 1}{g}", i)
                        dd.wait(pe, f"sp{q}{g}", i)
                        for st in range(*key_tiles(g, tt)):
                            ins = M.transpose(bank[2 + g][:, P * st:P * st + P], pd[:, q % 2, g, P * st:P * st + P],
                                              ident)
                        dp.done(ins, f"pt{q}{g}")
                    if q + 2 < len(TRIPLES):
                        scores_of(q + 2, f"ev{q}" + "{g}")
                    for g in range(3):
                        lo, hi = key_tiles(g, tt)
                        dd.wait(pe, f"ev{q}{g}", i)
                        for st in range(lo, hi):
                            ins = M.matmul(bank[5 + g][:, P * tt:P * tt + P], vp[:, g, a_, st], ptd[:, g, st],
                                           start=(a_ == 0 and st == lo), stop=(a_ == 1 and st == hi - 1))
                        dp.done(ins, f"pv{q}{g}")

            dd.wait_iterations(pe, DIL_S)
            with pe.Fori(0, HG) as i:
                for c in range(N_HGC):
                    take_acc(C_H + c, i, N_H)
                    for x in range(2):
                        chunk_half(C_H + c, i, N_H, x)

                def per_tile(out, lhs, rhs, name):
                    for tt in range(TT):
                        ins = M.matmul(out[:, P * tt:P * tt + P], lhs[:, P * tt:P * tt + P],
                                       rhs[:, P * tt:P * tt + P], start=True, stop=True)
                    hp.done(ins, name)

                for x in range(2 * N_HG_GATES):
                    n = C_H + N_HGC + x // 2
                    if x % 2 == 0:
                        take_acc(n, i, N_H)
                    chunk_half(n, i, N_H, x % 2)
                    if x == 0:
                        hd.wait_iterations(pe, i)
                        for tt in range(TT):
                            ins = M.transpose(bank[2][:, P * tt:P * tt + P], hv[:, P * tt:P * tt + P], ident)
                        hp.done(ins, "vt")
                    if x == 1:
                        hd.wait(pe, "ks", i)
                        per_tile(bank[3], hksum, hq, "p0")
                    l = x - 3
                    if 0 <= l < 7:
                        hd.wait(pe, f"ko{l}", i)
                        if l >= 2:
                            hd.wait(pe, f"cp{l - 2}", i)
                        per_tile(bank[4 + l % 2], hkl[:, l % 2], hql[:, l % 2], f"pl{l}")
                    if x == 10:
                        for d in range(2):
                            hd.wait(pe, f"ks{d}", i)
                            for k in range(3):
                                t0 = P * (k + d)
                                ins = M.transpose(bank[4 + d][:, P * k:P * k + P], hkst[:, d, t0:t0 + P], ident)
                            hp.done(ins, f"kt{d}")
                    if x == 11:
                        for d in range(2):
                            hd.wait(pe, f"et{d}", i)
                            for k in range(3):
                                ins = M.matmul(bank[6 + d][:, P * k:P * k + P], hkn[:, d, k], hvn[:, k + d],
                                               start=True, stop=True)
                            hp.done(ins, f"u{d}")
                    if x == 12:
                        hd.wait(pe, "sb0", i)
                        for tt in range(TT):
                            o = bank[2][:, P * tt:P * tt + P]
                            cols = slice(P * tt, P * tt + P)
                            if tt:
                                M.matmul(o, hst[:, 0, tt - 1], hqs[:, 0, cols], start=True, stop=False)
                            if tt < TT - 1:
                                M.matmul(o, hst[:, 1, tt], hqs[:, 1, cols], start=(tt == 0), stop=False)
                            ins = M.matmul(o, hvn[:, tt], ham[:, tt], start=False, stop=True)
                        hp.done(ins, "o")
                    if x == 13:
                        ha.wait(pe, "sq", i)
                        hp.done(M.matmul(bank[3][:], ones, hosq, start=True, stop=True), "nm")

            pe.wait_ge(acc_free, C_UP + 2)
            hd.wait_iterations(pe, HG)
            def merge_products(u, i, first=False):
                up.wait(pe, "m3", 2 * i + (u - 2))
                bk = [b[:] for b in bank[3 * u:3 * u + 3]]
                m = 4 * i + (2 * C_UP + 2 * u)
                ready = (lambda k: pe.wait_ge(mix_lo, k + 1)) if first else None
                half(m, 2 * u, bk[1], range(HG), 0, True, True, ready=ready)
                half(m, 2 * u, bk[2], range(HG, HT), 0, True, False, ready=ready).then_inc(half_done, 1)
                half(m + 1, 2 * u + 1, bk[2], range(2), HT, False, True, ready=ready)
                half(m + 1, 2 * u + 1, bk[0], range(2, HT), HT, True, True, ready=ready).then_inc(half_done, 1)

            merge_products(0, 0, True)
            merge_products(1, 0)
            with pe.Fori(1, KT // 2) as i:
                for u in range(2):
                    merge_products(u, i)

            up.wait(pe, "m3", KT - 2)
            def out_chunk(u, i, first=False):
                if first:
                    ready = lambda k: pe.wait_ge(merged_lo, k + 1)
                else:
                    ready = None
                    pe.wait_ge(out_read, 2 * i + (u + 1))
                chunk(C_OUT + u, i, 2, ready)

            out_chunk(0, 0, True)
            out_chunk(1, 0)
            with pe.Fori(1, KT // 2) as i:
                for u in range(2):
                    out_chunk(u, i)
            column_sum(2, T, KT + 1)

            pe.wait_ge(sub_keys_in, 16)
            def query_pair(i, first):
                def scores_of(u):
                    pe.wait_ge(acc2_free, 2 * i + (u + 3))
                    pe.wait_ge(score_saved, 2 * i + 1)
                    for tt in range(TT):
                        ins = M.matmul(bank[2 + u][:, P * tt:P * tt + P], qpt[:, u, P * tt:P * tt + P], skt[:, u],
                                       start=True, stop=True)
                    ins.then_inc(score_done, 1)

                for u in range(2):
                    take_acc2(C_PQ + u, i, 2)
                    for x in range(2):
                        chunk_half(C_PQ + u, i, 2, x, ready=tiles_split(2) if first and u == 0 else None)
                        if u == 1 and x == 0:
                            scores_of(0)
                scores_of(1)

            query_pair(0, True)
            with pe.Fori(1, PH) as i:
                query_pair(i, False)

            def expert_chunks(first, count):
                with pe.Fori(0, count // 2) as i:
                    for u in range(2):
                        n = C_U + first + u
                        take_acc2(n, i, 2)
                        for x in range(2):
                            chunk_half(n, i, 2, x)

            expert_chunks(0, U_1)
            expert_chunks(U_1, U_2)
            pe.wait_ge(gate_soft, 3)
            for k in range(3):
                for tt in range(TT):
                    ins = M.transpose(bank[4 + k][:, P * tt:P * tt + P], sel[:, k, tt], ident)
                ins.then_inc(sel_turned, 1)
            expert_chunks(U_1 + U_2, U_3)
            first = U_1 + U_2 + U_3
            with pe.Fori(0, NTB // 2) as i:
                for c in range(8):
                    n = C_U + first + c
                    take_acc2(n, i, 8)
                    for x in range(2):
                        chunk_half(n, i, 8, x)
                        q = 2 * c + x
                        pe.wait_ge(onehots, 16 * i + (q + 1) + 1)
                        pe.wait_ge(gmat_saved, 16 * i + max(q, 1))
                        for k in range(4):
                            o = bank[2 + 2 * (q % 2) + k // 2][:, 2 * P * (k % 2):2 * P * (k % 2) + 2 * P]
                            slot = 4 * (q % 2) + k
                            ins = M.matmul(o, oh_i[:, slot], oh_j[:, slot].rearrange("p h j -> p (h j)"),
                                           start=True, stop=True)
                        ins.then_inc(gmat_done, 1)
            expert_chunks(first + U_B, U_C)

            pe.wait_ge(acc2_free, 2 * PH + NK + 2)

            def sub_block_products(s, par):
                first = isinstance(s, int) and s == 0
                for x in range(KT):
                    if not (first and x < 2):
                        pe.wait_ge(y_added, KT * s + (x - 1))
                    if not first:
                        pe.wait_ge(hid_lo, 8 * s + 8)
                    m = KT * s + (2 * C_V + x)
                    half(m, (2 * C_V + x) % 4, acc[x % 2][:], list(range(8)), 8 * par, True, True,
                         ready=(lambda k: pe.wait_ge(hid_lo, k + 1)) if first and x == 0 else None)\
                        .then_inc(half_done, 1)

            sub_block_products(0, 0)
            sub_block_products(1, 1)
            with pe.Fori(1, 8) as i:
                for par in range(2):
                    sub_block_products(2 * i + par, par)
            column_sum(3, T, KT)


def _constants():
    import numpy as np

    c = np.zeros((P, NCONST), np.float32)
    c[:, C_ID:C_ID + P] = np.eye(P)
    c[:, C_ONE:C_ONE + P] = 1
    gap = np.arange(DMW)[None, :] - 3 * P - np.arange(P)[:, None]
    for g, dil in enumerate(DILATIONS):
        ok = (gap % dil == 0) & (np.abs(gap) <= REACH * dil)
        c[:, C_DM + g * DMW:C_DM + (g + 1) * DMW] = np.where(ok, np.abs(gap), 1e32)
    s = np.ones((TT, P + 1))
    s[:, 0] = 0
    c[:, C_SCAN:C_SCAN + TT * (P + 1)] = s.reshape(-1)
    c[:, C_IOTA:C_IOTA + P] = np.arange(P)
    c[:, C_IO16:C_IO16 + TOPK] = np.arange(TOPK)
    heads = np.arange(12).reshape(3, 2, 2).transpose(1, 0, 2).reshape(-1)
    c[:, C_SL:C_SL + 12] = -np.exp2(-8.0 * (heads + 1) / 12)
    k = np.arange(P)
    m = np.zeros((P, 7, P), np.int32)
    for l, L in enumerate(LEVELS):
        blk, odd = k // (2 * L), (k // L) % 2
        m[:, l] = (blk[:, None] == blk[None, :]) & (odd[:, None] != odd[None, :])
    return c, m


def kernel(**inputs):
    import numpy as np
    import concourse.bacc as bacc
    from concourse import mybir as _mybir
    from concourse.bass_utils import run_bass_kernel_spmd

    a = {k: np.asarray(v) for k, v in inputs.items()}

    def cols(v):
        return v.reshape(-1, P).T

    def rows(v):
        return np.ascontiguousarray(v.T.reshape(KT, P, -1).transpose(1, 0, 2))

    def halves(w):
        n = w.shape[1] // P
        return np.ascontiguousarray(w.reshape(2, HT, P, n, P).transpose(3, 0, 2, 1, 4)).reshape(2 * n, P, HT, P)

    w_in = a["w_in"][0]
    hg = w_in[:, :5 * HG * P].reshape(D, 5, HG, P)
    dil = w_in[:, 5 * HG * P:5 * HG * P + 18 * P].reshape(D, 3, 3, 2, P)
    mq = w_in[:, 5 * HG * P + 18 * P:5 * HG * P + 18 * P + MH * P]
    gates = w_in[:, 5 * HG * P + 18 * P + MH * P:].reshape(D, N_GATE, P)
    g = N_MEM_GATES
    order = [mq, gates[:, :g].reshape(D, -1)]
    for s in range(DIL_S):
        order += [dil[:, :, :, s].reshape(D, -1), gates[:, g:g + N_DIL_GATES].reshape(D, -1)]
        g += N_DIL_GATES
    for h in range(HG):
        order += [hg[:, :, h].reshape(D, -1), gates[:, g:g + N_HG_GATES].reshape(D, -1)]
        g += N_HG_GATES
    w_in = halves(np.concatenate(order, 1))

    u = a["peer_u"][0].reshape(P, NK, 2, HT, P).transpose(1, 2, 4, 3, 0)
    v = a["peer_v"][0].reshape(P, NK // 8, 8, KT, P).transpose(1, 3, 0, 2, 4)
    const, mask = _constants()
    prm = np.concatenate([cols(a["g_mix"][0]), cols(a["g_mem"][0]), cols(a["g_ffn"][0]), cols(a["g_final"]),
                          cols(a["b_gate"][0])]
                         + [cols(a[n][l]) for n in ("lb_fwd_logits", "lb_bwd_logits") for l in range(2)]
                         + [cols(a["g_hgrn"][0])], 1)
    arrays = {
        "x_t": rows(a["x"][0]), "mem_t": rows(a["mem"][0]), "const": const, "level_mask": mask,
        "params": np.ascontiguousarray(prm),
        "sub_keys_t": np.ascontiguousarray(a["peer_sub_keys"][0].transpose(2, 0, 1)),
        "w_kv": halves(a["w_mem_kv"][0]), "w_in": w_in, "w_up": halves(np.roll(a["w_up"][0], -HG * P, axis=0)),
        "w_out": halves(a["w_out"][0]), "w_pq": halves(a["w_peer_q"][0]),
        "w_u": np.ascontiguousarray(u).reshape(2 * NK, P, HT, P),
        "w_v": np.ascontiguousarray(v).reshape(2 * NK, P, HT, P),
    }
    nc = bacc.Bacc("TRN2", target_bir_lowering=False, num_devices=1)
    args = [nc.dram_tensor(n, x.shape, _mybir.dt.from_np(x.dtype), kind="ExternalInput").ap()
            for n, x in arrays.items()]
    out = nc.dram_tensor("out_t", [KT, P, T], _mybir.dt.float32, kind="ExternalOutput").ap()
    encoder_block_kernel(nc, *args, out)
    r = run_bass_kernel_spmd(nc, [arrays], core_ids=[0])
    got = np.asarray(r.results[0]["out_t"]).reshape(D, T)
    return np.ascontiguousarray(got.T).reshape(1, T, D)
```

```python
from contextlib import ExitStack

import concourse.bass as bass
from concourse import mybir

ALU = mybir.AluOpType
ACT = mybir.ActivationFunctionType
F32 = mybir.dt.float32
F32R = mybir.dt.float32r
U32 = mybir.dt.uint32
I32 = mybir.dt.int32
AX_X = mybir.AxisListType.X

P = 128
D = 2048
KT = D // P
T = 512
TT = T // P
MEM = 256
MT = MEM // P
EPS = 1e-6
HG = 6
DIL_G = 3
DIL_S = 2
MH = 4
PH = 8
TOPK = 16
NK = 128
LEVELS = [64, 32, 16, 8, 4, 2, 1]
HT = 8
HW = HT * P
DMW = T + 3 * P
NEG = -3.0e38

N_KV = 2 * MH
N_MQ = MH
N_DIL = 3 * DIL_G
N_MEM_GATES = 4
N_DIL_GATES = 1
N_D = N_DIL + N_DIL_GATES
N_HGC = 5
N_HG_GATES = 7
N_H = N_HGC + N_HG_GATES
N_GATE = 3 * KT
C_MQ = N_KV
C_MG = C_MQ + N_MQ
C_D = C_MG + N_MEM_GATES
C_H = C_D + DIL_S * N_D
C_UP = C_H + HG * N_H
C_OUT = C_UP + KT
C_PQ = C_OUT + KT
C_U = C_PQ + 2 * PH
C_V = C_U + NK
HALVES = 2 * (C_V + NK)
U_1, U_2, U_3, U_B, U_C = 24, 8, 8, 64, 24
TB = 32
NTB = T // TB
assert N_MEM_GATES + DIL_S * N_DIL_GATES + HG * N_HG_GATES == N_GATE
DILATIONS = (1, 4, 16)
REACH = 64

C_ID, C_ONE, C_DM = 0, P, 2 * P
C_SCAN = C_DM + 3 * DMW
C_IOTA = C_SCAN + TT * (P + 1)
C_IO16 = C_IOTA + P
C_SL = C_IO16 + TOPK
NCONST = C_SL + 12
P_MIX, P_MEM, P_FFN, P_FIN = 0, KT, 2 * KT, 3 * KT
P_BG = 4 * KT
P_LBF = P_BG + N_GATE
P_LBB = P_LBF + 2 * HG
P_HG = P_LBB + 2 * HG
NPRM = P_HG + 1


class Steps:

    def __init__(self, sem, names, base=0):
        self.sem, self.names, self.n = sem, list(names), len(names)
        self.where = {s: k + 1 for k, s in enumerate(self.names)}
        self.base, self.next = base, 0
        assert len(self.where) == self.n

    def done(self, instruction, name):
        assert self.names[self.next % self.n] == name, (self.names[self.next % self.n], name)
        self.next += 1
        instruction.then_inc(self.sem, 1)

    def at(self, name, it=0):
        return it * self.n + (self.base + self.where[name])

    def wait(self, eng, name, it=0):
        eng.wait_ge(self.sem, self.at(name, it))

    def wait_iterations(self, eng, it):
        eng.wait_ge(self.sem, it * self.n + self.base)


def norm_names(r):
    act = ["sqrt"] + [f"hi{k}" for k in range(KT)]
    xn, lo = [f"xn{k}" for k in range(KT)], [f"lo{k}" for k in range(KT)]
    dve = ["ms", "rcp", "diag"]
    if r in (0, 2):
        for k in range(0, KT, 2):
            dve += [xn[k], xn[k + 1], lo[k]]
        return act, dve
    return act, dve + xn + (lo if r == 1 else [])


def mem_names():
    u = [(h, tt) for h in range(MH) for tt in range(TT)]
    pe = [f"vt{h}" for h in range(MH)] + [f"sc{h}{tt}" for h, tt in u[:2]]
    for k, (h, tt) in enumerate(u):
        pe += [f"pt{h}{tt}"] + ([f"pv{u[k - 1][0]}{u[k - 1][1]}"] if k else [])
        pe += [f"sc{u[k + 2][0]}{u[k + 2][1]}"] if k + 2 < len(u) else []
    pe += [f"pv{MH - 1}{TT - 1}"]
    dve = [f"vm{h}" for h in range(MH)]

    def steps(names, k):
        return [f"{s}{u[k][0]}{u[k][1]}" for s in names] if k < len(u) else []

    dve += steps(("mx", "nm"), 0) + steps(("mx", "nm"), 1) + steps(("rc", "sp"), 0)
    for k, (h, tt) in enumerate(u):
        dve += steps(("rc", "sp"), k + 1) + [f"ev{h}{tt}"] + ([f"ov{h - 1}"] if h and tt == 0 else [])
        dve += steps(("mx", "nm"), k + 2)
    return pe, dve + [f"ov{MH - 1}"], [f"ex{h}{tt}" for h, tt in u]


PREPARED_AT = [0, 2, 4, 6, 8, 10, 12, 13]


def key_tiles(g, tt):
    r = -(-REACH * DILATIONS[g] // P)
    return max(0, tt - r), min(TT, tt + r + 1)


TRIPLES = [(tt, a) for tt in range(TT) for a in range(2)]


def dil_names():
    pe = [f"vt{g}" for g in range(3)]
    dve = ["slopes"] + [f"vp{g}{a}" for g in range(3) for a in range(2)]
    act = []
    n = len(TRIPLES)
    pe += [f"sc{q}{g}" for q in range(2) for g in range(3)]

    def maxima(q):
        return [f"{s}{q}{g}" for g in range(3) for s in ("sm", "mx")] + [f"{s}{q}" for s in ("nm", "mm", "dd")]

    def weights(q):
        return [f"{s}{q}" for s in ("zs", "z", "rz", "w")]

    def exps(q):
        return [f"ed{q}"] + [f"ex{q}{g}" for g in range(3)]

    dve += maxima(0) + maxima(1) + weights(0)
    act += exps(0) + exps(1)
    for q in range(n):
        pe += [f"{s}{r}{g}" for s, r in (("pt", q), ("sc", q + 2), ("pv", q)) if r < n for g in range(3)]
        dve += [f"sp{q}{g}" for g in range(3)] + [f"ev{q}0"]
        if q + 1 < n:
            dve += weights(q + 1)
        if q + 2 < n:
            dve += maxima(q + 2)
        act += [f"ev{q}1", f"ev{q}2"] + (exps(q + 2) if q + 2 < n else [])
    return pe, dve + [f"od{g}" for g in range(3)], act


def hg_names():
    dve = ["par", "f0", "f1", "k0", "k1", "ks", "vn", "sc0", "sc1", "t00", "t01", "a0"]
    act = ["ln0", "ln1"]
    for l in range(7):
        if l < 6:
            dve += [f"t{l + 1}0", f"t{l + 1}1"]
        dve += [f"qo{l}", f"qe{l}", f"ke{l}", f"ko{l}"]
        if l:
            dve += [f"wait{l - 1}", f"cp{l - 1}"]
        act += [f"ee{l}", f"eo{l}"]
    dve += ["ts0", "ts1", "wait6", "cp6", "qs0", "ks0", "qs1", "ks1", "et0", "et1",
            "sf1", "sb2", "sf2", "sb1", "sf3", "sb0", "silu", "ms", "rcp", "o1", "o2"]
    act += ["dec", "x10", "x20", "x11", "x21", "sq", "sqrt"]
    pe = ["vt", "p0"] + [f"pl{l}" for l in range(7)] + ["kt0", "kt1", "u0", "u1", "o", "nm"]
    return pe, dve, act


def topk_names():
    dve = ["cp"]
    for w, s in ((0, "ma"), (1, "ia"), (None, "mr"), (2, "mb"), (3, "ib")):
        dve += [f"wait{w}"] * (w is not None) + [f"{s}{x}{p}" for x in range(TT) for p in range(2)]
    dve += ["if", "cand"]
    for w, s in ((4, "Ma"), (5, "Ia"), (None, "Mr"), (6, "Mb"), (7, "Ib")):
        dve += [f"wait{w}"] * (w is not None) + [f"{s}{x}" for x in range(TT)]
    return dve + ["sub", "hi", "lo", "hif", "lof", "eq0", "pr0", "out0", "eq1", "pr1", "out1"]


def encoder_block_kernel(nc, x_t, mem_t, const, level_mask, params, sub_keys_t,
                         w_kv, w_in, w_up, w_out, w_pq, w_u, w_v, out_t):
    ctx = ExitStack()
    with ctx:
        def sb(name, shape, dt=F32):
            return ctx.enter_context(nc.sbuf_tensor(name, shape, dt))

        def sem(name):
            return ctx.enter_context(nc.semaphore(name))

        def dram(name, shape):
            return nc.dram_tensor(name, shape, F32, kind="Internal").ap()

        gate_dram = dram("gate_scratch", [N_GATE, P, T])
        mix_dram = dram("mix_scratch", [KT, P, T])
        res_dram = dram("residual_scratch", [KT, P, T])
        act_dram = dram("gelu_scratch", [NK, P, T])
        gmat_dram = dram("gate_matrix_scratch", [NTB, P, NK, TB])

        raw = [sb(f"w_raw{s}", [P, HT, P]) for s in range(4)]
        whi = [sb(f"w_hi{s}", [P, HT, P], F32R) for s in range(4)]
        wlo = [sb(f"w_lo{s}", [P, HT, P], F32R) for s in range(4)]
        xhi = sb("x_hi", [P, KT, T], F32R)
        xlo = sb("x_lo", [P, KT, T], F32R)
        early_a = sb("early_mix_or_gates", [P, 2, T])
        early_b = sb("early_mix_or_one_hots", [P, 6, T])
        ghi, glo = early_a[:, 0].bitcast(F32R), early_a[:, 1].bitcast(F32R)
        oh_i = early_b[:, 0:2].rearrange("p a b -> p (a b)").rearrange("p (a b) -> p a b", b=P).bitcast(F32R)
        oh_j = early_b[:, 2:6].rearrange("p a b -> p (a b)").rearrange("p (a h b) -> p a h b", h=2, b=P).bitcast(F32R)

        def early(k):
            return early_a[:, k] if k < 2 else early_b[:, k - 2]

        cst = sb("constants", [P, NCONST])
        lmask = sb("level_masks", [P, 7, P], I32)
        prm = sb("parameters", [P, NPRM])
        lbt = sb("lower_bounds", [P, HG, 4])
        small = sb("small", [P, 160])
        WA = 15400
        arena = sb("arena", [P, WA])

        ident = cst[:, C_ID:C_ID + P]
        ones = cst[:, C_ONE:C_ONE + P]
        dist = cst[:, C_DM:C_DM + 3 * DMW].rearrange("p (g w) -> p g w", g=3)
        scan_ones = cst[:, C_SCAN:C_SCAN + TT * (P + 1)]
        iota = cst[:, C_IOTA:C_IOTA + P]
        iota16 = cst[:, C_IO16:C_IO16 + TOPK]

        bank = [ctx.enter_context(nc.psum_tensor(f"bank{b}", [P, T], F32)) for b in range(8)]
        acc = bank[0:2]

        w_loaded = [sem(f"w_loaded{s}") for s in range(4)]
        w_hi_made = sem("w_hi_made")
        w_lo_made = sem("w_lo_made")
        half_done = sem("half_done")
        acc_free = sem("acc_free")
        consts_in = sem("consts_in")
        masks_in = sem("masks_in")
        mem_in = [sem(f"mem_in{b}") for b in range(2)]
        x_in = [sem(f"x_in{b}") for b in range(2)]
        lb_dve = sem("lower_bound_dve")
        lb_act = sem("lower_bound_act")
        pads_zero = sem("pads_zero")
        gate_out = [sem(f"gate_columns_out{b}") for b in range(2)]
        mem_out = [sem(f"mem_out{b}") for b in range(2)]
        dil_out = sem("dil_out")
        hg_out = sem("hg_out")
        mix_in = [sem(f"mix_in{b}") for b in range(3)]
        mix_hi = sem("mix_hi")
        mix_lo = sem("mix_lo")
        gate_in = [sem(f"gate_columns_in{b}") for b in range(2)]
        gates_made = sem("gates_made")
        merged_hi = sem("merged_hi")
        merged_lo = sem("merged_lo")
        xres_in = [sem(f"xres_in{b}") for b in range(2)]
        out_read = sem("out_read")
        residual_out = sem("residual_out")
        sub_keys_in = sem("sub_keys_in")
        acc2_free = sem("acc2_free")
        score_done = sem("score_done")
        score_saved = sem("score_saved")
        gate_exp = sem("gate_exp")
        gate_soft = sem("gate_soft")
        sel_turned = sem("sel_turned")
        sel_saved = sem("sel_saved")
        block_cols = sem("block_cols")
        onehots = sem("onehots")
        gmat_done = sem("gmat_done")
        gmat_hi = sem("gmat_hi")
        gmat_saved = sem("gmat_saved")
        gmat_out = [sem(f"gmat_out{b}") for b in range(2)]
        gelu_out = [sem(f"gelu_out{b}") for b in range(2)]
        residual_in = sem("residual_in")
        gmat_in = [sem(f"gmat_in{b}") for b in range(2)]
        gelu_in = [sem(f"gelu_in{b}") for b in range(4)]
        hid_product = sem("hid_product")
        hid_hi = sem("hid_hi")
        hid_lo = sem("hid_lo")
        y_added = sem("y_added")
        result_out = sem("result_out")
        squared = [sem(f"squared{r}") for r in range(4)]
        summed = [sem(f"squares_summed{r}") for r in range(4)]
        column_sums = sem("column_sums")
        norm = [tuple(Steps(sem(f"norm_{e}{r}"), n) for e, n in zip(("act", "dve"), norm_names(r)))
                for r in range(4)]
        odd_low = {r: Steps(sem(f"norm_pool{r}"), [f"lo{k}" for k in range(1, KT, 2)]) for r in (0, 2)}
        mp, md, ma = (Steps(sem(f"mem_{e}"), n) for e, n in zip(("pe", "dve", "act"), mem_names()))
        dp, dd, da = (Steps(sem(f"dil_{e}"), n, b) for e, n, b in zip(("pe", "dve", "act"), dil_names(), (0, 1, 0)))
        hp, hd, ha = (Steps(sem(f"hg_{e}"), n, b) for e, n, b in zip(("pe", "dve", "act"), hg_names(), (0, 1, 0)))
        UP = ["bg", "m1", "m2", "m3", "a1", "a2"]
        up = Steps(sem("merge_dve"), UP, 2 * len(UP))
        tk = Steps(sem("topk_dve"), topk_names(), 1)

        def squares_of(r):
            return nsq if r else nsq_mem

        def carve(at, *shape):
            n = 1
            for k in shape:
                n *= k
            assert at + n <= WA, (at, shape)
            v = arena[:, at:at + n]
            names = "abcd"[:len(shape)]
            if len(shape) > 1:
                v = v.rearrange(f"p ({' '.join(names)}) -> p {' '.join(names)}",
                                **{k: s for k, s in zip(names[:-1], shape[:-1])})
            return v

        class Area:
            def __init__(self, at=0):
                self.at = at

            def __call__(self, *shape):
                v = carve(self.at, *shape)
                n = 1
                for k in shape:
                    n *= k
                self.at += n
                return v

        a = Area()
        src_x = a(KT, T)
        src_mem = a(KT, MEM)
        nsq = a(2, T)
        nsq_mem = nsq.rearrange("p a (b c) -> p (a b) c", c=MEM)
        a(2, T)
        nrm = a(T)
        mhi = xlo[:, :, 0:MEM]
        mlo = xlo[:, :, MEM:2 * MEM]
        a = Area()
        qm = a(MH, T)
        vm = a(MT, MH, P)
        pm = a(2, MEM)
        ptm = a(2, MT, P)
        om = a(2, T)
        m_end = a.at
        kvm = carve(KT * T, N_KV, MEM)
        a = Area()
        pd = a(2, 3, T)
        ptd = a(3, TT, P)
        od = a(3, T)
        vp = a(3, 2, TT, P)
        assert a.at <= WA - 11 * T
        gst = carve(WA - 2 * T, 2, T)
        qkv = carve(WA - 2 * T - 9 * T, 3, 3, T)
        a = Area()
        hq = a(T)
        hv = a(T)
        hf = a(2, T)
        hk = a(2, T)
        hgt = a(T)
        hsg = a(T)
        hlf = a(2, TT, P + 1)
        hb = a(2, TT, P + 1)
        hksum = a(T)
        ht = a(2, T)
        he = a(2, T)
        hkl = a(2, T)
        hql = a(2, T)
        hqs = a(2, T)
        hkn = a(2, 3, P)
        hvn = a(TT, P)
        hst = a(2, 3, P)
        hres = a(T)
        assert a.at <= WA - 2 * T
        hkst = hf
        ham = hv.rearrange("p (a b) -> p a b", a=TT)
        hosq, hr = hkl[:, 0], hkl[:, 1]
        a = Area()
        merged = a(KT, T)
        xres = a(2, T)
        a(2, T)
        gt = a(2, 3, T)
        umul = a(2, T)
        late = merged[:, HT:KT]
        a = Area()
        qpt = a(2, T)
        scores = a(TT, 2 * PH, NK)
        sw = a(TT, 2, NK)
        sw2 = a(TT, 2, NK)
        cand = a(TT, TOPK, TOPK)
        cand2 = a(TT, TOPK, TOPK)
        sel = a(3, TT, P)
        v16 = a(TT, 2, TOPK)
        eq = sw.rearrange("p a b c -> p a (b c)").rearrange("p a (b c) -> p a b c", b=TOPK)
        eq2 = sw2.rearrange("p a b c -> p a (b c)").rearrange("p a (b c) -> p a b c", b=TOPK)
        tab = cst[:, C_DM:C_DM + 3 * DMW]
        i16 = tab[:, 0:128].bitcast(U32).rearrange("p (a b c) -> p a b c", a=TT, b=2)
        i16f = tab[:, 128:256].rearrange("p (a b c) -> p a b c", a=TT, b=2)
        best = tab[:, 256:320].rearrange("p (a b) -> p a b", a=TT)
        pos = tab[:, 320:384].bitcast(U32).rearrange("p (a b) -> p a b", a=TT)
        phi = tab[:, 384:448].bitcast(U32).rearrange("p (a b) -> p a b", a=TT)
        plo = tab[:, 448:512].bitcast(U32).rearrange("p (a b) -> p a b", a=TT)
        phif = tab[:, 512:576].rearrange("p (a b) -> p a b", a=TT)
        plof = tab[:, 576:640].rearrange("p (a b) -> p a b", a=TT)
        bsum = tab[:, 768:800]
        brcp = tab[:, 800:832]
        cur = tab[:, 896:896 + 4 * TB].rearrange("p (a b) -> p a b", a=4)
        skt = tab[:, 1024:1024 + 2 * NK].rearrange("p (a b) -> p a b", a=2)
        eg = qpt
        gstage = carve(2 * T, 2, NK, TB)
        iit = carve(2 * T + 2 * NK * TB, T)
        jjt = carve(3 * T + 2 * NK * TB, T)
        gtt = carve(4 * T + 2 * NK * TB, T)
        assert 5 * T + 2 * NK * TB <= 2 * T + TT * 2 * PH * NK + 4096
        a = Area()
        y = a(KT, T)
        gsb = a(2, NTB, 4 * TB)
        agb = a(4, T)
        htmp = a(2, T)

        mxs = small[:, 0:8]
        rms = [small[:, 24 + TT * r:24 + TT * r + TT] for r in range(4)]
        dsl = small[:, 8:14]
        dmx, dnm, ddd, ded, dsum = ([small[:, 80 + 32 * u + 4 * k:83 + 32 * u + 4 * k] for u in range(2)]
                                    for k in range(5))
        dzs, dw = (small[:, 16 + 4 * k:19 + 4 * k] for k in range(2))
        dmm, dz, drz = (small[:, 44 + k:45 + k] for k in range(3))
        hpar = small[:, 56:60]
        hdec = small[:, 60:68].rearrange("p (d t) -> p d t", d=2)
        bgc = small[:, 68:74].rearrange("p (u b) -> p u b", u=2)
        lbs = small[:, 80:160]
        gate_cols = gate_dram.rearrange("(b j) p t -> j p b t", b=3)
        dil_tiles = mix_dram[0:HG].rearrange("(g s) p t -> s p g t", s=2)

        block = ctx.enter_context(nc.Block())

        @block.sync
        def _(sp):
            def stream(w, first):
                skip = 4 if first == 0 else 0
                for s in range(skip):
                    sp.dma_start(raw[s][:], w[s]).then_inc(w_loaded[s], 16)
                with sp.Fori(skip // 4, w.shape[0] // 4) as i:
                    for s in range(4):
                        sp.wait_ge(w_lo_made, 4 * i + (first + s - 3))
                        sp.dma_start(raw[s][:], w[4 * i + s]).then_inc(w_loaded[s], 16)

            m = 0
            for w in (w_kv, w_in, w_up, w_out, w_pq, w_u, w_v):
                stream(w, m)
                m += w.shape[0]
            assert m == HALVES

        @block.gpsimd
        def _(pool):
            def low_halves(first, end):
                with pool.Fori(first // 4, end // 4) as i:
                    for s in range(4):
                        pool.wait_ge(w_hi_made, 4 * i + (s + 1))
                        nc.gpsimd.tensor_tensor(wlo[s][:], raw[s][:], whi[s][:], ALU.subtract).then_inc(w_lo_made, 1)

            def odd_tiles(r, src, his, lows):
                for k in range(1, KT, 2):
                    norm[r][0].wait(pool, f"hi{k}")
                    odd_low[r].done(nc.gpsimd.tensor_tensor(lows[:, k], src[:, k], his[:, k], ALU.subtract), f"lo{k}")

            low_halves(0, 4)
            odd_tiles(0, src_mem, mhi, mlo)
            assert 2 * C_PQ % 4 == 0
            low_halves(4, 2 * C_PQ + 4)
            odd_tiles(2, y, xhi, xlo)
            low_halves(2 * C_PQ + 4, HALVES)

        @block.scalar
        def _(act):
            A = nc.scalar

            def round_half(q, s, first=False):
                act.wait_ge(w_loaded[s], 16 * q + 16)
                if not first:
                    act.wait_ge(half_done, 4 * q + (s - 3))
                A.activation(whi[s][:], raw[s][:], ACT.Copy).then_inc(w_hi_made, 1)

            def ahead(n, i, per, part):
                m = 2 * n + 4 + part
                round_half(i * (per // 2) + m // 4, m % 4)

            def chunk_ready(n, i, per):
                act.wait_ge(half_done, i * (2 * per) + (2 * n + 2))

            for b in range(2):
                act.dma_start(src_mem[:, HT * b:HT * b + HT], mem_t[:, HT * b:HT * b + HT]).then_inc(mem_in[b], 16)
            act.dma_start(cst[:, 0:C_DM], const[:, 0:C_DM]).then_inc(consts_in, 16)
            act.dma_start(prm[:], params).then_inc(consts_in, 16)
            for b in range(2):
                act.dma_start(src_x[:, HT * b:HT * b + HT], x_t[:, HT * b:HT * b + HT]).then_inc(x_in[b], 16)
            act.dma_start(cst[:, C_DM:NCONST], const[:, C_DM:NCONST]).then_inc(masks_in, 16)
            act.dma_start(lmask[:], level_mask).then_inc(masks_in, 16)
            act.sem_inc(acc_free, 2)
            act.sem_inc(acc2_free, 2)
            for s_ in (*gate_out, dil_out, hg_out, *gelu_out, *gmat_out):
                act.sem_inc(s_, 16)
            for s_ in (gates_made, gmat_saved, score_saved):
                act.sem_inc(s_, 1)
            def square_tile(r, src, k):
                ring = squares_of(r)
                n = ring.shape[1]
                if k >= n:
                    act.wait_ge(summed[r], k - n + 1)
                A.activation(ring[:, k % n], src[:, k], ACT.Square).then_inc(squared[r], 1)

            def norm_root(r, width):
                norm[r][1].wait(act, "ms")
                norm[r][0].done(A.activation(rms[r][:, 0:width // P], rms[r][:, 0:width // P], ACT.Sqrt), "sqrt")

            def sqrt_table():
                A.activation(small[:, 77:78], ones[:, 0:1], ACT.Sqrt)

            def norm_hi(r, src, k, out):
                norm[r][1].wait(act, f"xn{k}")
                norm[r][0].done(A.activation(out, src, ACT.Copy), f"hi{k}")

            for k in range(KT):
                if k % HT == 0:
                    round_half(0, k // HT, first=True)
                    act.wait_ge(mem_in[k // HT], 16)
                square_tile(0, src_mem, k)
            act.wait_ge(consts_in, 32)
            sqrt_table()
            norm_root(0, MEM)
            for s in range(2, 4):
                round_half(0, s, first=True)
            for k in range(KT):
                norm_hi(0, src_mem[:, k], k, mhi[:, k])
            act.wait_ge(lb_dve, 6)
            A.activation(lbs[:, 24:48], lbs[:, 0:24], ACT.Exp).then_inc(lb_act, 1)

            act.wait_ge(summed[0], KT)
            norm[0][1].wait(act, f"lo{KT - 2}")
            odd_low[0].wait(act, f"lo{KT - 1}")
            for c in range(N_KV):
                if c == 5:
                    norm_root(1, T)
                ahead(c, 0, 2, 0)
                chunk_ready(c, 0, 2)
                A.activation(kvm[:, c], acc[c % 2][:, 0:MEM], ACT.Copy).then_inc(acc_free, 1)
                ahead(c, 0, 2, 1)
                if c < 4:
                    for k in range(4 * c, 4 * c + 4):
                        if k % HT == 0:
                            act.wait_ge(x_in[k // HT], 16)
                        square_tile(1, src_x, k)
                if c >= 5:
                    for k in range((0, 6, 11)[c - 5], (6, 11, KT)[c - 5]):
                        norm_hi(1, src_x[:, k], k, xhi[:, k])
            norm[1][1].wait(act, f"lo{KT - 1}")
            with act.Fori(0, N_MQ // 2) as i:
                for u in range(2):
                    ahead(C_MQ + u, i, 2, 0)
                    chunk_ready(C_MQ + u, i, 2)
                    A.activation(qm[:, 2 * i + u], acc[u][:], ACT.Copy).then_inc(acc_free, 1)
                    ahead(C_MQ + u, i, 2, 1)
            def gate_chunk_out(n, i, per, b, waited):
                act.wait_ge(gate_out[b], waited + 16)
                A.activation(gst[:, b], acc[n % 2][:], ACT.Copy).then_inc(acc_free, 1)

            def gate_store(n, i, per, b, tile):
                act.wait_ge(acc_free, i * per + (n + 3))
                act.dma_start(gate_dram[tile], gst[:, b]).then_inc(gate_out[b], 16)

            for h in range(MH):
                for tt in range(TT):
                    u = (h * TT + tt) % 2
                    md.wait(act, f"nm{h}{tt}")
                    ma.done(A.activation(pm[:, u], bank[2 + u][:, 0:MEM], ACT.Exp, bias=mxs[:, 2 + u:3 + u],
                                         scale=float(P) ** -0.5, accum_out=mxs[:, 4 + u:5 + u]), f"ex{h}{tt}")
                    k = h * TT + tt
                    if k % 2 and k // 2 < 2 * N_MEM_GATES:
                        x = k // 2
                        n = C_MG + x // 2
                        ahead(n, 0, 2, x % 2)
                        if x % 2:
                            g = x // 2
                            chunk_ready(n, 0, 2)
                            gate_chunk_out(n, 0, 2, g % 2, 16 * (g // 2))
                            gate_store(n, 0, 2, g % 2, g)
                if h:
                    md.wait(act, f"ov{h - 1}")
                    act.dma_start(mix_dram[HG + h - 1], om[:, (h - 1) % 2]).then_inc(mem_out[(h - 1) % 2], 16)
            md.wait(act, f"ov{MH - 1}")
            act.dma_start(mix_dram[HG + MH - 1], om[:, (MH - 1) % 2]).then_inc(mem_out[(MH - 1) % 2], 16)

            with act.Fori(0, DIL_S) as i:
                for c in range(N_DIL):
                    n = C_D + c
                    ahead(n, i, N_D, 0)
                    chunk_ready(n, i, N_D)
                    if c == 0:
                        dd.wait_iterations(act, i)
                    A.activation(qkv[:, c // 3, c % 3], acc[n % 2][:], ACT.Copy,
                                 scale=0.125 if c < 3 else 1.0).then_inc(acc_free, 1)
                    ahead(n, i, N_D, 1)
                def exponentials(q):
                    u = q % 2
                    dd.wait(act, f"dd{q}", i)
                    da.done(A.activation(ded[u], ddd[u], ACT.Exp), f"ed{q}")
                    for g in range(3):
                        lo, hi = (P * v for v in key_tiles(g, TRIPLES[q][0]))
                        da.done(A.activation(pd[:, u, g, lo:hi], pd[:, u, g, lo:hi], ACT.Exp, bias=dnm[u][:, g:g + 1],
                                             accum_out=dsum[u][:, g:g + 1]), f"ex{q}{g}")

                exponentials(0)
                exponentials(1)
                for q in range(len(TRIPLES)):
                    if q < 2 * N_DIL_GATES:
                        x = q // 2
                        n = C_D + N_DIL + x
                        ahead(n, i, N_D, q % 2)
                        if q % 2:
                            chunk_ready(n, i, N_D)
                            gate_chunk_out(n, i, N_D, x % 2, i * (16 * ((N_DIL_GATES + 1 - x % 2) // 2))
                                           + 16 * (N_MEM_GATES // 2 + x // 2))
                            gate_store(n, i, N_D, x % 2, i * N_DIL_GATES + (N_MEM_GATES + x))
                    for g in range(1, 3):
                        lo, hi = key_tiles(g, TRIPLES[q][0])
                        dp.wait(act, f"pt{q}{g}", i)
                        da.done(A.activation(ptd[:, g, lo:hi],
                                             bank[2 + g][:, P * lo:P * hi].rearrange("p (a b) -> p a b", b=P),
                                             ACT.Copy), f"ev{q}{g}")
                    if q + 2 < len(TRIPLES):
                        exponentials(q + 2)
                dd.wait(act, "od2", i)
                act.dma_start(dil_tiles[i], od).then_inc(dil_out, 16)

            before_hg = [N_MEM_GATES // 2 + DIL_S * ((N_DIL_GATES + 1 - b) // 2) for b in range(2)]
            act.wait_ge(dil_out, 16 * DIL_S + 16)
            act.wait_ge(mem_out[0], 32)
            act.wait_ge(mem_out[1], 32)
            act.wait_ge(pads_zero, 4)
            act.dma_start(early_a[:], mix_dram[0:2].rearrange("k p t -> p k t")).then_inc(mix_in[0], 16)
            act.dma_start(early_b[:], mix_dram[2:HT].rearrange("k p t -> p k t")).then_inc(mix_in[0], 16)
            with act.Fori(0, HG) as i:
                for c in range(N_HGC):
                    n = C_H + c
                    a_ = acc[n % 2]
                    ahead(n, i, N_H, 0)
                    chunk_ready(n, i, N_H)
                    if c == 0:
                        hd.wait_iterations(act, i)
                        A.activation(hq, a_[:], ACT.Copy).then_inc(acc_free, 1)
                    elif c == 1:
                        A.activation(hv, a_[:], ACT.Copy).then_inc(acc_free, 1)
                    elif c < 4:
                        A.activation(hf[:, c - 2], a_[:], ACT.Sigmoid).then_inc(acc_free, 1)
                    else:
                        A.activation(hgt, a_[:], ACT.Copy)
                        A.activation(hsg, a_[:], ACT.Sigmoid).then_inc(acc_free, 1)
                    ahead(n, i, N_H, 1)
                for d in range(2):
                    hd.wait(act, f"f{d}", i)
                    ha.done(A.activation(hlf[:, d, :, 1:P + 1], hf[:, d].rearrange("p (a b) -> p a b", a=TT),
                                         ACT.Ln), f"ln{d}")
                for x in range(2 * N_HG_GATES):
                    n = C_H + N_HGC + x // 2
                    ahead(n, i, N_H, x % 2)
                    if x % 2:
                        g = x // 2
                        chunk_ready(n, i, N_H)
                        gate_chunk_out(n, i, N_H, g % 2, i * (16 * ((N_HG_GATES + 1 - g % 2) // 2))
                                       + (16 * (g // 2) + 16 * before_hg[g % 2]))
                    l = x - 1
                    if 0 <= l < 7:
                        blk = 2 * LEVELS[l]
                        te = ht.rearrange("p a b -> p (a b)").rearrange("p (m c) -> p m c", c=blk)
                        ee = he.rearrange("p a b -> p (a b)").rearrange("p (m c) -> p m c", c=blk)
                        hd.wait(act, f"t{l}1", i)
                        if l:
                            hd.wait(act, f"ko{l - 1}", i)
                        ha.done(A.activation(ee[:, :, 0:blk // 2], te[:, :, 0:blk // 2], ACT.Exp, scale=-1.0), f"ee{l}")
                        ha.done(A.activation(ee[:, :, blk // 2:blk], te[:, :, blk // 2:blk], ACT.Exp), f"eo{l}")
                    if x == 8:
                        hd.wait(act, "ts1", i)
                        ha.done(A.activation(hdec, hb[:, :, :, P], ACT.Exp), "dec")
                        for d in range(2):
                            if d:
                                hd.wait(act, "ks0", i)
                            ha.done(A.activation(he[:, 0].rearrange("p (a b) -> p a b", a=TT),
                                                 hb[:, d, :, 1 - d:P + 1 - d], ACT.Exp), f"x1{d}")
                            ha.done(A.activation(he[:, 1], ht[:, d], ACT.Exp, scale=-1.0), f"x2{d}")
                    if x == 12:
                        hp.wait(act, "o", i)
                        hd.wait(act, "sb0", i)
                        ha.done(A.activation(hosq, bank[2][:], ACT.Square), "sq")
                        sqrt_table()
                    if x % 2:
                        gate_store(n, i, N_H, g % 2, i * N_HG_GATES + (N_MEM_GATES + DIL_S * N_DIL_GATES + g))
                hd.wait(act, "ms", i)
                ha.done(A.activation(hr, hr, ACT.Sqrt), "sqrt")
                hd.wait(act, "o2", i)
                act.dma_start(mix_dram[HG + MH + i], hres).then_inc(hg_out, 16)

            hd.wait_iterations(act, HG)
            act.wait_ge(half_done, 2 * C_UP)
            for k in range(KT):
                if k == 1:
                    act.dma_start(late[:, 0:HT - 1], mix_dram[HT:KT - 1].rearrange("k p t -> p k t"))\
                        .then_inc(mix_in[1], 16)
                if k == HT - 1:
                    act.wait_ge(hg_out, 16 * HG + 16)
                    act.dma_start(late[:, HT - 1], mix_dram[KT - 1]).then_inc(mix_in[2], 16)
                if k in (0, HT, KT - 1):
                    act.wait_ge(mix_in[(0, HT, KT - 1).index(k)], 32 if k == 0 else 16)
                A.activation(xhi[:, k], early(k) if k < HT else late[:, k - HT], ACT.Copy).then_inc(mix_hi, 1)
            for b in range(2):
                act.wait_ge(gate_out[b], 16 * (before_hg[b] + HG * ((N_HG_GATES + 1 - b) // 2)) + 16)
            act.dma_start(gt[:, 0], gate_cols[0]).then_inc(gate_in[0], 16)
            act.dma_start(xres[:, 0], x_t[:, 0]).then_inc(xres_in[0], 16)
            act.dma_start(skt, sub_keys_t).then_inc(sub_keys_in, 16)

            def merge_tile(u, i, last):
                if not last:
                    up.wait_iterations(act, 2 * i + u)
                    act.dma_start(gt[:, 1 - u], gate_cols[2 * i + (u + 1)]).then_inc(gate_in[1 - u], 16)
                ahead(C_UP + u, i, 2, 0)
                act.wait_ge(gate_in[u], 16 * i + 16)
                up.wait(act, "bg", 2 * i + u)
                for b in range(3):
                    A.activation(gt[:, u, b], gt[:, u, b], ACT.Sigmoid, bias=bgc[:, u, b:b + 1]).then_inc(gates_made, 1)
                ahead(C_UP + u, i, 2, 1)

            E2 = KT // 2 - 1
            with act.Fori(0, E2) as i:
                for u in range(2):
                    merge_tile(u, i, False)
            merge_tile(0, E2, False)
            merge_tile(1, E2, True)

            act.wait_ge(mix_lo, KT)
            act.wait_ge(half_done, 2 * C_OUT)
            for k in range(KT):
                up.wait(act, "a2", KT - 2 if k < KT - 1 else KT - 1)
                A.activation(xhi[:, k], merged[:, k], ACT.Copy).then_inc(merged_hi, 1)

            def out_tile(u, i, last):
                if not last:
                    act.wait_ge(out_read, 2 * i + u + 2)
                    act.dma_start(xres[:, 1 - u], x_t[:, 2 * i + (u + 1)]).then_inc(xres_in[1 - u], 16)
                ahead(C_OUT + u, i, 2, 0)
                ahead(C_OUT + u, i, 2, 1)
                act.wait_ge(summed[2], 2 * i + u + 1)
                act.wait_ge(out_read, 2 * i + u + 3)
                act.dma_start(res_dram[2 * i + u], y[:, 2 * i + u]).then_inc(residual_out, 16)
                A.activation(nsq[:, u], y[:, 2 * i + u], ACT.Square).then_inc(squared[2], 1)

            with act.Fori(0, E2) as i:
                for u in range(2):
                    out_tile(u, i, False)
            out_tile(0, E2, False)
            sqrt_table()
            out_tile(1, E2, True)

            norm_root(2, T)
            act.wait_ge(half_done, 2 * C_PQ)
            for k in range(KT):
                norm_hi(2, y[:, k], k, xhi[:, k])
            norm[2][1].wait(act, f"lo{KT - 2}")
            odd_low[2].wait(act, f"lo{KT - 1}")

            def save_scores(u, i):
                act.wait_ge(score_done, 2 * i + (u + 1))
                A.activation(scores[:, :, 2 * i + u], bank[2 + u][:].rearrange("p (a b) -> p a b", a=TT), ACT.Copy)\
                    .then_inc(score_saved, 1)

            def query_chunk(u, i):
                chunk_ready(C_PQ + u, i, 2)
                A.activation(qpt[:, u], acc[u][:], ACT.Copy).then_inc(acc2_free, 1)
                ahead(C_PQ + u, i, 2, 1)

            ahead(C_PQ, 0, 2, 0)
            query_chunk(0, 0)
            ahead(C_PQ + 1, 0, 2, 0)
            save_scores(0, 0)
            query_chunk(1, 0)
            with act.Fori(1, PH) as i:
                ahead(C_PQ, i, 2, 0)
                save_scores(1, i - 1)
                query_chunk(0, i)
                ahead(C_PQ + 1, i, 2, 0)
                save_scores(0, i)
                query_chunk(1, i)

            def expert_chunk(c, i, per, beside=None, after=None, staging=eg):
                n = C_U + c
                u = c % 2
                ahead(n, i, per, 0)
                if beside is not None:
                    beside()
                chunk_ready(n, i, per)
                if after is not None:
                    after()
                act.wait_ge(gelu_out[u], i * (8 * per) + 16 * (c // 2) + 16)
                A.activation(staging[:, u], acc[n % 2][:], ACT.Gelu).then_inc(acc2_free, 1)
                ahead(n, i, per, 1)
                act.wait_ge(acc2_free, i * per + (2 * PH + c + 3))
                act.dma_start(act_dram[i * per + c], staging[:, u]).then_inc(gelu_out[u], 16)

            def expert_chunks(first, count, staging=eg):
                with act.Fori(0, count // 2) as i:
                    for u in range(2):
                        expert_chunk(first + u, i, 2, staging=staging)

            expert_chunk(0, 0, 2, lambda: save_scores(1, PH - 1), staging=early_a)
            expert_chunk(1, 0, 2, staging=early_a)
            expert_chunks(2, U_1 - 2)
            tk.wait_iterations(act, PH)
            A.activation(sel[:, 2], sel[:, 2], ACT.Exp).then_inc(gate_exp, 1)
            expert_chunks(U_1, U_2)
            expert_chunks(U_1 + U_2, U_3)
            act.wait_ge(sel_saved, 5)
            first = U_1 + U_2 + U_3
            with act.Fori(0, NTB // 2) as i:
                for c in range(8):
                    b = c // 4

                    def save_high(q):
                        if q % 8 == 0:
                            act.wait_ge(gmat_out[b], 16 * i + 16)
                        act.wait_ge(gmat_done, 16 * i + (q + 1) + 1)
                        for x in range(2):
                            pair = bank[2 + 2 * (q % 2) + x][:].rearrange("p (t h j) -> p t h j", t=2, h=2)
                            t0 = 4 * (q % 8) + 2 * x
                            last = A.activation(gstage[:, b, :, t0:t0 + 2].rearrange("p j t -> p t j"),
                                                pair[:, :, 0], ACT.Copy)
                        last.then_inc(gmat_hi, 1)

                    expert_chunk(first + c, i, 8, lambda: save_high(2 * c), lambda: save_high(2 * c + 1))
                    if c % 4 == 3:
                        act.wait_ge(gmat_saved, 16 * i + (2 * c + 2) + 1)
                        act.dma_start(gmat_dram[2 * i + b], gstage[:, b]).then_inc(gmat_out[b], 16)

            for b in range(2):
                act.wait_ge(gmat_out[b], 16 * (NTB // 2) + 16)

            def load_gates(s, r):
                act.dma_start(gsb[:, r], gmat_dram[:, :, bass.ds(8 * s + 4 * r, 4), :]
                              .rearrange("b p j t -> p b (j t)")).then_inc(gmat_in[r], 16)

            def load_gelu(s, k):
                act.dma_start(agb[:, k % 4], act_dram[8 * s + k]).then_inc(gelu_in[k % 4], 16)

            def hidden(s, k, half):
                act.wait_ge(hid_product, 8 * s + (k + 1))
                A.activation(xhi[:, 8 * half + k], htmp[:, k % 2], ACT.Copy).then_inc(hid_hi, 1)

            for r in range(2):
                load_gates(0, r)
            for k in range(4):
                load_gelu(0, k)
            for b in range(2):
                act.wait_ge(gelu_out[b], 8 * (first + U_B) + 16)
            act.dma_start(y, res_dram.rearrange("k p t -> p k t")).then_inc(residual_in, 16)
            expert_chunks(first + U_B, U_C - 2, early_a)

            def hidden_first(k):
                hidden(0, k, 0)
                if k >= 2:
                    load_gelu((k + 4) // 8, (k + 4) % 8)

            expert_chunk(NK - 2, 0, 2, staging=early_a)
            for k in range(2):
                act.wait_ge(hid_product, k + 1)
                load_gelu(0, k + 4)
            expert_chunk(NK - 1, 0, 2, lambda: [hidden_first(k) for k in range(4)], staging=early_a)
            for k in range(4, 8):
                hidden_first(k)
            for r in range(2):
                load_gates(1, r)
            for b in range(2):
                act.wait_ge(gelu_out[b], 16 * (NK // 2) + 16)

            def sub_block(s, par, prepare, more):
                for x in range(KT):
                    if prepare and x in PREPARED_AT:
                        k = PREPARED_AT.index(x)
                        hidden(s + 1, k, 1 - par)
                        if k < 4:
                            load_gelu(s + 1, k + 4)
                        elif more:
                            load_gelu(s + 2, k - 4)
                        if more and k % 4 == 3:
                            load_gates(s + 2, k // 4)
                    m = 2 * C_V + KT * par + x + 4
                    if isinstance(s, int) and s == 15:
                        if x < KT - 4:
                            round_half((2 * C_V + KT * s + x + 4) // 4, (x + 4) % 4)
                        act.wait_ge(y_added, KT * s + x + 1)
                        square_tile(3, y, x)
                    elif isinstance(s, int):
                        m = 2 * C_V + KT * s + x + 4
                        round_half(m // 4, m % 4)
                    else:
                        round_half((s - par) * 4 + m // 4, m % 4)

            with act.Fori(0, 7) as i:
                for par in range(2):
                    sub_block(2 * i + par, par, True, True)
            sub_block(14, 0, True, False)
            sqrt_table()
            sub_block(15, 1, False, False)

            norm_root(3, T)
            for k in range(0, KT, 2):
                norm[3][1].wait(act, f"xn{k + 1}")
                act.dma_start(out_t[k:k + 2].rearrange("k p t -> p k t"), y[:, k:k + 2]).then_inc(result_out, 16)
            act.wait_ge(result_out, 16 * (KT // 2))

        @block.vector
        def _(dve):
            V = nc.vector

            for s_ in (dd.sem, hd.sem, tk.sem, onehots):
                dve.sem_inc(s_, 1)
            dve.sem_inc(out_read, 2)

            def sum_tile(r, k, width):
                dve.wait_ge(squared[r], k + 1)
                ring = squares_of(r)
                if k == 0:
                    V.tensor_copy(nrm[:, 0:width], ring[:, 0]).then_inc(summed[r], 1)
                else:
                    dve.wait_ge(summed[r], k)
                    V.tensor_tensor(nrm[:, 0:width], nrm[:, 0:width], ring[:, k % ring.shape[1]], ALU.add)\
                        .then_inc(summed[r], 1)

            for k in range(KT):
                sum_tile(0, k, MEM)
            dve.wait_ge(consts_in, 32)
            lgt = prm[:, P_LBF:P_LBF + 24].rearrange("p (d l h) -> p d l h", d=2, l=2)
            sh = lbs[:, 0:24].rearrange("p (d l h) -> p d l h", d=2, l=2)
            ex = lbs[:, 24:48].rearrange("p (d l h) -> p d l h", d=2, l=2)
            mx = lbs[:, 48:60].rearrange("p (d h) -> p d h", d=2)
            sm = lbs[:, 60:72].rearrange("p (d h) -> p d h", d=2)
            count = [0]

            def pause(steps, after, name, it):
                steps.wait(dve, after, it)
                steps.done(V.memset(small[:, 76:77], 0.0), name)

            def link(ins):
                count[0] += 1
                ins.then_inc(lb_dve, 1)
                dve.wait_ge(lb_dve, count[0])

            link(V.tensor_tensor(mx[:, 0], lgt[:, 0, 0], lgt[:, 0, 1], ALU.max))
            link(V.tensor_tensor(mx[:, 1], lgt[:, 1, 0], lgt[:, 1, 1], ALU.max))
            for d in range(2):
                for l in range(2):
                    link(V.tensor_tensor(sh[:, d, l], lgt[:, d, l], mx[:, d], ALU.subtract))

            def norm_rest(r, src, width, gcol, his=None, lows=None):
                na_, nd_ = norm[r]
                b = bank[7 - r % 2]
                n = width // P
                dve.wait_ge(column_sums, 2 * r + 1)
                nd_.done(V.tensor_scalar(rms[r][:, 0:n], b[:, 0:n], 1.0 / D, EPS, ALU.mult, ALU.add), "ms")
                na_.wait(dve, "sqrt")
                nd_.done(V.reciprocal(rms[r][:, 0:n], rms[r][:, 0:n]), "rcp")
                nd_.wait(dve, "rcp")
                for tt in range(n):
                    ins = V.tensor_scalar(nrm[:, P * tt:P * tt + P], ident, rms[r][:, tt:tt + 1], None, ALU.mult)
                nd_.done(ins, "diag")
                dve.wait_ge(column_sums, 2 * r + 2)

                def lo(k):
                    na_.wait(dve, f"hi{k}")
                    nd_.done(V.tensor_tensor(lows[:, k], src[:, k], his[:, k], ALU.subtract), f"lo{k}")

                for k in range(KT):
                    nd_.done(V.scalar_tensor_tensor(src[:, k], src[:, k], prm[:, gcol + k:gcol + k + 1],
                                                    b[:, 0:width], ALU.mult, ALU.mult), f"xn{k}")
                    if r in odd_low and k % 2:
                        lo(k - 1)
                if r == 1:
                    dve.wait_ge(half_done, 2 * N_KV)
                    for k in range(KT):
                        lo(k)

            dve.wait_ge(mem_in[0], 16)
            dve.wait_ge(mem_in[1], 16)
            norm_rest(0, src_mem, MEM, P_MEM, mhi, mlo)
            dve.wait_ge(lb_act, 1)
            for d in range(2):
                link(V.tensor_tensor(sm[:, d], ex[:, d, 0], ex[:, d, 1], ALU.add))
            link(V.reciprocal(sm, sm))
            for d in range(2):
                link(V.tensor_tensor(lbt[:, :, 2 * d], ex[:, d, 0], sm[:, d], ALU.mult))
            for d in range(2):
                link(V.tensor_scalar(lbt[:, :, 2 * d + 1], lbt[:, :, 2 * d], -1.0, 1.0, ALU.mult, ALU.add))
            for k in range(KT):
                sum_tile(1, k, T)
            dve.wait_ge(x_in[0], 16)
            dve.wait_ge(x_in[1], 16)
            norm_rest(1, src_x, T, P_MIX, xhi, xlo)

            for h in range(MH):
                mp.wait(dve, f"vt{h}")
                md.done(V.tensor_copy(vm[:, :, h, :], bank[4 + h % 2][:, 0:MEM].rearrange("p (a b) -> p a b", a=MT)),
                        f"vm{h}")

            def save_output(h):
                if h >= 2:
                    dve.wait_ge(mem_out[h % 2], 16)
                mp.wait(dve, f"pv{h}{TT - 1}")
                md.done(V.tensor_copy(om[:, h % 2], bank[6 + h % 2][:]), f"ov{h}")

            units = [(h, tt) for h in range(MH) for tt in range(TT)]

            def mem_maximum(k):
                if k < len(units):
                    n, u = "%d%d" % units[k], k % 2
                    mp.wait(dve, f"sc{n}")
                    md.done(V.reduce_max(mxs[:, u:u + 1], bank[2 + u][:, 0:MEM], AX_X), f"mx{n}")
                    md.wait(dve, f"mx{n}")
                    md.done(V.tensor_scalar(mxs[:, 2 + u:3 + u], mxs[:, u:u + 1], -float(P) ** -0.5, None, ALU.mult),
                            f"nm{n}")

            def mem_weights(k):
                if k < len(units):
                    n, u = "%d%d" % units[k], k % 2
                    ma.wait(dve, f"ex{n}")
                    md.done(V.reciprocal(mxs[:, 6 + u:7 + u], mxs[:, 4 + u:5 + u]), f"rc{n}")
                    md.wait(dve, f"rc{n}")
                    md.done(V.tensor_scalar(pm[:, u], pm[:, u], mxs[:, 6 + u:7 + u], None, ALU.mult), f"sp{n}")

            mem_maximum(0)
            mem_maximum(1)
            mem_weights(0)
            for k, (h, tt) in enumerate(units):
                mem_weights(k + 1)
                mp.wait(dve, f"pt{h}{tt}")
                md.done(V.tensor_copy(ptm[:, k % 2], bank[4 + k % 2][:, 0:MEM].rearrange("p (a b) -> p a b", a=MT)),
                        f"ev{h}{tt}")
                if h and tt == 0:
                    save_output(h - 1)
                mem_maximum(k + 2)
            save_output(MH - 1)

            dve.wait_ge(masks_in, 32)
            V.memset(vp, 0.0).then_inc(pads_zero, 1)
            dve.wait_ge(pads_zero, 1)
            dve.wait_ge(mem_out[0], 32)
            dve.wait_ge(mem_out[1], 32)
            md.wait(dve, f"ov{MH - 1}")
            with dve.Fori(0, DIL_S) as i:
                dd.done(V.tensor_copy(dsl, cst[:, bass.ds(C_SL + 6 * i, 6)]), "slopes")
                for g in range(3):
                    dp.wait(dve, f"vt{g}", i)
                    for a_ in range(2):
                        vals = bank[2 + g][:].rearrange("p (s c) -> p s c", s=TT)
                        dd.done(V.tensor_copy(vp[:, g, a_, :, 64 * a_:64 * a_ + 64], vals[:, :, 64 * a_:64 * a_ + 64]),
                                f"vp{g}{a_}")
                dd.wait(dve, "slopes", i)

                def maxima(q):
                    tt, a_ = TRIPLES[q]
                    u = q % 2
                    for g in range(3):
                        lo, hi = (P * v for v in key_tiles(g, tt))
                        dp.wait(dve, f"sc{q}{g}", i)
                        dd.done(V.scalar_tensor_tensor(pd[:, u, g, lo:hi],
                                                       dist[:, g, 3 * P - P * tt + lo:3 * P - P * tt + hi],
                                                       dsl[:, 2 * g + a_:2 * g + a_ + 1], bank[2 + g][:, lo:hi],
                                                       ALU.mult, ALU.add), f"sm{q}{g}")
                        dd.wait(dve, f"sm{q}{g}", i)
                        dd.done(V.reduce_max(dmx[u][:, g:g + 1], pd[:, u, g, lo:hi], AX_X), f"mx{q}{g}")
                    dd.wait(dve, f"mx{q}2", i)
                    dd.done(V.tensor_scalar(dnm[u], dmx[u], -1.0, None, ALU.mult), f"nm{q}")
                    dd.done(V.reduce_max(dmm, dmx[u], AX_X), f"mm{q}")
                    dd.wait(dve, f"mm{q}", i)
                    dd.done(V.tensor_scalar(ddd[u], dmx[u], dmm, None, ALU.subtract), f"dd{q}")

                def weights(q):
                    u = q % 2
                    da.wait(dve, f"ex{q}2", i)
                    dd.done(V.tensor_tensor(dzs, ded[u], dsum[u], ALU.mult), f"zs{q}")
                    dd.wait(dve, f"zs{q}", i)
                    dd.done(V.reduce_sum(dz, dzs, AX_X), f"z{q}")
                    dd.wait(dve, f"z{q}", i)
                    dd.done(V.reciprocal(drz, dz), f"rz{q}")
                    dd.wait(dve, f"rz{q}", i)
                    dd.done(V.tensor_scalar(dw, ded[u], drz, None, ALU.mult), f"w{q}")

                maxima(0)
                maxima(1)
                weights(0)
                for q, (tt, a_) in enumerate(TRIPLES):
                    u = q % 2
                    dd.wait(dve, f"w{q}", i)
                    for g in range(3):
                        lo, hi = (P * v for v in key_tiles(g, tt))
                        dd.done(V.tensor_scalar(pd[:, u, g, lo:hi], pd[:, u, g, lo:hi], dw[:, g:g + 1], None,
                                                ALU.mult), f"sp{q}{g}")
                    lo, hi = key_tiles(0, tt)
                    dp.wait(dve, f"pt{q}0", i)
                    dd.done(V.tensor_copy(ptd[:, 0, lo:hi],
                                          bank[2][:, P * lo:P * hi].rearrange("p (a b) -> p a b", b=P)), f"ev{q}0")
                    if q + 1 < len(TRIPLES):
                        weights(q + 1)
                    if q + 2 < len(TRIPLES):
                        maxima(q + 2)
                dve.wait_ge(dil_out, 16 * i + 16)
                dp.wait(dve, f"pv{len(TRIPLES) - 1}2", i)
                for g in range(3):
                    dd.done(V.tensor_copy(od[:, g], bank[5 + g][:]), f"od{g}")

            dd.wait_iterations(dve, DIL_S)
            dve.wait_ge(dil_out, 16 * DIL_S + 16)
            dp.wait(dve, f"pv{len(TRIPLES) - 1}2", DIL_S - 1)
            for d in range(2):
                V.memset(hlf[:, d, :, 0:1], 0.0).then_inc(pads_zero, 1)
            V.memset(hst, 0.0).then_inc(pads_zero, 1)
            with dve.Fori(0, HG) as i:
                hd.done(V.tensor_copy(hpar, lbt[:, i]), "par")
                for d in range(2):
                    dve.wait_ge(acc_free, i * N_H + (C_H + 2 + d + 3))
                    hd.wait(dve, "par", i)
                    hd.done(V.tensor_scalar(hf[:, d], hf[:, d], hpar[:, 2 * d + 1:2 * d + 2], hpar[:, 2 * d:2 * d + 1],
                                            ALU.mult, ALU.add), f"f{d}")
                for d in range(2):
                    hd.wait(dve, f"f{d}", i)
                    hd.done(V.tensor_scalar(hk[:, d], hf[:, d], -1.0, 1.0, ALU.mult, ALU.add), f"k{d}")
                hd.wait(dve, "k1", i)
                hd.done(V.tensor_tensor(hksum, hk[:, 0], hk[:, 1], ALU.add), "ks")
                hp.wait(dve, "vt", i)
                hd.done(V.tensor_copy(hvn, bank[2][:].rearrange("p (a b) -> p a b", a=TT)), "vn")
                for d in range(2):
                    ha.wait(dve, f"ln{d}", i)
                    hd.done(V.tensor_tensor_scan(hb[:, d].rearrange("p a b -> p (a b)"), scan_ones,
                                                 hlf[:, d].rearrange("p a b -> p (a b)"), 0.0, ALU.mult, ALU.add),
                            f"sc{d}")
                hd.wait(dve, "sc1", i)

                def level_diff(l):
                    L = LEVELS[l]
                    for d in range(2):
                        b = hb[:, d, :, 1 - d:P + 1 - d].rearrange("p a (m c) -> p a m c", c=2 * L)
                        ref = hb[:, d, :, L:P:2 * L] if 2 * L < P else hb[:, d, :, L:L + 1]
                        if l:
                            ha.wait(dve, f"eo{l - 1}", i)
                        o = ht[:, d].rearrange("p (a m c) -> p a m c", a=TT, c=2 * L)
                        hd.done(V.tensor_tensor(o, b, ref.unsqueeze(3).broadcast_to([P, TT, P // (2 * L), 2 * L]),
                                                ALU.subtract), f"t{l}{d}")

                level_diff(0)
                hp.wait(dve, "p0", i)
                hd.done(V.tensor_copy(ham, bank[3][:].rearrange("p (a b) -> p a b", a=TT)), "a0")

                def keep_level(l):
                    hp.wait(dve, f"pl{l}", i)
                    pause(hd, f"cp{l - 1}" if l else "a0", f"wait{l}", i)
                    hd.done(V.copy_predicated(ham, lmask[:, l:l + 1, :].broadcast_to([P, TT, P]),
                                              bank[4 + l % 2][:].rearrange("p (a b) -> p a b", a=TT)), f"cp{l}")

                for l in range(7):
                    L = LEVELS[l]
                    if l < 6:
                        level_diff(l + 1)
                    ha.wait(dve, f"eo{l}", i)
                    if l >= 2:
                        hp.wait(dve, f"pl{l - 2}", i)

                    def half(ap, odd):
                        return ap.rearrange("p (m c) -> p m c", c=2 * L)[:, :, L * odd:L * odd + L]

                    b = l % 2
                    hd.done(V.tensor_tensor(half(hql[:, b], 1), half(hq, 1), half(he[:, 0], 1), ALU.mult), f"qo{l}")
                    hd.done(V.tensor_tensor(half(hql[:, b], 0), half(hq, 0), half(he[:, 1], 0), ALU.mult), f"qe{l}")
                    hd.done(V.tensor_tensor(half(hkl[:, b], 0), half(hk[:, 0], 0), half(he[:, 0], 0), ALU.mult), f"ke{l}")
                    hd.done(V.tensor_tensor(half(hkl[:, b], 1), half(hk[:, 1], 1), half(he[:, 1], 1), ALU.mult), f"ko{l}")
                    if l:
                        keep_level(l - 1)
                for d in range(2):
                    ha.wait(dve, "eo6", i)
                    hd.done(V.tensor_tensor(ht[:, d].rearrange("p (a b) -> p a b", a=TT),
                                            hb[:, d, :, 1 - d:P + 1 - d],
                                            hb[:, d, :, P:P + 1].broadcast_to([P, TT, P]), ALU.subtract), f"ts{d}")
                keep_level(6)
                for d in range(2):
                    ha.wait(dve, f"x2{d}", i)
                    hd.done(V.tensor_tensor(hqs[:, d], hq, he[:, d], ALU.mult), f"qs{d}")
                    hd.done(V.tensor_tensor(hkst[:, d], hk[:, d], he[:, 1 - d], ALU.mult), f"ks{d}")
                for d in range(2):
                    hp.wait(dve, f"kt{d}", i)
                    hd.done(V.tensor_copy(hkn[:, d], bank[4 + d][:, 0:3 * P].rearrange("p (a b) -> p a b", a=3)),
                            f"et{d}")
                hp.wait(dve, "u1", i)
                uf, ub = bank[6], bank[7]
                hd.done(V.tensor_copy(hst[:, 0, 0], uf[:, 0:P]), "sf1")
                hd.done(V.tensor_copy(hst[:, 1, 2], ub[:, 2 * P:3 * P]), "sb2")
                hd.wait(dve, "sb2", i)
                hd.done(V.scalar_tensor_tensor(hst[:, 0, 1], hst[:, 0, 0], hdec[:, 0, 1:2], uf[:, P:2 * P],
                                               ALU.mult, ALU.add), "sf2")
                hd.done(V.scalar_tensor_tensor(hst[:, 1, 1], hst[:, 1, 2], hdec[:, 1, 2:3], ub[:, P:2 * P],
                                               ALU.mult, ALU.add), "sb1")
                hd.wait(dve, "sb1", i)
                hd.done(V.scalar_tensor_tensor(hst[:, 0, 2], hst[:, 0, 1], hdec[:, 0, 2:3], uf[:, 2 * P:3 * P],
                                               ALU.mult, ALU.add), "sf3")
                hd.done(V.scalar_tensor_tensor(hst[:, 1, 0], hst[:, 1, 1], hdec[:, 1, 1:2], ub[:, 0:P],
                                               ALU.mult, ALU.add), "sb0")
                hd.done(V.tensor_tensor(hsg, hsg, hgt, ALU.mult), "silu")
                hp.wait(dve, "nm", i)
                hd.done(V.tensor_scalar(hr, bank[3][:], 1.0 / P, EPS, ALU.mult, ALU.add), "ms")
                ha.wait(dve, "sqrt", i)
                hd.done(V.reciprocal(hr, hr), "rcp")
                hd.wait(dve, "rcp", i)
                dve.wait_ge(hg_out, 16 * i + 16)
                hd.done(V.scalar_tensor_tensor(hres, bank[2][:], prm[:, P_HG:P_HG + 1], hr, ALU.mult, ALU.mult), "o1")
                hd.wait(dve, "o1", i)
                hd.done(V.tensor_tensor(hres, hres, hsg, ALU.mult), "o2")

            dve.sem_inc(up.sem, 2 * len(UP))
            for k in range(KT):
                dve.wait_ge(mix_hi, k + 1)
                V.tensor_tensor(xlo[:, k], early(k) if k < HT else late[:, k - HT], xhi[:, k], ALU.subtract)\
                    .then_inc(mix_lo, 1)
            dve.wait_ge(mix_lo, KT)
            dve.wait_ge(hg_out, 16 * HG + 16)
            bg_v = prm[:, P_BG:P_BG + N_GATE].rearrange("p (b j) -> p b j", b=3)
            with dve.Fori(0, KT // 2) as i:
                for u in range(2):
                    j = 2 * i + u
                    dve.wait_ge(gates_made, 6 * i + 3 * u + 1)
                    up.done(V.tensor_copy(bgc[:, u], bg_v[:, :, 2 * i + u]), "bg")
                    dve.wait_ge(gates_made, 6 * i + (3 * u + 3) + 1)
                    bk = bank[3 * u:3 * u + 3]
                    dve.wait_ge(half_done, 4 * i + (2 * C_UP + 2 * u + 1))
                    up.done(V.tensor_tensor(merged[:, 2 * i + u], gt[:, u, 1], bk[1][:], ALU.mult), "m1")
                    dve.wait_ge(half_done, 4 * i + (2 * C_UP + 2 * u + 2))
                    up.done(V.tensor_tensor(umul[:, 0], gt[:, u, 0], bk[0][:], ALU.mult), "m2")
                    up.done(V.tensor_tensor(umul[:, 1], gt[:, u, 2], bk[2][:], ALU.mult), "m3")
                    up.wait(dve, "m2", j)
                    up.done(V.tensor_tensor(merged[:, 2 * i + u], merged[:, 2 * i + u], umul[:, 0], ALU.add), "a1")
                    up.wait(dve, "a1", j)
                    up.done(V.tensor_tensor(merged[:, 2 * i + u], merged[:, 2 * i + u], umul[:, 1], ALU.add), "a2")

            up.wait(dve, "a2", KT - 1)
            V.memset(nrm, 0.0).then_inc(summed[2], 1)
            for k in range(KT):
                dve.wait_ge(merged_hi, k + 1)
                V.tensor_tensor(xlo[:, k], merged[:, k], xhi[:, k], ALU.subtract).then_inc(merged_lo, 1)
            with dve.Fori(0, KT // 2) as i:
                for u in range(2):
                    dve.wait_ge(xres_in[u], 16 * i + 16)
                    dve.wait_ge(half_done, 4 * i + (2 * C_OUT + 2 * u + 2))
                    dve.wait_ge(merged_lo, KT)
                    V.tensor_tensor(y[:, 2 * i + u], xres[:, u], acc[u][:], ALU.add).then_inc(out_read, 1)
                    dve.wait_ge(squared[2], 2 * i + (u + 1))
                    dve.wait_ge(summed[2], 2 * i + (u + 1))
                    V.tensor_tensor(nrm, nrm, nsq[:, u], ALU.add).then_inc(summed[2], 1)
            dve.wait_ge(out_read, KT + 2)
            dve.wait_ge(residual_out, 16 * KT)
            norm_rest(2, y, T, P_FFN, xhi, xlo)

            with dve.Fori(0, PH) as i:
                dve.wait_ge(score_saved, 2 * i + 2 + 1)
                tk.wait_iterations(dve, i)
                pairs = [(x, p) for x in range(TT) for p in range(2)]
                tk.done(V.tensor_copy(sw, scores[:, :, bass.ds(2 * i, 2), :]), "cp")
                pause(tk, "cp", "wait0", i)
                for x, p in pairs:
                    tk.done(V.max(v16[:, x, p, 0:8], sw[:, x, p]), f"ma{x}{p}")
                pause(tk, "ma31", "wait1", i)
                for x, p in pairs:
                    tk.done(V.max_index(i16[:, x, p, 0:8], v16[:, x, p, 0:8], sw[:, x, p]), f"ia{x}{p}")
                for x, p in pairs:
                    tk.done(V.match_replace(sw2[:, x, p], v16[:, x, p, 0:8], sw[:, x, p], NEG), f"mr{x}{p}")
                pause(tk, "mr31", "wait2", i)
                for x, p in pairs:
                    tk.done(V.max(v16[:, x, p, 8:16], sw2[:, x, p]), f"mb{x}{p}")
                pause(tk, "mb31", "wait3", i)
                for x, p in pairs:
                    tk.done(V.max_index(i16[:, x, p, 8:16], v16[:, x, p, 8:16], sw2[:, x, p]), f"ib{x}{p}")
                tk.wait(dve, "ib31", i)
                tk.done(V.tensor_copy(i16f, i16), "if")
                tk.done(V.tensor_tensor(cand, v16[:, :, 0].unsqueeze(3).broadcast_to([P, TT, TOPK, TOPK]),
                                        v16[:, :, 1].unsqueeze(2).broadcast_to([P, TT, TOPK, TOPK]), ALU.add), "cand")
                pause(tk, "cand", "wait4", i)
                cf = cand.rearrange("p a b c -> p a (b c)")
                cf2 = cand2.rearrange("p a b c -> p a (b c)")
                for x in range(TT):
                    tk.done(V.max(best[:, x, 0:8], cf[:, x]), f"Ma{x}")
                pause(tk, "Ma3", "wait5", i)
                for x in range(TT):
                    tk.done(V.max_index(pos[:, x, 0:8], best[:, x, 0:8], cf[:, x]), f"Ia{x}")
                for x in range(TT):
                    tk.done(V.match_replace(cf2[:, x], best[:, x, 0:8], cf[:, x], NEG), f"Mr{x}")
                pause(tk, "Mr3", "wait6", i)
                for x in range(TT):
                    tk.done(V.max(best[:, x, 8:16], cf2[:, x]), f"Mb{x}")
                pause(tk, "Mb3", "wait7", i)
                for x in range(TT):
                    tk.done(V.max_index(pos[:, x, 8:16], best[:, x, 8:16], cf2[:, x]), f"Ib{x}")
                tk.done(V.tensor_tensor(sel[:, 2, :, bass.ds(TOPK * i, TOPK)], best,
                                        best[:, :, 0:1].broadcast_to([P, TT, TOPK]), ALU.subtract), "sub")
                tk.wait(dve, "Ib3", i)
                tk.done(V.tensor_scalar(phi, pos, 4, None, ALU.logical_shift_right), "hi")
                tk.done(V.tensor_scalar(plo, pos, 15, None, ALU.bitwise_and), "lo")
                tk.wait(dve, "lo", i)
                tk.done(V.tensor_copy(phif, phi), "hif")
                tk.done(V.tensor_copy(plof, plo), "lof")
                for p, f in ((0, phif), (1, plof)):
                    tk.wait(dve, "lof", i)
                    tk.done(V.tensor_tensor(
                        eq.rearrange("p a b c -> p (a b) c"), f.rearrange("p a b -> p (a b)").unsqueeze(2).broadcast_to([P, TT * TOPK, TOPK]),
                        iota16.unsqueeze(1).broadcast_to([P, TT * TOPK, TOPK]), ALU.is_equal), f"eq{p}")
                    tk.wait(dve, f"eq{p}", i)
                    tk.done(V.tensor_tensor(eq2, eq, i16f[:, :, p].unsqueeze(2).broadcast_to([P, TT, TOPK, TOPK]),
                                            ALU.mult), f"pr{p}")
                    tk.wait(dve, f"pr{p}", i)
                    tk.done(V.reduce_sum(sel[:, p, :, bass.ds(TOPK * i, TOPK)], eq2, AX_X), f"out{p}")
            dve.wait_ge(gate_exp, 1)
            e = sel[:, 2].rearrange("p a (h k) -> p (a h) k", k=TOPK)
            V.reduce_sum(bsum, e, AX_X).then_inc(gate_soft, 1)
            dve.wait_ge(gate_soft, 1)
            V.reciprocal(brcp, bsum).then_inc(gate_soft, 1)
            dve.wait_ge(gate_soft, 2)
            V.tensor_tensor(e, e, brcp.unsqueeze(2).broadcast_to([P, TT * PH, TOPK]), ALU.mult).then_inc(gate_soft, 1)
            dve.wait_ge(sel_turned, 3)
            V.tensor_copy(iit, bank[4][:]).then_inc(sel_saved, 1)
            V.tensor_copy(jjt, bank[5][:]).then_inc(sel_saved, 1)
            V.tensor_copy(gtt, bank[6][:]).then_inc(sel_saved, 1)
            dve.wait_ge(sel_saved, 3)
            V.tensor_copy(ghi, gtt).then_inc(sel_saved, 1)
            dve.wait_ge(sel_saved, 4)
            V.tensor_tensor(glo, gtt, ghi, ALU.subtract).then_inc(sel_saved, 1)
            dve.wait_ge(sel_saved, 5)

            def save_products(i, q):
                b = q // 8
                dve.wait_ge(gmat_hi, 16 * i + (q + 1))
                for x in range(2):
                    pair = bank[2 + 2 * (q % 2) + x][:].rearrange("p (t h j) -> p t h j", t=2, h=2)
                    t0 = 4 * (q % 8) + 2 * x
                    o = gstage[:, b, :, t0:t0 + 2].rearrange("p j t -> p t j")
                    last = V.tensor_tensor(o, o, pair[:, :, 1], ALU.add)
                last.then_inc(gmat_saved, 1)

            with dve.Fori(0, NTB // 2) as i:
                for b in range(2):
                    for k, s in enumerate((iit, jjt, early_a[:, 0], early_a[:, 1])):
                        dve.wait_ge(onehots, 16 * i + 8 * b + 1)
                        V.tensor_copy(cur[:, k], s[:, bass.ds((2 * TB) * i + TB * b, TB)]).then_inc(block_cols, 1)
                    dve.wait_ge(block_cols, 8 * i + (4 * b + 4))
                    for g in range(8):
                        q = 8 * b + g
                        dve.wait_ge(gmat_done, 16 * i + max(q - 1, 0) + 1)
                        for x in range(4):
                            t, slot = 4 * g + x, 4 * (q % 2) + x
                            V.tensor_scalar(oh_i[:, slot], iota, cur[:, 0, t:t + 1], None, ALU.is_equal)
                            for h in range(2):
                                last = V.tensor_scalar(oh_j[:, slot, h], iota, cur[:, 1, t:t + 1],
                                                       cur[:, 2 + h, t:t + 1], ALU.is_equal, ALU.mult)
                        last.then_inc(onehots, 1)
                        if q >= 2:
                            save_products(i, q - 2)
                save_products(i, 14)
                save_products(i, 15)

            def product(s, k):
                dve.wait_ge(gmat_in[k // 4], 16 * s + 16)
                dve.wait_ge(gelu_in[k % 4], 32 * s + 16 * (k // 4 + 1))
                if not (isinstance(s, int) and s == 0 and k < 2):
                    dve.wait_ge(hid_lo, 8 * s + (k - 1))
                g4 = gsb[:, k // 4].rearrange("p b (j t) -> p b j t", j=4)
                V.tensor_tensor(htmp[:, k % 2].rearrange("p (b t) -> p b t", b=NTB),
                                agb[:, k % 4].rearrange("p (b t) -> p b t", b=NTB), g4[:, :, k % 4], ALU.mult)\
                    .then_inc(hid_product, 1)

            def low_part(s, k, half):
                dve.wait_ge(hid_hi, 8 * s + (k + 1))
                V.tensor_tensor(xlo[:, 8 * half + k], htmp[:, k % 2], xhi[:, 8 * half + k], ALU.subtract)\
                    .then_inc(hid_lo, 1)

            product(0, 0)
            product(0, 1)
            dve.wait_ge(half_done, 2 * C_V - 1)
            for k in range(8):
                low_part(0, k, 0)
                if k < 6:
                    product(0, k + 2)
            dve.wait_ge(residual_in, 16)

            def sub_block_add(s, par, prepare):
                last = isinstance(s, int) and s == 15
                for x in range(KT):
                    if prepare and x in PREPARED_AT:
                        product(s + 1, PREPARED_AT.index(x))
                    dve.wait_ge(half_done, KT * s + (2 * C_V + x + 1))
                    if not (isinstance(s, int) and s == 0):
                        dve.wait_ge(y_added, KT * s + (x + 1 - KT))
                    V.tensor_tensor(y[:, x], y[:, x], acc[x % 2][:], ALU.add).then_inc(y_added, 1)
                    if prepare and x - 1 in PREPARED_AT:
                        low_part(s + 1, PREPARED_AT.index(x - 1), 1 - par)
                    if last:
                        sum_tile(3, x, T)

            sub_block_add(0, 0, True)
            sub_block_add(1, 1, True)
            with dve.Fori(1, 7) as i:
                for par in range(2):
                    sub_block_add(2 * i + par, par, True)
            sub_block_add(14, 0, True)
            sub_block_add(15, 1, False)
            norm_rest(3, y, T, P_FIN)

        @block.tensor
        def _(pe):
            M = nc.tensor

            def half(m, s, out, tiles, k0, first, last, his=xhi, los=xlo, ready=None):
                pe.wait_ge(w_lo_made, m + 1)
                for k in tiles:
                    if ready is not None:
                        ready(k0 + k)
                    h, l = his[:, k0 + k], los[:, k0 + k]
                    f, e = first and k == tiles[0], last and k == tiles[-1]
                    M.matmul(out, whi[s][:, k], h, start=f, stop=False)
                    M.matmul(out, whi[s][:, k], l, start=False, stop=False)
                    ins = M.matmul(out, wlo[s][:, k], h, start=False, stop=e)
                return ins

            def chunk_half(n, i, per, x, width=T, **operands):
                s = (2 * n + x) % 4
                half(i * (2 * per) + (2 * n + x), s, acc[n % 2][:, 0:width], list(range(8)), 8 * x, x == 0, x == 1,
                     **operands).then_inc(half_done, 1)

            def take_acc(n, i, per):
                pe.wait_ge(acc_free, i * per + (n + 1))

            def take_acc2(n, i, per):
                pe.wait_ge(acc2_free, i * per + (n - C_PQ + 1))

            def column_sum(r, width, steps):
                pe.wait_ge(summed[r], steps)
                for tt in range(width // P):
                    ins = M.matmul(bank[7 - r % 2][:, tt:tt + 1], nrm[:, P * tt:P * tt + P], ones[:, 0:1],
                                   start=True, stop=True)
                ins.then_inc(column_sums, 1)

            def spread(r, width):
                norm[r][1].wait(pe, "diag")
                M.matmul(bank[7 - r % 2][:, 0:width], ones, nrm[:, 0:width], start=True, stop=True)\
                    .then_inc(column_sums, 1)

            def chunk(n, i, per, ready=None):
                for x in range(2):
                    chunk_half(n, i, per, x, ready=ready)

            def tiles_split(r):
                return lambda k: (odd_low[r] if r in odd_low and k % 2 else norm[r][1]).wait(pe, f"lo{k}")

            pe.sem_inc(gmat_done, 1)
            pe.wait_ge(consts_in, 32)
            column_sum(0, MEM, KT)
            spread(0, MEM)
            for c in range(N_KV):
                take_acc(c, 0, 2)
                for x in range(2):
                    chunk_half(c, 0, 2, x, MEM, his=mhi, los=mlo, ready=tiles_split(0) if c == 0 else None)
                    if c == 5 and x == 0:
                        spread(1, T)
                if c == 4:
                    column_sum(1, T, KT)
            for c in range(N_MQ):
                take_acc(C_MQ + c, 0, 2)
                chunk(C_MQ + c, 0, 2, tiles_split(1) if c == 0 else None)

            pe.wait_ge(acc_free, C_MG + 2)
            for h in range(MH):
                if h >= 2:
                    md.wait(pe, f"vm{h - 2}")
                for m in range(MT):
                    ins = M.transpose(bank[4 + h % 2][:, P * m:P * m + P], kvm[:, MH + h, P * m:P * m + P], ident)
                mp.done(ins, f"vt{h}")

            units = [(h, tt) for h in range(MH) for tt in range(TT)]

            def mem_scores(k):
                h, tt = units[k]
                if k >= 2:
                    ma.wait(pe, f"ex{units[k - 2][0]}{units[k - 2][1]}")
                mp.done(M.matmul(bank[2 + k % 2][:, 0:MEM], qm[:, h, P * tt:P * tt + P], kvm[:, h],
                                 start=True, stop=True), f"sc{h}{tt}")

            def mem_output(k):
                h, tt = units[k]
                md.wait(pe, f"ev{h}{tt}")
                if tt == 0 and h >= 2:
                    md.wait(pe, f"ov{h - 2}")
                for m in range(MT):
                    ins = M.matmul(bank[6 + h % 2][:, P * tt:P * tt + P], vm[:, m, h], ptm[:, k % 2, m],
                                   start=(m == 0), stop=(m == MT - 1))
                mp.done(ins, f"pv{h}{tt}")

            mem_scores(0)
            mem_scores(1)
            for k, (h, tt) in enumerate(units):
                u = k % 2
                if k % 2 == 0 and k // 2 < 2 * N_MEM_GATES:
                    n, x = C_MG + k // 4, (k // 2) % 2
                    if x == 0:
                        take_acc(n, 0, 2)
                    chunk_half(n, 0, 2, x)
                md.wait(pe, f"sp{h}{tt}")
                if k < 2:
                    md.wait(pe, f"vm{MH - 1}")
                for m in range(MT):
                    ins = M.transpose(bank[4 + u][:, P * m:P * m + P], pm[:, u, P * m:P * m + P], ident)
                mp.done(ins, f"pt{h}{tt}")
                if k:
                    mem_output(k - 1)
                if k + 2 < len(units):
                    mem_scores(k + 2)
            mem_output(len(units) - 1)

            with pe.Fori(0, DIL_S) as i:
                for c in range(N_DIL):
                    take_acc(C_D + c, i, N_D)
                    for x in range(2):
                        chunk_half(C_D + c, i, N_D, x)
                pe.wait_ge(acc_free, i * N_D + (C_D + N_DIL + 2))
                dd.wait_iterations(pe, i)
                md.wait(pe, f"ov{MH - 1}")
                pe.wait_ge(pads_zero, 1)
                for g in range(3):
                    for st in range(TT):
                        ins = M.transpose(bank[2 + g][:, P * st:P * st + P], qkv[:, 2, g, P * st:P * st + P], ident)
                    dp.done(ins, f"vt{g}")

                def scores_of(q, after):
                    tt, a_ = TRIPLES[q]
                    r = slice(64 * a_, 64 * a_ + 64)
                    for g in range(3):
                        lo, hi = (P * v for v in key_tiles(g, tt))
                        steps = da if g and after.startswith("ev") else dd
                        steps.wait(pe, f"{after}{g}" + ("1" if q == 0 else ""), i)
                        dp.done(M.matmul(bank[2 + g][:, lo:hi], qkv[r, 0, g, P * tt:P * tt + P], qkv[r, 1, g, lo:hi],
                                         start=True, stop=True), f"sc{q}{g}")

                scores_of(0, "vp")
                scores_of(1, "sm0")
                for q, (tt, a_) in enumerate(TRIPLES):
                    if q < 2 * N_DIL_GATES:
                        n = C_D + N_DIL + q // 2
                        if q % 2 == 0:
                            take_acc(n, i, N_D)
                        chunk_half(n, i, N_D, q % 2)
                    for g in range(3):
                        if q + 1 < len(TRIPLES):
                            dd.wait(pe, f"sm{q + 1}{g}", i)
                        dd.wait(pe, f"sp{q}{g}", i)
                        for st in range(*key_tiles(g, tt)):
                            ins = M.transpose(bank[2 + g][:, P * st:P * st + P], pd[:, q % 2, g, P * st:P * st + P],
                                              ident)
                        dp.done(ins, f"pt{q}{g}")
                    if q + 2 < len(TRIPLES):
                        scores_of(q + 2, f"ev{q}")
                    for g in range(3):
                        lo, hi = key_tiles(g, tt)
                        (da if g else dd).wait(pe, f"ev{q}{g}", i)
                        for st in range(lo, hi):
                            ins = M.matmul(bank[5 + g][:, P * tt:P * tt + P], vp[:, g, a_, st], ptd[:, g, st],
                                           start=(a_ == 0 and st == lo), stop=(a_ == 1 and st == hi - 1))
                        dp.done(ins, f"pv{q}{g}")

            dd.wait_iterations(pe, DIL_S)
            with pe.Fori(0, HG) as i:
                for c in range(N_HGC):
                    take_acc(C_H + c, i, N_H)
                    for x in range(2):
                        chunk_half(C_H + c, i, N_H, x)

                def per_tile(out, lhs, rhs, name):
                    for tt in range(TT):
                        ins = M.matmul(out[:, P * tt:P * tt + P], lhs[:, P * tt:P * tt + P],
                                       rhs[:, P * tt:P * tt + P], start=True, stop=True)
                    hp.done(ins, name)

                for x in range(2 * N_HG_GATES):
                    n = C_H + N_HGC + x // 2
                    if x % 2 == 0:
                        take_acc(n, i, N_H)
                    chunk_half(n, i, N_H, x % 2)
                    if x == 0:
                        hd.wait_iterations(pe, i)
                        for tt in range(TT):
                            ins = M.transpose(bank[2][:, P * tt:P * tt + P], hv[:, P * tt:P * tt + P], ident)
                        hp.done(ins, "vt")
                    if x == 1:
                        hd.wait(pe, "ks", i)
                        per_tile(bank[3], hksum, hq, "p0")
                    l = x - 3
                    if 0 <= l < 7:
                        hd.wait(pe, f"ko{l}", i)
                        if l >= 2:
                            hd.wait(pe, f"cp{l - 2}", i)
                        per_tile(bank[4 + l % 2], hkl[:, l % 2], hql[:, l % 2], f"pl{l}")
                    if x == 10:
                        for d in range(2):
                            hd.wait(pe, f"ks{d}", i)
                            for k in range(3):
                                t0 = P * (k + d)
                                ins = M.transpose(bank[4 + d][:, P * k:P * k + P], hkst[:, d, t0:t0 + P], ident)
                            hp.done(ins, f"kt{d}")
                    if x == 11:
                        for d in range(2):
                            hd.wait(pe, f"et{d}", i)
                            for k in range(3):
                                ins = M.matmul(bank[6 + d][:, P * k:P * k + P], hkn[:, d, k], hvn[:, k + d],
                                               start=True, stop=True)
                            hp.done(ins, f"u{d}")
                    if x == 12:
                        hd.wait(pe, "sb0", i)
                        for tt in range(TT):
                            o = bank[2][:, P * tt:P * tt + P]
                            cols = slice(P * tt, P * tt + P)
                            if tt:
                                M.matmul(o, hst[:, 0, tt - 1], hqs[:, 0, cols], start=True, stop=False)
                            if tt < TT - 1:
                                M.matmul(o, hst[:, 1, tt], hqs[:, 1, cols], start=(tt == 0), stop=False)
                            ins = M.matmul(o, hvn[:, tt], ham[:, tt], start=False, stop=True)
                        hp.done(ins, "o")
                    if x == 13:
                        ha.wait(pe, "sq", i)
                        hp.done(M.matmul(bank[3][:], ones, hosq, start=True, stop=True), "nm")

            pe.wait_ge(acc_free, C_UP + 2)
            hd.wait_iterations(pe, HG)
            def merge_products(u, i, first=False):
                up.wait(pe, "m3", 2 * i + (u - 2))
                bk = [b[:] for b in bank[3 * u:3 * u + 3]]
                m = 4 * i + (2 * C_UP + 2 * u)
                ready = (lambda k: pe.wait_ge(mix_lo, k + 1)) if first else None
                half(m, 2 * u, bk[1], range(HG), 0, True, True, ready=ready)
                half(m, 2 * u, bk[2], range(HG, HT), 0, True, False, ready=ready).then_inc(half_done, 1)
                half(m + 1, 2 * u + 1, bk[2], range(2), HT, False, True, ready=ready)
                half(m + 1, 2 * u + 1, bk[0], range(2, HT), HT, True, True, ready=ready).then_inc(half_done, 1)

            merge_products(0, 0, True)
            merge_products(1, 0)
            with pe.Fori(1, KT // 2) as i:
                for u in range(2):
                    merge_products(u, i)

            up.wait(pe, "m3", KT - 2)
            def out_chunk(u, i, first=False):
                if first:
                    ready = lambda k: pe.wait_ge(merged_lo, k + 1)
                else:
                    ready = None
                    pe.wait_ge(out_read, 2 * i + (u + 1))
                chunk(C_OUT + u, i, 2, ready)

            out_chunk(0, 0, True)
            out_chunk(1, 0)
            with pe.Fori(1, KT // 2) as i:
                for u in range(2):
                    out_chunk(u, i)
            column_sum(2, T, KT + 1)
            spread(2, T)

            pe.wait_ge(sub_keys_in, 16)
            def scores_of(u, i):
                pe.wait_ge(acc2_free, 2 * i + (u + 3))
                if u or not isinstance(i, int):
                    pe.wait_ge(score_saved, 2 * i + u)
                for tt in range(TT):
                    ins = M.matmul(bank[2 + u][:, P * tt:P * tt + P], qpt[:, u, P * tt:P * tt + P], skt[:, u],
                                   start=True, stop=True)
                ins.then_inc(score_done, 1)

            def query_pair(i, first):
                for u in range(2):
                    take_acc2(C_PQ + u, i, 2)
                    for x in range(2):
                        chunk_half(C_PQ + u, i, 2, x, ready=tiles_split(2) if first and u == 0 else None)
                        if x == 0 and u == 1:
                            scores_of(0, i)
                        elif x == 0 and not first:
                            scores_of(1, i - 1)

            query_pair(0, True)
            with pe.Fori(1, PH) as i:
                query_pair(i, False)

            def expert_chunks(first, count):
                with pe.Fori(0, count // 2) as i:
                    for u in range(2):
                        n = C_U + first + u
                        take_acc2(n, i, 2)
                        for x in range(2):
                            chunk_half(n, i, 2, x)

            take_acc2(C_U, 0, 2)
            for x in range(2):
                chunk_half(C_U, 0, 2, x)
                if x == 0:
                    scores_of(1, PH - 1)
            take_acc2(C_U + 1, 0, 2)
            chunk(C_U + 1, 0, 2)
            expert_chunks(2, U_1 - 2)
            expert_chunks(U_1, U_2)
            pe.wait_ge(gate_soft, 3)
            for k in range(3):
                for tt in range(TT):
                    ins = M.transpose(bank[4 + k][:, P * tt:P * tt + P], sel[:, k, tt], ident)
                ins.then_inc(sel_turned, 1)
            expert_chunks(U_1 + U_2, U_3)
            first = U_1 + U_2 + U_3
            with pe.Fori(0, NTB // 2) as i:
                for c in range(8):
                    n = C_U + first + c
                    take_acc2(n, i, 8)
                    for x in range(2):
                        chunk_half(n, i, 8, x)
                        q = 2 * c + x
                        pe.wait_ge(onehots, 16 * i + (q + 1) + 1)
                        pe.wait_ge(gmat_saved, 16 * i + max(q, 1))
                        for k in range(4):
                            o = bank[2 + 2 * (q % 2) + k // 2][:, 2 * P * (k % 2):2 * P * (k % 2) + 2 * P]
                            slot = 4 * (q % 2) + k
                            ins = M.matmul(o, oh_i[:, slot], oh_j[:, slot].rearrange("p h j -> p (h j)"),
                                           start=True, stop=True)
                        ins.then_inc(gmat_done, 1)
            expert_chunks(first + U_B, U_C)

            pe.wait_ge(acc2_free, 2 * PH + NK + 2)

            def sub_block_products(s, par):
                first = isinstance(s, int) and s == 0
                for x in range(KT):
                    if not (first and x < 2):
                        pe.wait_ge(y_added, KT * s + (x - 1))
                    if not first:
                        pe.wait_ge(hid_lo, 8 * s + 8)
                    m = KT * s + (2 * C_V + x)
                    half(m, (2 * C_V + x) % 4, acc[x % 2][:], list(range(8)), 8 * par, True, True,
                         ready=(lambda k: pe.wait_ge(hid_lo, k + 1)) if first and x == 0 else None)\
                        .then_inc(half_done, 1)

            sub_block_products(0, 0)
            sub_block_products(1, 1)
            with pe.Fori(1, 8) as i:
                for par in range(2):
                    sub_block_products(2 * i + par, par)
            column_sum(3, T, KT)
            spread(3, T)


def _constants():
    import numpy as np

    c = np.zeros((P, NCONST), np.float32)
    c[:, C_ID:C_ID + P] = np.eye(P)
    c[:, C_ONE:C_ONE + P] = 1
    gap = np.arange(DMW)[None, :] - 3 * P - np.arange(P)[:, None]
    for g, dil in enumerate(DILATIONS):
        ok = (gap % dil == 0) & (np.abs(gap) <= REACH * dil)
        c[:, C_DM + g * DMW:C_DM + (g + 1) * DMW] = np.where(ok, np.abs(gap), 1e32)
    s = np.ones((TT, P + 1))
    s[:, 0] = 0
    c[:, C_SCAN:C_SCAN + TT * (P + 1)] = s.reshape(-1)
    c[:, C_IOTA:C_IOTA + P] = np.arange(P)
    c[:, C_IO16:C_IO16 + TOPK] = np.arange(TOPK)
    heads = np.arange(12).reshape(3, 2, 2).transpose(1, 0, 2).reshape(-1)
    c[:, C_SL:C_SL + 12] = -np.exp2(-8.0 * (heads + 1) / 12)
    k = np.arange(P)
    m = np.zeros((P, 7, P), np.int32)
    for l, L in enumerate(LEVELS):
        blk, odd = k // (2 * L), (k // L) % 2
        m[:, l] = (blk[:, None] == blk[None, :]) & (odd[:, None] != odd[None, :])
    return c, m


def kernel(**inputs):
    import numpy as np
    import concourse.bacc as bacc
    from concourse import mybir as _mybir
    from concourse.bass_utils import run_bass_kernel_spmd

    a = {k: np.asarray(v) for k, v in inputs.items()}

    def cols(v):
        return v.reshape(-1, P).T

    def rows(v):
        return np.ascontiguousarray(v.T.reshape(KT, P, -1).transpose(1, 0, 2))

    def halves(w):
        n = w.shape[1] // P
        return np.ascontiguousarray(w.reshape(2, HT, P, n, P).transpose(3, 0, 2, 1, 4)).reshape(2 * n, P, HT, P)

    w_in = a["w_in"][0]
    hg = w_in[:, :5 * HG * P].reshape(D, 5, HG, P)
    dil = w_in[:, 5 * HG * P:5 * HG * P + 18 * P].reshape(D, 3, 3, 2, P)
    mq = w_in[:, 5 * HG * P + 18 * P:5 * HG * P + 18 * P + MH * P]
    gates = w_in[:, 5 * HG * P + 18 * P + MH * P:].reshape(D, N_GATE, P)
    g = N_MEM_GATES
    order = [mq, gates[:, :g].reshape(D, -1)]
    for s in range(DIL_S):
        order += [dil[:, :, :, s].reshape(D, -1), gates[:, g:g + N_DIL_GATES].reshape(D, -1)]
        g += N_DIL_GATES
    for h in range(HG):
        order += [hg[:, :, h].reshape(D, -1), gates[:, g:g + N_HG_GATES].reshape(D, -1)]
        g += N_HG_GATES
    w_in = halves(np.concatenate(order, 1))

    u = a["peer_u"][0].reshape(P, NK, 2, HT, P).transpose(1, 2, 4, 3, 0)
    v = a["peer_v"][0].reshape(P, NK // 8, 8, KT, P).transpose(1, 3, 0, 2, 4)
    const, mask = _constants()
    prm = np.concatenate([cols(a["g_mix"][0]), cols(a["g_mem"][0]), cols(a["g_ffn"][0]), cols(a["g_final"]),
                          cols(a["b_gate"][0])]
                         + [cols(a[n][l]) for n in ("lb_fwd_logits", "lb_bwd_logits") for l in range(2)]
                         + [cols(a["g_hgrn"][0])], 1)
    arrays = {
        "x_t": rows(a["x"][0]), "mem_t": rows(a["mem"][0]), "const": const, "level_mask": mask,
        "params": np.ascontiguousarray(prm),
        "sub_keys_t": np.ascontiguousarray(a["peer_sub_keys"][0].transpose(2, 0, 1)),
        "w_kv": halves(a["w_mem_kv"][0]), "w_in": w_in, "w_up": halves(np.roll(a["w_up"][0], -HG * P, axis=0)),
        "w_out": halves(a["w_out"][0]), "w_pq": halves(a["w_peer_q"][0]),
        "w_u": np.ascontiguousarray(u).reshape(2 * NK, P, HT, P),
        "w_v": np.ascontiguousarray(v).reshape(2 * NK, P, HT, P),
    }
    nc = bacc.Bacc("TRN2", target_bir_lowering=False, num_devices=1)
    args = [nc.dram_tensor(n, x.shape, _mybir.dt.from_np(x.dtype), kind="ExternalInput").ap()
            for n, x in arrays.items()]
    out = nc.dram_tensor("out_t", [KT, P, T], _mybir.dt.float32, kind="ExternalOutput").ap()
    encoder_block_kernel(nc, *args, out)
    r = run_bass_kernel_spmd(nc, [arrays], core_ids=[0])
    got = np.asarray(r.results[0]["out_t"]).reshape(D, T)
    return np.ascontiguousarray(got.T).reshape(1, T, D)
```
